# Optimizing a Trainium2 kernel written in Bass

```python
import jax, jax.numpy as jnp
from jax import lax
import numpy as np

D_MODEL = 1024
BATCH = 1
SEQ = 256
DEPTH = 2

CTX_LEN = 256
GRID_W = 64
CHUNK = GRID_W
D_MIX = D_MODEL
M_W = D_MIX // 2
M_H = 4
M_DH = M_W // M_H
F_W = D_MIX // 4
F_G = 4
C_W = D_MIX // 4
C_G = 4
CONV_K = 31
FFN_HIDDEN = 2816
N_EXPERTS = 8
TOP_K = 2
EPS = 1e-6
N_DENSE = (DEPTH + 1) // 2
N_MOE = DEPTH // 2

O_Q = 0
O_K = O_Q + M_W
O_V = O_K + M_W
O_O = O_V + M_W
O_G = O_O + M_W
O_F = O_G + 4 * M_H
O_CU = O_F + F_W
O_CG = O_CU + C_W
P_IN = O_CG + C_W

kernel_name = "hybrid_mlstm_fourier_conformer_moe_dit"

def rmsnorm(x, g):
    xf = x.astype(jnp.float32)
    y = xf * lax.rsqrt(jnp.mean(xf * xf, axis=-1, keepdims=True) + EPS) * g.astype(jnp.float32)
    return y.astype(x.dtype)

def ada_modulation(cond, w_mod, b_mod):
    return jnp.split(jax.nn.silu(cond) @ w_mod + b_mod, 6, axis=-1)

def modulate(h, shift, scale):
    return h * (1 + scale) + shift

def mlstm_inputs(p, b_gate):
    bsz, n, _ = p.shape
    def heads(a):
        return jnp.transpose(a.reshape(bsz, n, M_H, M_DH), (0, 2, 1, 3)).astype(jnp.float32)
    q = heads(p[..., O_Q:O_K])
    k = heads(p[..., O_K:O_V]) * (M_DH ** -0.5)
    v = heads(p[..., O_V:O_O])
    o = p[..., O_O:O_G]
    g = p[..., O_G:O_F].reshape(bsz, n, 4, M_H) + b_gate.reshape(4, M_H)
    g = jnp.transpose(g, (2, 0, 3, 1)).astype(jnp.float32)
    return q, k, v, o, g

def mlstm_init_state(bsz):
    return (jnp.zeros((bsz, M_H, M_DH, M_DH), jnp.float32),
            jnp.zeros((bsz, M_H, M_DH), jnp.float32),
            jnp.full((bsz, M_H), -1e30, jnp.float32))

def mlstm_chunk_scan(q, k, v, ig, lf, state):
    bsz, nh, n, d = q.shape
    rows = n // CHUNK
    def to_chunks(a):
        return jnp.moveaxis(a.reshape(bsz, nh, rows, CHUNK, *a.shape[3:]), 2, 0)
    tril = jnp.tril(jnp.ones((CHUNK, CHUNK), dtype=bool))

    def step(carry, xs):
        c0, n0, m0 = carry
        qc, kc, vc, igc, lfc = xs
        bcum = jnp.cumsum(lfc, axis=-1)
        dmat = jnp.where(tril, bcum[..., :, None] - bcum[..., None, :] + igc[..., None, :], -jnp.inf)
        m_inter = bcum + m0[..., None]
        m_t = jnp.maximum(m_inter, jnp.max(dmat, axis=-1))
        s = jnp.einsum('bhtd,bhsd->bhts', qc, kc) * jnp.exp(dmat - m_t[..., None])
        inter = jnp.exp(m_inter - m_t)
        num = jnp.einsum('bhts,bhse->bhte', s, vc) + inter[..., None] * jnp.einsum('bhtd,bhde->bhte', qc, c0)
        den = jnp.sum(s, axis=-1) + inter * jnp.einsum('bhtd,bhd->bht', qc, n0)
        h = num / jnp.maximum(jnp.abs(den), jnp.exp(-m_t))[..., None]
        b_last = bcum[..., -1]
        gs = b_last[..., None] - bcum + igc
        m_new = jnp.maximum(b_last + m0, jnp.max(gs, axis=-1))
        wk = jnp.exp(gs - m_new[..., None])
        decay = jnp.exp(b_last + m0 - m_new)
        c_new = decay[..., None, None] * c0 + jnp.einsum('bhs,bhsd,bhse->bhde', wk, kc, vc)
        n_new = decay[..., None] * n0 + jnp.einsum('bhs,bhsd->bhd', wk, kc)
        return (c_new, n_new, m_new), h

    state, hs = lax.scan(step, state, (to_chunks(q), to_chunks(k), to_chunks(v), to_chunks(ig), to_chunks(lf)))
    return jnp.moveaxis(hs, 0, 2).reshape(bsz, nh, n, d), state

def flip_seq(a):
    return jnp.flip(a, axis=2)

def mlstm_output(h_sum, o, norm_g):
    bsz, _, n, _ = h_sum.shape
    h = jnp.swapaxes(h_sum, 1, 2)
    h = h * lax.rsqrt(jnp.mean(h * h, axis=-1, keepdims=True) + EPS) * norm_g.reshape(M_H, M_DH).astype(jnp.float32)
    return (jax.nn.sigmoid(o.astype(jnp.float32)) * h.reshape(bsz, n, M_W)).astype(o.dtype)

def bidir_scan(q, k, v, g, init_f, init_b):
    h_f, s_f = mlstm_chunk_scan(q, k, v, g[0], jax.nn.log_sigmoid(g[1]), init_f)
    h_b, s_b = mlstm_chunk_scan(flip_seq(q), flip_seq(k), flip_seq(v), flip_seq(g[2]),
                                flip_seq(jax.nn.log_sigmoid(g[3])), init_b)
    return h_f + flip_seq(h_b), s_f, s_b

def mlstm_mixer(p_lat, p_ctx, b_gate, norm_g, need_ctx):
    ql, kl, vl, ol, gl = mlstm_inputs(p_lat, b_gate)
    qc, kc, vc, oc, gc = mlstm_inputs(p_ctx, b_gate)
    s0 = mlstm_init_state(p_lat.shape[0])
    h_ctx, s_f, s_b = bidir_scan(qc, kc, vc, gc, s0, s0)
    h_lat, _, _ = bidir_scan(ql, kl, vl, gl, s_f, s_b)
    y_lat = mlstm_output(h_lat, ol, norm_g)
    y_ctx = mlstm_output(h_ctx, oc, norm_g) if need_ctx else None
    return y_lat, y_ctx

def fourier_mix(u):
    bsz, n, _ = u.shape
    z = u.astype(jnp.float32).reshape(bsz, n, F_G, F_W // F_G)
    y = jnp.real(jnp.fft.fftn(z, axes=(1, 3), norm="ortho"))
    return y.reshape(bsz, n, F_W).astype(u.dtype)

def conv_module(u, g, dw, db, ln_g, ln_b):
    bsz, n, _ = u.shape
    a = u * jax.nn.sigmoid(g)
    y = lax.conv_general_dilated(a, dw[:, None, :], window_strides=(1,),
                                 padding=[(CONV_K // 2, CONV_K // 2)],
                                 dimension_numbers=('NWC', 'WIO', 'NWC'),
                                 feature_group_count=C_W) + db
    yf = y.astype(jnp.float32).reshape(bsz, n, C_G, C_W // C_G)
    mu = jnp.mean(yf, axis=-1, keepdims=True)
    var = jnp.mean(jnp.square(yf - mu), axis=-1, keepdims=True)
    yf = ((yf - mu) * lax.rsqrt(var + EPS)).reshape(bsz, n, C_W) * ln_g.astype(jnp.float32) + ln_b.astype(jnp.float32)
    return jax.nn.silu(yf).astype(u.dtype)

def merge_heads(p, y_mlstm, dw, db, ln_g, ln_b, w_out):
    y_f = fourier_mix(p[..., O_F:O_CU])
    y_c = conv_module(p[..., O_CU:O_CG], p[..., O_CG:P_IN], dw, db, ln_g, ln_b)
    return jnp.concatenate([y_mlstm, y_f, y_c], axis=-1) @ w_out

def swiglu(h, w_gate_up, w_down):
    gt, up = jnp.split(h @ w_gate_up, 2, axis=-1)
    return (jax.nn.silu(gt) * up) @ w_down

def moe_swiglu(h, w_router, b_router, w_gate_up, w_down):
    logits = (h @ w_router).astype(jnp.float32) + b_router.astype(jnp.float32)
    top_v, top_i = lax.top_k(logits, TOP_K)
    top_w = jax.nn.softmax(top_v, axis=-1)
    gates = jnp.sum(jax.nn.one_hot(top_i, N_EXPERTS, dtype=jnp.float32) * top_w[..., None], axis=-2).astype(h.dtype)
    y = jnp.zeros_like(h)
    for e in range(N_EXPERTS):
        y = y + gates[..., e:e + 1] * swiglu(h, w_gate_up[e], w_down[e])
    return y

def channel_mixer(h, layer, ffn_w_gate_up, ffn_w_down, moe_w_router, moe_b_router, moe_w_gate_up, moe_w_down):
    idx = layer // 2
    if layer % 2 == 0:
        return swiglu(h, ffn_w_gate_up[idx], ffn_w_down[idx])
    return moe_swiglu(h, moe_w_router[idx], moe_b_router[idx], moe_w_gate_up[idx], moe_w_down[idx])

def setup_inputs(seed: int = 0) -> dict:
    key = jax.random.key(seed)
    ks = jax.random.split(key, 26)
    D = D_MODEL
    def nrm(k, shape, s):
        return jax.random.normal(k, shape, jnp.float32) * s
    f_bias = jnp.linspace(3.0, 6.0, M_H, dtype=jnp.float32)
    b_gate = jnp.concatenate([
        nrm(ks[9], (DEPTH, M_H), 0.1),
        f_bias + nrm(ks[10], (DEPTH, M_H), 0.1),
        nrm(ks[11], (DEPTH, M_H), 0.1),
        f_bias + nrm(ks[12], (DEPTH, M_H), 0.1)], axis=-1)
    return {
        "x": nrm(ks[0], (BATCH, SEQ, D), 1.0),
        "c": nrm(ks[1], (BATCH, D), 1.0),
        "ctx": nrm(ks[2], (BATCH, CTX_LEN, D), 1.0),
        "c_ctx": nrm(ks[3], (D,), 1.0),
        "norm1_g": 1.0 + nrm(ks[4], (DEPTH, D), 0.02),
        "norm2_g": 1.0 + nrm(ks[5], (DEPTH, D), 0.02),
        "w_mod": nrm(ks[6], (DEPTH, D, 6 * D), 0.5 * D ** -0.5),
        "b_mod": nrm(ks[7], (DEPTH, 6 * D), 0.02),
        "w_in": nrm(ks[8], (DEPTH, D, P_IN), D ** -0.5),
        "b_gate": b_gate,
        "mlstm_norm_g": 1.0 + nrm(ks[13], (DEPTH, M_W), 0.02),
        "conv_dw": nrm(ks[14], (DEPTH, CONV_K, C_W), CONV_K ** -0.5),
        "conv_db": nrm(ks[15], (DEPTH, C_W), 0.02),
        "conv_norm_g": 1.0 + nrm(ks[16], (DEPTH, C_W), 0.02),
        "conv_norm_b": nrm(ks[17], (DEPTH, C_W), 0.02),
        "w_out": nrm(ks[18], (DEPTH, D_MIX, D), D_MIX ** -0.5),
        "ffn_w_gate_up": nrm(ks[19], (N_DENSE, D, 2 * FFN_HIDDEN), D ** -0.5),
        "ffn_w_down": nrm(ks[20], (N_DENSE, FFN_HIDDEN, D), FFN_HIDDEN ** -0.5),
        "moe_w_router": nrm(ks[21], (N_MOE, D, N_EXPERTS), D ** -0.5),
        "moe_b_router": nrm(ks[22], (N_MOE, N_EXPERTS), 0.01),
        "moe_w_gate_up": nrm(ks[23], (N_MOE, N_EXPERTS, D, 2 * FFN_HIDDEN), D ** -0.5),
        "moe_w_down": nrm(ks[24], (N_MOE, N_EXPERTS, FFN_HIDDEN, D), FFN_HIDDEN ** -0.5),
        "final_norm_g": 1.0 + nrm(ks[25], (D,), 0.02),
    }

def reference(x, c, ctx, c_ctx, norm1_g, norm2_g, w_mod, b_mod, w_in, b_gate, mlstm_norm_g,
              conv_dw, conv_db, conv_norm_g, conv_norm_b, w_out, ffn_w_gate_up, ffn_w_down,
              moe_w_router, moe_b_router, moe_w_gate_up, moe_w_down, final_norm_g):
    xc = ctx
    for layer in range(DEPTH):
        need_ctx = layer < DEPTH - 1
        sh1, sc1, g1, sh2, sc2, g2 = [m[:, None, :] for m in ada_modulation(c, w_mod[layer], b_mod[layer])]
        csh1, csc1, cg1, csh2, csc2, cg2 = ada_modulation(c_ctx, w_mod[layer], b_mod[layer])

        px = modulate(rmsnorm(x, norm1_g[layer]), sh1, sc1) @ w_in[layer]
        pc = modulate(rmsnorm(xc, norm1_g[layer]), csh1, csc1) @ w_in[layer]
        m_lat, m_ctx = mlstm_mixer(px, pc, b_gate[layer], mlstm_norm_g[layer], need_ctx)
        x = x + g1 * merge_heads(px, m_lat, conv_dw[layer], conv_db[layer], conv_norm_g[layer],
                                 conv_norm_b[layer], w_out[layer])
        if need_ctx:
            xc = xc + cg1 * merge_heads(pc, m_ctx, conv_dw[layer], conv_db[layer], conv_norm_g[layer],
                                        conv_norm_b[layer], w_out[layer])

        hx = modulate(rmsnorm(x, norm2_g[layer]), sh2, sc2)
        x = x + g2 * channel_mixer(hx, layer, ffn_w_gate_up, ffn_w_down, moe_w_router, moe_b_router,
                                   moe_w_gate_up, moe_w_down)
        if need_ctx:
            hc = modulate(rmsnorm(xc, norm2_g[layer]), csh2, csc2)
            xc = xc + cg2 * channel_mixer(hc, layer, ffn_w_gate_up, ffn_w_down, moe_w_router, moe_b_router,
                                          moe_w_gate_up, moe_w_down)
    return rmsnorm(x, final_norm_g)


_drawn_inputs = setup_inputs


def setup_inputs(seed=0):
    import zlib

    import numpy as np

    out = dict(_drawn_inputs(seed))
    spreads = {}
    factors = {'norm1_g': 3.955,
     'norm2_g': 2.901,
     'mlstm_norm_g': 5.777,
     'conv_db': 5.735,
     'conv_norm_g': 5.35,
     'conv_norm_b': 8.0,
     'moe_b_router': 5.67,
     'final_norm_g': 2.805}
    for name, (base, spread) in spreads.items():
        noise = np.random.default_rng([zlib.crc32(name.encode()), seed]).standard_normal(out[name].shape)
        drawn = base * np.exp(spread * noise) if base else spread * noise
        out[name] = __import__('jax').numpy.asarray(drawn.astype(out[name].dtype))
    for name, factor in factors.items():
        out[name] = (out[name] * factor).astype(out[name].dtype)
    return out
```

```python
import concourse.bass as bass
from concourse import mybir
from contextlib import ExitStack

P = 128
D = 1024
KT = D // P
CTX = 256
LAT = 256
TOK = CTX + LAT
NTB = TOK // P
LTB = LAT // P
LAYERS = 2
MW = 512
MH = 4
CW = 256
TAPS = 31
HALF = TAPS // 2
PADW = CTX + 2 * HALF
HID = 2816
NHT = HID // P
NE = 8
EPS = 1e-6
PIN = 2832
NCOL = 512
SLOTW = KT * NCOL
RING = 5
GU = HID // 256
DOWN = [3, 3, 3, 3, 2, 2, 2, 2, 2]
DOWN_AT = [sum(DOWN[:i]) for i in range(len(DOWN))]
MLP_SLOTS = GU + len(DOWN)
MOD_SLOTS = 6 * D // NCOL
NEG = -1e30

C_ID, C_ONE, C_GRP, C_UT, C_IOTA, C_MF, C_MB = [P * i for i in range(7)]
C_COS = 7 * P
C_SIN = C_COS + 2 * 256
C_BD = C_SIN + 2 * 256
C_EPS = C_BD + 256
NCONST = C_EPS + 1

V_N1, V_N2, V_MG, V_DB, V_CG, V_CB, V_FIN, V_C, V_CC = 0, 16, 32, 40, 44, 48, 52, 60, 68
V_MOD = 76
V_DW = V_MOD + 96
NVEC = V_DW + LAYERS * TAPS * 2


def causal_cols(direction, sb, lat_only):
    if direction == 0:
        full = [((sb + 1) * P, TOK)] if sb < 3 else []
    else:
        full = {0: [(CTX, TOK)], 1: [(0, P), (CTX, TOK)], 2: [], 3: [(CTX, CTX + P)]}[sb]
    diag = sb
    if lat_only:
        full = [(max(a, CTX), b) for a, b in full if b > CTX]
        if sb < 2:
            diag = None
    spans = list(full)
    if diag is not None:
        spans.append((diag * P, diag * P + P))
    spans.sort()
    merged = []
    for a, b in spans:
        if merged and merged[-1][1] == a:
            merged[-1] = (merged[-1][0], b)
        else:
            merged.append((a, b))
    return diag, full, merged


def key_blocks(direction, tb):
    if direction == 0:
        return list(range(tb + 1))
    return {0: [0, 1], 1: [1], 2: [0, 1, 2, 3], 3: [0, 1, 3]}[tb]


def build(nc, x, c, ctx, c_ctx, norm1_g, norm2_g, w_mod, b_mod, w_in, b_gate, mlstm_norm_g, conv_dw, conv_db,
          conv_norm_g, conv_norm_b, w_out, ffn_w_gate_up, ffn_w_down, moe_w_router, moe_b_router,
          moe_w_gate_up, moe_w_down, final_norm_g, const_tab, out):
    f32 = mybir.dt.float32
    i32 = mybir.dt.int32
    ALU = mybir.AluOpType
    ACT = mybir.ActivationFunctionType
    AX = mybir.AxisListType

    es = ExitStack()
    with es:
        def sb(name, shape, dt=f32):
            return es.enter_context(nc.sbuf_tensor(name, shape, dt))

        def sem(name):
            return es.enter_context(nc.semaphore(name))

        def per_layer(name):
            return [sem(f"{name}_{layer}") for layer in range(LAYERS)]

        xT = sb("xT", [P, KT, TOK])
        hT = sb("hT", [P, KT, TOK])
        ycat = hT
        ring = sb("ring", [P, RING, SLOTW])
        U = sb("U", [P, 21128])
        const = sb("const", [P, NCONST])
        vec = sb("vec", [P, NVEC])
        cond = sb("cond", [P, KT, 2])
        mod = sb("mod", [P, LAYERS, 48, 2])
        amp = sb("amp", [P, LAYERS, 2, KT, 2])
        wr = sb("wr", [P, KT, NE])
        wgate = sb("wgate", [P, KT, 2, 8])
        rbias = sb("rbias", [P, NE])
        gbias = sb("gbias", [8, LAYERS, 2])
        acol = sb("acol", [P, 2, NTB, 8])
        floorc = sb("floorc", [P, 2 * NTB, MH])
        dmax = sb("dmax", [P, 8])
        rden = sb("rden", [P, 8])
        ss16 = sb("ss16", [P, 16])

        ident = const[:, C_ID:C_ID + P]
        ones = const[:, C_ONE:C_ONE + P]
        grp = const[:, C_GRP:C_GRP + P]
        before = const[:, C_UT:C_UT + P]
        iota = const[:, C_IOTA:C_IOTA + P]
        masks = [const[:, C_MF:C_MF + P], const[:, C_MB:C_MB + P]]
        cosn = const[:, C_COS:C_COS + 512].rearrange("p (b n) -> p b n", b=2)
        sinn = const[:, C_SIN:C_SIN + 512].rearrange("p (b n) -> p b n", b=2)
        dftc = const[:, C_BD:C_BD + 256]
        eps = const[:, C_EPS:C_EPS + 1]

        def u(at, n):
            return U[:, at:at + n]

        xin = u(0, 4096).rearrange("p (b d) -> p b d", b=NTB)
        rows = u(4096, 3 * P).rearrange("p (r c) -> p r c", r=3)
        modrow = u(10256, 512)
        sq = u(0, 4096).rearrange("p (k t) -> p k t", k=KT)
        rstd = u(4096, TOK)
        qT = u(0, 2048).rearrange("p (h t) -> p h t", h=MH)
        kT = u(2048, 2048).rearrange("p (h t) -> p h t", h=MH)
        vtok = u(4096, 2064).rearrange("p (b h e) -> p b h e", b=NTB, h=MH)
        sigo = u(6160, 2048).rearrange("p (b c) -> p b c", b=NTB)
        fT = u(8208, 1024).rearrange("p (c t) -> p c t", c=2)
        cu = u(9232, 1024).rearrange("p (c t) -> p c t", c=2)
        Hs = u(8208, 2048).rearrange("p (b c) -> p b c", b=NTB)
        apad = u(10256, 2 * 2 * PADW).rearrange("p (c s t) -> p c s t", c=2, s=2)
        acc = u(11400, 1024).rearrange("p (c s t) -> p c s t", c=2, s=2)
        acc2 = u(11400, 1024).rearrange("p (c t) -> p c t", c=2)
        prob = u(12424, 4096).rearrange("p (d s t) -> p d s t", d=2, s=NTB)
        fab = u(12424, 2048).rearrange("p (b c f) -> p b c f", b=NTB, c=2)
        sigc = u(14472, 1024).rearrange("p (c t) -> p c t", c=2)
        csq = u(12424, 1024).rearrange("p (c t) -> p c t", c=2)
        crs = u(13448, 1024).rearrange("p (c t) -> p c t", c=2)
        hsq = u(14472, 2048).rearrange("p (b c) -> p b c", b=NTB)
        rowsg = U[0:8, 16520:20616].rearrange("p (r t) -> p r t", r=8)
        dm = u(20616, 512).rearrange("p (b t) -> p b t", b=NTB)
        act0 = u(0, NHT * TOK).rearrange("p (i t) -> p i t", i=NHT)
        sil0 = u(NHT * TOK, 2 * TOK).rearrange("p (i t) -> p i t", i=2)
        hxtok = u(0, 2048).rearrange("p (b d) -> p b d", b=LTB)
        hTe = u(2048, KT * P).rearrange("p (k t) -> p k t", k=KT)
        sil = u(3072, 512).rearrange("p (i t) -> p i t", i=2)
        act = u(3584, 512).rearrange("p (i t) -> p i t", i=2)
        actT = u(4096, NHT * P).rearrange("p (i t) -> p i t", i=NHT)
        ysb = u(6912, D)
        pick = u(7936, 256).rearrange("p (b s) -> p b s", b=LTB)
        wpick = u(8192, 256).rearrange("p (b s) -> p b s", b=LTB)
        spread = u(8448, 256)
        NITEM = 2 * NE
        slotpos = u(8704, LTB * 24).rearrange("p (b i) -> p b i", b=LTB)
        gatecol = u(8752, LTB * 24).rearrange("p (b i) -> p b i", b=LTB)
        rt = u(8800, 160)
        nitems = sb("nitems", [1, 2], i32)
        outsb = u(12000, LTB * D).rearrange("p (b d) -> p b d", b=LTB)
        sqf = u(14048, KT * LAT).rearrange("p (k t) -> p k t", k=KT)
        rsf = u(16096, LAT)

        bank = [es.enter_context(nc.psum_tensor(f"bank{i}", [P, NCOL], f32)) for i in range(8)]

        const_in = sem("const_in")
        rows_in = sem("rows_in")
        x_in = sem("x_in")
        small_in = sem("small_in")
        slot_in = [sem(f"slot_in{r}") for r in range(RING)]
        dve_step = sem("dve_step")
        act_step = sem("act_step")
        vec_tp = sem("vec_tp")
        vec_ready = sem("vec_ready")
        cond_ready = sem("cond_ready")
        xt_tp = sem("xt_tp")
        xt_ready = sem("xt_ready")
        mod_mm = sem("mod_mm")
        mod_row = sem("mod_row")
        mod_tp = sem("mod_tp")
        mod_col = sem("mod_col")
        wgate_ready = per_layer("wgate_ready")
        amp_ready = per_layer("amp_ready")
        sq_ready = [[sem(f"sq_ready_{a}{b}") for b in range(2)] for a in range(LAYERS)]
        ssq_done = [[sem(f"ssq_done_{a}{b}") for b in range(2)] for a in range(LAYERS)]
        root_ready = [[sem(f"root_ready_{a}{b}") for b in range(2)] for a in range(LAYERS)]
        xr_ready = [[sem(f"xr_ready_{a}{b}") for b in range(2)] for a in range(LAYERS)]
        h_ready = [[sem(f"h_ready_{a}{b}") for b in range(2)] for a in range(LAYERS)]
        proj_mm = per_layer("proj_mm")
        proj_ready = per_layer("proj_ready")
        nabs_ready = per_layer("nabs_ready")
        ln_ready = per_layer("ln_ready")
        gate_rows = per_layer("gate_rows")
        gate_tp = per_layer("gate_tp")
        gate_cols = per_layer("gate_cols")
        fab_mm = per_layer("fab_mm")
        fab_ready = per_layer("fab_ready")
        fy_mm = per_layer("fy_mm")
        score_mm = per_layer("score_mm")
        mbc_mm = per_layer("mbc_mm")
        dm_ready = per_layer("dm_ready")
        e_ready = per_layer("e_ready")
        p_ready = per_layer("p_ready")
        out_mm = per_layer("out_mm")
        hs_ready = per_layer("hs_ready")
        ss_ready = per_layer("ss_ready")
        hroot_ready = per_layer("hroot_ready")
        ytok_ready = per_layer("ytok_ready")
        yt_tp = per_layer("yt_tp")
        conv_ready = per_layer("conv_ready")
        cmean_mm = per_layer("cmean_mm")
        cdev_ready = per_layer("cdev_ready")
        csq_ready = per_layer("csq_ready")
        cvar_mm = per_layer("cvar_mm")
        croot_ready = per_layer("croot_ready")
        cnorm_ready = per_layer("cnorm_ready")
        ycat_ready = per_layer("ycat_ready")
        wout_mm = per_layer("wout_mm")
        xo_ready = per_layer("xo_ready")
        gu0_mm = sem("gu0_mm")
        sil0_ready = sem("sil0_ready")
        act0_ready = sem("act0_ready")
        down0_mm = sem("down0_mm")
        x2_ready = sem("x2_ready")
        logit_mm = sem("logit_mm")
        hxtok_tp = sem("hxtok_tp")
        hxtok_ready = sem("hxtok_ready")
        mask_ready = sem("mask_ready")
        wdiff_ready = sem("wdiff_ready")
        wexp_ready = sem("wexp_ready")
        pos_mm = sem("pos_mm")
        route_ready = sem("route_ready")
        pick_ready = sem("pick_ready")
        gather_mm = sem("gather_mm")
        hte_ready = sem("hte_ready")
        gu_mm = sem("gu_mm")
        sil_ready = sem("sil_ready")
        act_ready = sem("act_ready")
        act_tp = sem("act_tp")
        actT_ready = sem("actT_ready")
        wpick_ready = sem("wpick_ready")
        spread_tp = sem("spread_tp")
        spread_ready = sem("spread_ready")
        down_mm = sem("down_mm")
        y_ready = sem("y_ready")
        scatter_mm = sem("scatter_mm")
        xacc_ready = sem("xacc_ready")
        fsq_ready = sem("fsq_ready")
        fssq_mm = sem("fssq_mm")
        froot_ready = sem("froot_ready")
        fin_ready = sem("fin_ready")
        fin_tp = sem("fin_tp")
        out_ready = sem("out_ready")
        out_stored = sem("out_stored")

        def ksplit(w):
            return w.rearrange("(k p) n -> p k n", p=P)

        def mlp_pieces(gate_up, down, n):
            if n < GU:
                v = ksplit(gate_up)
                return [(0, v[:, :, n * 256:n * 256 + 256]), (256, v[:, :, HID + n * 256:HID + n * 256 + 256])]
            v = ksplit(down)
            i = n - GU
            return [(None, v[:, DOWN_AT[i]:DOWN_AT[i] + DOWN[i], :])]

        stream = []
        def mod_stream(layer):
            for n in range(MOD_SLOTS):
                stream.append(("mod", layer, n, [(0, ksplit(w_mod[layer])[:, :, n * NCOL:(n + 1) * NCOL])]))

        O_G = 4 * MW
        O_F = O_G + 16
        O_CU = O_F + 256
        IN_SLOTS = [("gf", O_G, 272), ("cc", O_CU, 512), ("q", 0, 512), ("k", 512, 512), ("v", 1024, 512),
                    ("o", 1536, 512)]
        mod_stream(0)
        for layer in range(LAYERS):
            for name, at, w in IN_SLOTS:
                stream.append((name, layer, 0, [(0, ksplit(w_in[layer])[:, :, at:at + w])]))
            if layer == 0:
                mod_stream(1)
            for n in range(2):
                stream.append(("wout", layer, n, [(0, ksplit(w_out[layer])[:, :, n * NCOL:(n + 1) * NCOL])]))
            if layer == 0:
                for n in range(MLP_SLOTS):
                    stream.append(("mlp", 0, n, mlp_pieces(ffn_w_gate_up[0], ffn_w_down[0], n)))
        place = {(name, layer, n): i for i, (name, layer, n, _) in enumerate(stream)}
        BASE = len(stream)
        assert MLP_SLOTS % RING == 0
        TURNS = MLP_SLOTS // RING

        def wslot(n):
            return ring[:, n % RING, :].rearrange("p (k c) -> p k c", k=KT)

        def dslot(n):
            return ring[:, n % RING, :].rearrange("p (k c) -> p k c", c=D)

        def load(eng, n, pieces):
            for off, src in pieces:
                if off is None:
                    dst = dslot(n)[:, 0:src.shape[1], :]
                else:
                    dst = wslot(n)[:, :, off:off + src.shape[2]]
                eng.dma_start(dst, src).then_inc(slot_in[n % RING], 32 // len(pieces))

        def landed(eng, key):
            n = place[key]
            eng.wait_ge(slot_in[n % RING], 32 * (n // RING + 1))
            return n

        def proj_units(layer):
            tbs = range(NTB) if layer == 0 else range(LTB, NTB)
            units = [("gi", 0), ("gf", 0), ("f", 0), ("f", 1), ("cu", 0), ("cg", 0), ("cu", 1), ("cg", 1)]
            units += [("q", h) for h in range(MH)] + [("k", h) for h in range(MH)]
            units += [("v", b) for b in range(NTB)] + [("o", b) for b in tbs]
            return units

        SLOT_OF = {"gi": "gf", "gf": "gf", "f": "gf", "cu": "cc", "cg": "cc", "q": "q", "k": "k", "v": "v", "o": "o"}
        units_of = [proj_units(layer) for layer in range(LAYERS)]

        def unit_count(layer, kind, i):
            return units_of[layer].index((kind, i)) + 1

        def mod_bank(g):
            return bank[4] if g >= MOD_SLOTS or g % 2 == 0 else bank[7]

        def consumed(n):
            name, layer, i, _ = stream[n]
            if name == "mod":
                return mod_mm, layer * MOD_SLOTS + i + 1
            if name == "wout":
                return wout_mm[layer], 4 * (i + 1)
            if name == "mlp":
                return (gu0_mm, 4 * (i + 1)) if i < GU else (down0_mm, i - GU + 1)
            return proj_mm[layer], max(m + 1 for m, (kind, _) in enumerate(units_of[layer]) if SLOT_OF[kind] == name)

        def cols(layer, both):
            return (0, TOK) if layer == 0 or both else (CTX, TOK)

        def streams_of(layer, both=False):
            return (0, 1) if layer == 0 or both else (1,)

        block = es.enter_context(nc.Block())

        @block.sync
        def _(sp):
            sp.dma_start(const[:, :], const_tab).then_inc(const_in, 16)
            r0, r1, r2 = rows[:, 0, :], rows[:, 1, :], rows[:, 2, :]
            flat = [(V_N1, norm1_g.rearrange("l (k p) -> (l k) p", p=P)), (V_N2, norm2_g.rearrange("l (k p) -> (l k) p", p=P)),
                    (V_MG, mlstm_norm_g.rearrange("l (k p) -> (l k) p", p=P)), (V_DB, conv_db.rearrange("l (k p) -> (l k) p", p=P)),
                    (V_CG, conv_norm_g.rearrange("l (k p) -> (l k) p", p=P)), (V_CB, conv_norm_b.rearrange("l (k p) -> (l k) p", p=P)),
                    (V_FIN, final_norm_g.rearrange("(k p) -> k p", p=P)), (V_C, c[0].rearrange("(k p) -> k p", p=P)),
                    (V_CC, c_ctx.rearrange("(k p) -> k p", p=P))]
            for at, src in flat:
                sp.dma_start(r0[at:at + src.shape[0], :], src).then_inc(rows_in, 16)
            sp.dma_start(r1[0:96, :], b_mod.rearrange("l (k p) -> (l k) p", p=P)).then_inc(rows_in, 16)
            sp.dma_start(r2[0:124, :], conv_dw.rearrange("l t (k p) -> (l t k) p", p=P)).then_inc(rows_in, 16)
            for n in range(2):
                load(sp, n, stream[n][3])
            sp.dma_start(xin[:, 0:2, :], ctx[0].rearrange("(b p) d -> p b d", p=P)).then_inc(x_in, 16)
            sp.dma_start(xin[:, 2:4, :], x[0].rearrange("(b p) d -> p b d", p=P)).then_inc(x_in, 16)
            for n in range(2, RING):
                load(sp, n, stream[n][3])
            with nc.allow_non_contiguous_dma(reason="a few small vectors"):
                for layer in range(LAYERS):
                    for kind in range(2):
                        for d in range(2):
                            at = (2 * d + kind) * MH
                            sp.dma_start(gbias[d * MH:d * MH + MH, layer, kind:kind + 1],
                                         b_gate[layer, at:at + MH].rearrange("(h o) -> h o", o=1)).then_inc(small_in, 16)
                sp.dma_start(wr[:, :, :], moe_w_router[0].rearrange("(k p) e -> p k e", p=P)).then_inc(small_in, 16)
                sp.dma_start(rbias[:, :], moe_b_router.to_broadcast([P, NE])).then_inc(small_in, 16)
            for n in range(RING, BASE):
                sp.wait_ge(*consumed(n - RING))
                load(sp, n, stream[n][3])

            def expert(item, e, first):
                for n in range(MLP_SLOTS):
                    old = n - RING
                    if old >= GU:
                        sp.wait_ge(down_mm, item * len(DOWN) + old - GU + 1)
                    elif old >= 0:
                        sp.wait_ge(gu_mm, item * GU + old + 1)
                    elif first:
                        sp.wait_ge(*consumed(BASE + old))
                    else:
                        sp.wait_ge(down_mm, item * len(DOWN) + old + 1)
                    load(sp, BASE + n, mlp_pieces(moe_w_gate_up[0, e], moe_w_down[0, e], n))

            expert(0, 0, True)
            sp.wait_ge(route_ready, 1)
            n_items = sp.value_load(nitems[0:1, 0:1], min_val=NE, max_val=2 * NE)
            with sp.Fori(1, n_items) as item:
                expert(item, item % NE, False)
            for b in range(LTB):
                sp.wait_ge(out_ready, 2 * (b + 1))
                sp.dma_start(out[0, b * P:(b + 1) * P, :], outsb[:, b, :]).then_inc(out_stored, 16)
            sp.wait_ge(out_stored, 16 * LTB)

        @block.tensor
        def _(pe):
            mm = nc.tensor.matmul
            tp = nc.tensor.transpose

            def mod_transposes(g):
                pe.wait_ge(mod_row, g + 1)
                for j in range(4):
                    last = tp(mod_bank(g)[:, 2 * j:2 * j + 2], modrow[0:2, j * P:(j + 1) * P], ident[0:2, 0:2])
                last.then_inc(mod_tp, 1)

            def mod_chunk(layer, n):
                g = layer * MOD_SLOTS + n
                if n >= 1:
                    mod_transposes(g - 1)
                before_it = g if mod_bank(g) is mod_bank(g - 1) else g - 1
                if before_it >= 1:
                    pe.wait_ge(mod_col, before_it)
                at = landed(pe, ("mod", layer, n))
                for k in range(KT):
                    last = mm(mod_bank(g)[0:2, :], cond[:, k, :], wslot(at)[:, k, :], start=k == 0, stop=k == KT - 1)
                last.then_inc(mod_mm, 1)

            def norm_sum(layer, i, lo, hi):
                for k in range(KT):
                    pe.wait_ge(sq_ready[layer][i], k + 1)
                    last = mm(bank[6][:, lo:hi], ones, sq[:, k, lo:hi], start=k == 0, stop=k == KT - 1)
                last.then_inc(ssq_done[layer][i], 1)

            def projections(layer):
                for n, (kind, i) in enumerate(units_of[layer]):
                    b = bank[n % 2]
                    if n >= 2:
                        pe.wait_ge(proj_ready[layer], n - 1)
                    at = landed(pe, (SLOT_OF[kind], layer, 0))
                    w = wslot(at)
                    lo, hi = cols(layer, kind in ("gi", "gf", "k"))
                    if n == 0:
                        pe.wait_ge(wgate_ready[layer], 1)
                    for k in range(KT):
                        if n == 0:
                            pe.wait_ge(h_ready[layer][0], k + 1)
                        st = dict(start=k == 0, stop=k == KT - 1)
                        if kind in ("gi", "gf"):
                            wg = wgate[:, k, 0 if kind == "gi" else 1, :]
                            last = mm(b[0:8, lo:hi], wg, hT[:, k, lo:hi], **st)
                        elif kind in ("v", "o"):
                            last = mm(b[:, :], hT[:, k, i * P:(i + 1) * P], w[:, k, :], **st)
                        else:
                            off = {"f": 16, "cu": 0, "cg": CW, "q": 0, "k": 0}[kind] + i * P
                            last = mm(b[:, lo:hi], w[:, k, off:off + P], hT[:, k, lo:hi], **st)
                    last.then_inc(proj_mm[layer], 1)
                    if (kind, i) == ("k", MH - 1):
                        gate_transposes(layer)

            def gate_transposes(layer):
                pe.wait_ge(gate_rows[layer], 1)
                for d in range(2):
                    for b in range(NTB):
                        at = (d * NTB + b) * 8
                        tp(bank[7][:, at:at + 8], rowsg[:, 4 + d, b * P:(b + 1) * P], ident[0:8, 0:8])
                        last = tp(bank[7][:, 64 + at:72 + at], rowsg[:, 2 + d, b * P:(b + 1) * P], ident[0:8, 0:8])
                last.then_inc(gate_tp[layer], 1)

            def fourier(layer):
                fb = [2, 3, 5, 6]
                for s in streams_of(layer):
                    for ct in range(2):
                        b = bank[fb[s * 2 + ct]]
                        for j in range(2):
                            tb = 2 * s + j
                            last = mm(b[:, j * 256:(j + 1) * 256], fT[:, ct, tb * P:(tb + 1) * P], dftc, start=True, stop=True)
                        last.then_inc(fab_mm[layer], 1)
                pe.wait_ge(fab_ready[layer], 2 * len(streams_of(layer)))
                for ct in range(2):
                    for s in streams_of(layer):
                        for j in range(2):
                            tb = 2 * s + j
                            o = bank[2 + ct][:, s * 256:(s + 1) * 256]
                            mm(o, fab[:, tb, ct, 0:P], cosn[:, j, :], start=j == 0, stop=False)
                            last = mm(o, fab[:, tb, ct, P:2 * P], sinn[:, j, :], start=False, stop=j == 1)
                    last.then_inc(fy_mm[layer], 1)

            def heads(layer):
                lo, hi = cols(layer, False)
                tbs = range(NTB) if layer == 0 else range(LTB, NTB)

                def running_max(h, d):
                    if h or d:
                        pe.wait_ge(e_ready[layer], 2 * h + d)
                    mm(bank[3][:, lo:hi], ident[0:8, d * MH + h:d * MH + h + 1].to_broadcast([8, P]),
                       rowsg[:, 6 + d, lo:hi], start=True, stop=True).then_inc(mbc_mm[layer], 1)

                def read_values(h, d):
                    pe.wait_ge(p_ready[layer], 2 * h + d + 1)
                    for j, tb in enumerate(tbs):
                        idx = d * NTB + tb
                        b = bank[5 + idx // 3]
                        o = b[:, (idx % 3) * 129:(idx % 3) * 129 + 129]
                        keys = key_blocks(d, tb)
                        for n, s in enumerate(keys):
                            last = mm(o, prob[:, d, s, tb * P:(tb + 1) * P], vtok[:, s, h, :],
                                      start=n == 0, stop=n == len(keys) - 1)
                    last.then_inc(out_mm[layer], 1)

                pe.wait_ge(gate_cols[layer], 2)
                pe.wait_ge(ycat_ready[layer], 2)
                for h in range(MH):
                    if h:
                        pe.wait_ge(p_ready[layer], 2 * h)
                    for s in range(NTB):
                        a, z = (lo, hi) if s < 2 else (CTX, TOK)
                        o = bank[s][:, a:z] if s < 2 else bank[2][:, (s - 2) * LAT:(s - 1) * LAT]
                        last = mm(o, kT[:, h, s * P:(s + 1) * P], qT[:, h, a:z], start=True, stop=True)
                    last.then_inc(score_mm[layer], 1)
                    running_max(h, 0)
                    if layer == 0:
                        mod_chunk(1, 3 * h)
                    running_max(h, 1)
                    if layer == 0:
                        mod_chunk(1, 3 * h + 1)
                    if h:
                        pe.wait_ge(hs_ready[layer], h)
                    read_values(h, 0)
                    if layer == 0:
                        mod_chunk(1, 3 * h + 2)
                    read_values(h, 1)
                if layer == 0:
                    mod_transposes(2 * MOD_SLOTS - 1)

            def conv_norm(layer):
                lo, hi = cols(layer, False)
                pe.wait_ge(conv_ready[layer], 1)
                pe.wait_ge(hs_ready[layer], MH)
                for ct in range(2):
                    last = mm(bank[5 + ct][:, lo:hi], grp, acc2[:, ct, lo:hi], start=True, stop=True)
                    last.then_inc(cmean_mm[layer], 1)
                for ct in range(2):
                    pe.wait_ge(csq_ready[layer], ct + 1)
                    last = mm(bank[5 + ct][:, lo:hi], grp, csq[:, ct, lo:hi], start=True, stop=True)
                    last.then_inc(cvar_mm[layer], 1)

            def y_transposes(layer):
                tbs = range(NTB) if layer == 0 else range(LTB, NTB)
                pe.wait_ge(p_ready[layer], 2 * MH)
                pe.wait_ge(e_ready[layer], 2 * MH)
                pe.wait_ge(ytok_ready[layer], 1)
                for h in range(MH):
                    for tb in tbs:
                        last = tp(bank[h][:, tb * P:(tb + 1) * P], Hs[:, tb, h * P:(h + 1) * P], ident)
                    last.then_inc(yt_tp[layer], 1)

            def out_projection(layer):
                lo, hi = cols(layer, False)
                pe.wait_ge(ycat_ready[layer], 8)
                for m in range(KT):
                    if m >= 2:
                        pe.wait_ge(xo_ready[layer], m - 1)
                    at = landed(pe, ("wout", layer, m // 4))
                    for k in range(KT):
                        last = mm(bank[m % 2][:, lo:hi], wslot(at)[:, k, (m % 4) * P:(m % 4 + 1) * P], ycat[:, k, lo:hi],
                                  start=k == 0, stop=k == KT - 1)
                    last.then_inc(wout_mm[layer], 1)

            def dense_mixer():
                for n in range(GU):
                    at = landed(pe, ("mlp", 0, n))
                    for j in range(2):
                        i = 2 * n + j
                        if i >= 2:
                            pe.wait_ge(act0_ready, i - 1)
                        for side in range(2):
                            off = side * 256 + j * P
                            for k in range(KT):
                                if n == 0 and j == 0 and side == 0:
                                    pe.wait_ge(h_ready[0][1], k + 1)
                                last = mm(bank[2 * (i % 2) + side][:, :], wslot(at)[:, k, off:off + P], hT[:, k, :],
                                          start=k == 0, stop=k == KT - 1)
                            last.then_inc(gu0_mm, 1)
                for n, tiles in enumerate(DOWN):
                    at = landed(pe, ("mlp", 0, GU + n))
                    for j in range(tiles):
                        i = DOWN_AT[n] + j
                        if n == 0 and j == 0:
                            pe.wait_ge(act0_ready, NHT)
                        for m in range(KT):
                            last = mm(bank[m][:, :], dslot(at)[:, j, m * P:(m + 1) * P], act0[:, i, :],
                                      start=i == 0, stop=i == NHT - 1)
                    last.then_inc(down0_mm, 1)

            pe.wait_ge(const_in, 16)
            pe.wait_ge(rows_in, 16 * 11)
            for r, (at, n) in enumerate(((0, 76), (V_MOD, 96), (V_DW, 124))):
                last = tp(bank[0][:, at:at + n], rows[0:n, r, :], ident[0:n, 0:n])
            last.then_inc(vec_tp, 1)
            pe.wait_ge(cond_ready, 2)
            for n in range(MOD_SLOTS):
                mod_chunk(0, n)
                if n < KT:
                    pe.wait_ge(x_in, 32)
                    if n >= 2:
                        pe.wait_ge(xt_ready, n - 1)
                    for b in range(NTB):
                        last = tp(bank[5 + n % 2][:, b * P:(b + 1) * P], xin[:, b, n * P:(n + 1) * P], ident)
                    last.then_inc(xt_tp, 1)
            mod_transposes(MOD_SLOTS - 1)

            for layer in range(LAYERS):
                norm_sum(layer, 0, 0, TOK)
                projections(layer)
                fourier(layer)
                heads(layer)
                conv_norm(layer)
                y_transposes(layer)
                out_projection(layer)
                norm_sum(layer, 1, *cols(layer, False))
                if layer == 0:
                    dense_mixer()

            pe.wait_ge(h_ready[1][1], KT)
            pe.wait_ge(small_in, 16 * 10)
            for b in range(LTB):
                for k in range(KT):
                    last = mm(bank[0][:, b * NE:(b + 1) * NE], hT[:, k, CTX + b * P:CTX + (b + 1) * P], wr[:, k, :],
                              start=k == 0, stop=k == KT - 1)
            last.then_inc(logit_mm, 1)
            for b in range(LTB):
                for half in range(2):
                    for j in range(4):
                        k = 4 * half + j
                        last = tp(bank[2 + 2 * b + half][:, j * P:(j + 1) * P], hT[:, k, CTX + b * P:CTX + (b + 1) * P], ident)
                    last.then_inc(hxtok_tp, 1)
            pe.wait_ge(mask_ready, 1)
            mask = rt[:, 0:16].rearrange("p (b e) -> p b e", b=LTB)
            mm(bank[1][:, 0:8], before, mask[:, 0, :], start=True, stop=True)
            mm(bank[1][:, 8:16], ones, mask[:, 0, :], start=True, stop=False)
            mm(bank[1][:, 8:16], before, mask[:, 1, :], start=False, stop=True)
            mm(bank[1][:, 16:24], ones, mask[:, 0, :], start=True, stop=False)
            mm(bank[1][:, 16:24], ones, mask[:, 1, :], start=False, stop=True).then_inc(pos_mm, 1)

            def gather():
                for k in range(KT):
                    for b in range(LTB):
                        last = mm(bank[6 + k // 4][:, (k % 4) * P:(k % 4 + 1) * P], hxtok[:, b, k * P:(k + 1) * P],
                                  pick[:, b, :], start=b == 0, stop=b == LTB - 1)
                last.then_inc(gather_mm, 1)

            def scatter(r):
                for j in range(4):
                    m = 4 * r + j
                    last = mm(bank[6 + j // 2][:, (j % 2) * LAT:(j % 2 + 1) * LAT], ysb[:, m * P:(m + 1) * P], spread,
                              start=True, stop=True)
                last.then_inc(scatter_mm, 1)

            def transposes(item, j):
                cnt = GU * item + j
                pe.wait_ge(act_ready, cnt + 3)
                pe.wait_ge(actT_ready, cnt + (2 if j == 0 else 1))
                for i in range(2):
                    last = tp(bank[2 + j % 2][:, i * P:(i + 1) * P], act[:, j % 2, i * P:(i + 1) * P], ident)
                last.then_inc(act_tp, 1)

            pe.wait_ge(hxtok_ready, 4)
            pe.wait_ge(pick_ready, 1)
            gather()
            n_items = pe.value_load(nitems[0:1, 0:1], min_val=NE, max_val=2 * NE)
            with pe.Fori(0, n_items) as item:
                pe.wait_ge(hte_ready, item + 1)
                for j in range(GU):
                    n = BASE + j
                    pe.wait_ge(slot_in[n % RING], item * (32 * TURNS) + 32 * (n // RING + 1))
                    pe.wait_ge(act_ready, item * GU + j + (2 if j == 0 else 1))
                    for k in range(KT):
                        last = mm(bank[j % 2][:, :], hTe[:, k, :], wslot(n)[:, k, :], start=k == 0, stop=k == KT - 1)
                    last.then_inc(gu_mm, 1)
                    if j < 2:
                        if j == 0:
                            pe.wait_ge(y_ready, item + 1)
                            pe.wait_ge(spread_ready, item + 1)
                        pe.wait_ge(xacc_ready, 2 * item + j + 1)
                        scatter(j)
                    if j == 4:
                        pe.wait_ge(spread_ready, item + 2)
                    if j >= 1:
                        transposes(item, j - 1)
                    if j == 3:
                        pe.wait_ge(wpick_ready, item + 1)
                        pe.wait_ge(actT_ready, item * GU + 4)
                        for b in range(LTB):
                            last = tp(bank[3][:, 256 + b * P:256 + (b + 1) * P], wpick[:, b, :], ident)
                        last.then_inc(spread_tp, 1)
                pe.wait_ge(pick_ready, item + 2)
                pe.wait_ge(xacc_ready, 2 * item + 3)
                gather()
                transposes(item, GU - 1)
                for n, tiles in enumerate(DOWN):
                    at = BASE + GU + n
                    pe.wait_ge(slot_in[at % RING], item * (32 * TURNS) + 32 * (at // RING + 1))
                    for j in range(tiles):
                        i = DOWN_AT[n] + j
                        pe.wait_ge(actT_ready, item * GU + i // 2 + 3)
                        for half in range(2):
                            last = mm(bank[4 + half][:, :], actT[:, i, :], dslot(at)[:, j, half * NCOL:(half + 1) * NCOL],
                                      start=i == 0, stop=i == NHT - 1)
                    last.then_inc(down_mm, 1)
            pe.wait_ge(y_ready, n_items + 1)
            pe.wait_ge(spread_ready, n_items + 1)
            for r in range(2):
                pe.wait_ge(xacc_ready, 2 * n_items + r + 1)
                if r == 0:
                    pe.wait_ge(hte_ready, n_items + 1)
                scatter(r)

            for k in range(KT):
                pe.wait_ge(fsq_ready, k + 1)
                last = mm(bank[0][:, 0:LAT], ones, sqf[:, k, :], start=k == 0, stop=k == KT - 1)
            last.then_inc(fssq_mm, 1)
            for b in range(LTB):
                for half in range(2):
                    for j in range(4):
                        k = 4 * half + j
                        if b == 0:
                            pe.wait_ge(fin_ready, k + 1)
                        last = tp(bank[2 + 2 * b + half][:, j * P:(j + 1) * P], xT[:, k, CTX + b * P:CTX + (b + 1) * P], ident)
                    last.then_inc(fin_tp, 1)

        @block.scalar
        def _(sc):
            act_fn = nc.scalar.activation

            def norm(layer, i):
                lo, hi = cols(layer, i == 0)
                for k in range(KT):
                    if layer == 0 and i == 0:
                        sc.wait_ge(xt_ready, KT)
                    elif i == 1:
                        sc.wait_ge(xo_ready[layer], KT)
                    else:
                        sc.wait_ge(x2_ready, KT)
                    act_fn(sq[:, k, lo:hi], xT[:, k, lo:hi], ACT.Square).then_inc(sq_ready[layer][i], 1)
                sc.wait_ge(ssq_done[layer][i], 1)
                act_fn(rstd[:, lo:hi], bank[6][:, lo:hi], ACT.Sqrt, bias=eps, scale=1.0 / D).then_inc(root_ready[layer][i], 1)
                sc.wait_ge(amp_ready[layer], 1)
                for k in range(KT):
                    sc.wait_ge(xr_ready[layer][i], k + 1)
                    for s in streams_of(layer, i == 0):
                        v = hT[:, k, s * 256:(s + 1) * 256]
                        last = act_fn(v, v, ACT.Identity, bias=mod[:, layer, 24 * i + k, s:s + 1],
                                      scale=amp[:, layer, i, k, s:s + 1])
                    last.then_inc(h_ready[layer][i], 1)

            def mixer(layer):
                lo, hi = cols(layer, False)
                for n, (kind, i) in enumerate(units_of[layer]):
                    b = bank[n % 2]
                    sc.wait_ge(proj_mm[layer], n + 1)
                    if n == 0:
                        sc.wait_ge(small_in, 16 * 10)
                    if kind in ("gi", "gf"):
                        r = 0 if kind == "gi" else 1
                        o = act_fn(rowsg[:, r, :], b[0:8, :], ACT.Identity, bias=gbias[:, layer, r:r + 1])
                    elif kind == "f":
                        o = act_fn(fT[:, i, lo:hi], b[:, lo:hi], ACT.Copy)
                    elif kind == "cu":
                        o = act_fn(cu[:, i, lo:hi], b[:, lo:hi], ACT.Copy)
                    elif kind == "cg":
                        o = act_fn(sigc[:, i, lo:hi], b[:, lo:hi], ACT.Sigmoid)
                    elif kind == "q":
                        o = act_fn(qT[:, i, lo:hi], b[:, lo:hi], ACT.Copy)
                    elif kind == "k":
                        o = act_fn(kT[:, i, :], b[:, :], ACT.Copy, scale=float(P) ** -0.5)
                    elif kind == "v":
                        o = act_fn(vtok[:, i, :, 0:P], b[:, :].rearrange("p (h e) -> p h e", h=MH), ACT.Copy)
                    else:
                        o = act_fn(sigo[:, i, :], b[:, :], ACT.Sigmoid)
                    o.then_inc(proj_ready[layer], 1)
                    if kind == "gf":
                        sc.wait_ge(nabs_ready[layer], 1)
                        act_fn(rowsg[:, 2, :], rowsg[:, 2, :], ACT.Exp).then_inc(nabs_ready[layer], 1)
                        sc.wait_ge(nabs_ready[layer], 2)
                        act_fn(rowsg[:, 2, :], rowsg[:, 2, :], ACT.Ln, bias=1.0).then_inc(ln_ready[layer], 1)
                    if (kind, i) == ("k", MH - 1):
                        sc.wait_ge(gate_tp[layer], 1)
                        act_fn(acol[:, :, :, :], bank[7][:, 0:64].rearrange("p (d b r) -> p d b r", d=2, b=NTB),
                               ACT.Copy).then_inc(gate_cols[layer], 1)
                        for d in range(2):
                            m = bank[7][:, 64 + 32 * d:96 + 32 * d].rearrange("p (b r) -> p b r", b=NTB)
                            last = act_fn(floorc[:, d * NTB:(d + 1) * NTB, :], m[:, :, d * MH:(d + 1) * MH], ACT.Exp)
                        last.then_inc(gate_cols[layer], 1)
                fb = [2, 3, 5, 6]
                n = 0
                for s in streams_of(layer):
                    for ct in range(2):
                        n += 1
                        sc.wait_ge(fab_mm[layer], n)
                        act_fn(fab[:, 2 * s:2 * s + 2, ct, :], bank[fb[s * 2 + ct]][:, :].rearrange("p (b f) -> p b f", b=2),
                               ACT.Copy).then_inc(fab_ready[layer], 1)
                for ct in range(2):
                    sc.wait_ge(fy_mm[layer], ct + 1)
                    act_fn(ycat[:, 4 + ct, lo:hi], bank[2 + ct][:, lo:hi], ACT.Copy).then_inc(ycat_ready[layer], 1)
                sc.wait_ge(gate_cols[layer], 2)
                sc.wait_ge(conv_ready[layer], 1)
                for h in range(MH):
                    for d in range(2):
                        sc.wait_ge(mbc_mm[layer], 2 * h + d + 1)
                        if h:
                            sc.wait_ge(out_mm[layer], 2 * (h - 1) + d + 1)
                        sc.wait_ge(dm_ready[layer], 2 * h + d + 1)
                        last = None
                        for s in range(NTB):
                            diag, full, _ = causal_cols(d, s, layer == 1)
                            bias = acol[:, d, s, d * MH + h:d * MH + h + 1]
                            for a, z in full:
                                last = act_fn(prob[:, d, s, a:z], bank[3][:, a:z], ACT.Exp, bias=bias, scale=-1.0)
                        for s in range(NTB):
                            diag, full, _ = causal_cols(d, s, layer == 1)
                            bias = acol[:, d, s, d * MH + h:d * MH + h + 1]
                            if diag is not None:
                                last = act_fn(prob[:, d, s, diag * P:(diag + 1) * P], dm[:, diag, :], ACT.Exp, bias=bias)
                        last.then_inc(e_ready[layer], 1)
                for ct in range(2):
                    sc.wait_ge(cdev_ready[layer], ct + 1)
                    if ct == 0:
                        sc.wait_ge(out_mm[layer], 2 * MH)
                    act_fn(csq[:, ct, lo:hi], acc2[:, ct, lo:hi], ACT.Square).then_inc(csq_ready[layer], 1)
                for ct in range(2):
                    sc.wait_ge(cvar_mm[layer], ct + 1)
                    act_fn(crs[:, ct, lo:hi], bank[5 + ct][:, lo:hi], ACT.Sqrt, bias=eps).then_inc(croot_ready[layer], 1)
                sc.wait_ge(ss_ready[layer], 1)
                act_fn(ss16[:, :], ss16[:, :], ACT.Sqrt, bias=eps, scale=1.0 / P).then_inc(hroot_ready[layer], 1)
                for ct in range(2):
                    sc.wait_ge(cnorm_ready[layer], ct + 1)
                    w = layer * 2 + ct
                    act_fn(ycat[:, 6 + ct, lo:hi], acc2[:, ct, lo:hi], ACT.Silu, bias=vec[:, V_CB + w:V_CB + w + 1],
                           scale=vec[:, V_CG + w:V_CG + w + 1]).then_inc(ycat_ready[layer], 1)
                for h in range(MH):
                    sc.wait_ge(yt_tp[layer], h + 1)
                    w = V_MG + layer * MH + h
                    act_fn(ycat[:, h, lo:hi], bank[h][:, lo:hi], ACT.Copy, scale=vec[:, w:w + 1]).then_inc(ycat_ready[layer], 1)

            sc.wait_ge(vec_tp, 1)
            act_fn(vec[:, :], bank[0][:, 0:NVEC], ACT.Copy).then_inc(vec_ready, 1)
            sc.wait_ge(vec_ready, 1)
            act_fn(cond[:, :, 0], vec[:, V_CC:V_CC + KT], ACT.Silu).then_inc(cond_ready, 1)
            act_fn(cond[:, :, 1], vec[:, V_C:V_C + KT], ACT.Silu).then_inc(cond_ready, 1)
            for layer in range(LAYERS):
                norm(layer, 0)
                mixer(layer)
                norm(layer, 1)
                if layer == 0:
                    for i in range(NHT):
                        sc.wait_ge(gu0_mm, 2 * i + 1)
                        if i >= 2:
                            sc.wait_ge(act0_ready, i - 1)
                        act_fn(sil0[:, i % 2, :], bank[2 * (i % 2)][:, :], ACT.Silu).then_inc(sil0_ready, 1)
            for n in range(4):
                sc.wait_ge(hxtok_tp, n + 1)
                b, half = n // 2, n % 2
                act_fn(hxtok[:, b, half * NCOL:(half + 1) * NCOL], bank[2 + n][:, :], ACT.Copy).then_inc(hxtok_ready, 1)

            sc.wait_ge(wdiff_ready, 1)
            act_fn(rt[:, 88:90], rt[:, 88:90], ACT.Exp).then_inc(wexp_ready, 1)

            def gathered():
                for half in range(2):
                    last = act_fn(hTe[:, 4 * half:4 * half + 4, :], bank[6 + half][:, :].rearrange("p (k t) -> p k t", k=4), ACT.Copy)
                last.then_inc(hte_ready, 1)

            def transposed(item, j):
                sc.wait_ge(act_tp, item * GU + j + 3)
                act_fn(actT[:, 2 * j:2 * j + 2, :], bank[2 + j % 2][:, 0:256].rearrange("p (i t) -> p i t", i=2),
                       ACT.Copy).then_inc(actT_ready, 1)

            sc.sem_inc(actT_ready, 2)
            sc.wait_ge(gather_mm, 1)
            gathered()
            sc.wait_ge(route_ready, 1)
            n_items = sc.value_load(nitems[0:1, 0:1], min_val=NE, max_val=2 * NE)
            with sc.Fori(0, n_items) as item:
                for j in range(GU):
                    sc.wait_ge(gu_mm, item * GU + j + 1)
                    sc.wait_ge(act_ready, item * GU + j + (2 if j == 0 else 1))
                    act_fn(sil[:, j % 2, :], bank[j % 2][:, 0:256], ACT.Silu).then_inc(sil_ready, 1)
                    if j == 1:
                        sc.wait_ge(y_ready, item + 1)
                    if j >= 1:
                        transposed(item, j - 1)
                sc.wait_ge(gather_mm, item + 2)
                gathered()
                transposed(item, GU - 1)
            for k in range(KT):
                sc.wait_ge(xacc_ready, 2 * n_items + 3)
                act_fn(sqf[:, k, :], xT[:, k, CTX:TOK], ACT.Square).then_inc(fsq_ready, 1)
            sc.wait_ge(fssq_mm, 1)
            act_fn(rsf, bank[0][:, 0:LAT], ACT.Sqrt, bias=eps, scale=1.0 / D).then_inc(froot_ready, 1)
            for n in range(4):
                sc.wait_ge(fin_tp, n + 1)
                b, half = n // 2, n % 2
                act_fn(outsb[:, b, half * NCOL:(half + 1) * NCOL], bank[2 + n][:, :], ACT.Copy).then_inc(out_ready, 1)

        @block.vector
        def _(dve):
            V = nc.vector
            steps = [0]

            def link(ins):
                steps[0] += 1
                ins.then_inc(dve_step, 1)
                dve.wait_ge(dve_step, steps[0])

            def mark(ins):
                steps[0] += 1
                ins.then_inc(dve_step, 1)
                return steps[0]

            def mod_rows(g):
                dve.wait_ge(mod_mm, g + 1)
                if g:
                    dve.wait_ge(mod_tp, g)
                V.tensor_copy(modrow[0:2, :], mod_bank(g)[0:2, :]).then_inc(mod_row, 1)

            def mod_cols(g):
                layer, n = divmod(g, MOD_SLOTS)
                dve.wait_ge(mod_tp, g + 1)
                at = V_MOD + layer * 48 + 4 * n
                V.tensor_tensor(mod[:, layer, 4 * n:4 * n + 4, :], mod_bank(g)[:, 0:8].rearrange("p (j s) -> p j s", s=2),
                                vec[:, at:at + 4].unsqueeze(2).to_broadcast([P, 4, 2]), ALU.add).then_inc(mod_col, 1)

            def amplitudes(layer):
                dve.wait_ge(mod_col, (layer + 1) * MOD_SLOTS)
                for i in range(2):
                    sc1 = mod[:, layer, 24 * i + 8:24 * i + 16, :]
                    g = vec[:, 16 * i + 8 * layer:16 * i + 8 * layer + 8].unsqueeze(2).to_broadcast([P, KT, 2])
                    link(V.tensor_scalar(amp[:, layer, i], sc1, 1.0, None, ALU.add))
                    ins = V.tensor_tensor(amp[:, layer, i], amp[:, layer, i], g, ALU.mult)
                    if i == 0:
                        link(ins)
                    else:
                        ins.then_inc(amp_ready[layer], 1)
                        dve.wait_ge(amp_ready[layer], 1)

            def norm(layer, i):
                lo, hi = cols(layer, i == 0)
                dve.wait_ge(root_ready[layer][i], 1)
                link(V.reciprocal(rstd[:, lo:hi], rstd[:, lo:hi]))
                for k in range(KT):
                    V.tensor_tensor(hT[:, k, lo:hi], xT[:, k, lo:hi], rstd[:, lo:hi], ALU.mult).then_inc(xr_ready[layer][i], 1)

            def gates(layer):
                R = [rowsg[:, r, :] for r in range(8)]
                dve.wait_ge(proj_ready[layer], 2)
                ins = V.scalar_tensor_tensor(R[2], R[1], -1.0, R[1], ALU.mult, ALU.min)
                ins.then_inc(nabs_ready[layer], 1)
                dve.wait_ge(ln_ready[layer], 1)
                link(V.scalar_tensor_tensor(R[1], R[1], 0.0, R[2], ALU.min, ALU.subtract))

                def run(d, o, src, first, kind):
                    if d == 0:
                        spans = [slice(0, TOK)]
                    else:
                        spans = [slice(CTX - 1, None, -1), slice(TOK - 1, CTX - 1, -1)]
                    init = first
                    for n, s in enumerate(spans):
                        a = src[:, s]
                        if kind == "sum":
                            link(V.tensor_tensor_scan(o[:, s], onesrow[:, s], a, init, ALU.mult, ALU.add))
                        else:
                            link(V.tensor_tensor_scan(o[:, s], a, a, init, ALU.max, ALU.max))
                        init = o[:, 0:1]

                onesrow = R[6]
                link(V.memset(onesrow, 1.0))
                for d in range(2):
                    run(d, R[2 + d], R[1], 0.0, "sum")
                for d in range(2):
                    link(V.tensor_tensor(R[4 + d], R[0], R[2 + d], ALU.subtract))
                for d in range(2):
                    run(d, R[6 + d], R[4 + d], NEG, "max")
                for d in range(2):
                    ins = V.scalar_tensor_tensor(R[2 + d], R[2 + d], -1.0, R[6 + d], ALU.mult, ALU.subtract)
                    if d == 0:
                        link(ins)
                    else:
                        ins.then_inc(gate_rows[layer], 1)

            def convolution(layer):
                ss = slice(0, 2) if layer == 0 else slice(1, 2)
                lo, hi = cols(layer, False)
                dve.wait_ge(proj_ready[layer], unit_count(layer, "cg", 1))
                for ct in range(2):
                    w = CTX
                    cuv = cu[:, ct, lo:hi].rearrange("p (s t) -> p s t", t=w)
                    sgv = sigc[:, ct, lo:hi].rearrange("p (s t) -> p s t", t=w)
                    last = V.tensor_tensor(apad[:, ct, ss, HALF:HALF + w], cuv, sgv, ALU.mult)
                    link(last)
                for t in range(TAPS):
                    for ct in range(2):
                        wcol = vec[:, V_DW + layer * 62 + t * 2 + ct:V_DW + layer * 62 + t * 2 + ct + 1]
                        src = apad[:, ct, ss, t:t + CTX]
                        if t == 0:
                            db = vec[:, V_DB + 2 * layer + ct:V_DB + 2 * layer + ct + 1]
                            mark(V.tensor_scalar(acc[:, ct, ss, :], src, wcol, db, ALU.mult, ALU.add))
                        else:
                            dve.wait_ge(dve_step, steps[0] - 1)
                            ins = V.scalar_tensor_tensor(acc[:, ct, ss, :], src, wcol, acc[:, ct, ss, :], ALU.mult, ALU.add)
                            mark(ins)
                dve.wait_ge(dve_step, steps[0])
                dve.sem_inc(conv_ready[layer], 1)

            def mod_late(layer, g):
                if layer == 0:
                    if g > MOD_SLOTS:
                        mod_cols(g - 1)
                    mod_rows(g)

            def heads(layer):
                tbs = list(range(NTB)) if layer == 0 else list(range(LTB, NTB))
                b0 = tbs[0]

                def differences(h, d):
                    dve.wait_ge(mbc_mm[layer], 2 * h + d + 1)
                    V.tensor_tensor(dm[:, b0:NTB, :], masks[d].unsqueeze(1).to_broadcast([P, NTB - b0, P]),
                                    bank[3][:, b0 * P:TOK].rearrange("p (b t) -> p b t", t=P),
                                    ALU.subtract).then_inc(dm_ready[layer], 1)

                def weigh(h, d):
                    dve.wait_ge(e_ready[layer], 2 * h + d + 1)
                    dve.wait_ge(score_mm[layer], h + 1)
                    last = None
                    for s in range(NTB):
                        for a, z in causal_cols(d, s, layer == 1)[2]:
                            sco = bank[s][:, a:z] if s < 2 else bank[2][:, (s - 2) * LAT + a - CTX:(s - 2) * LAT + z - CTX]
                            last = V.tensor_tensor(prob[:, d, s, a:z], prob[:, d, s, a:z], sco, ALU.mult)
                    last.then_inc(p_ready[layer], 1)

                for h in range(MH):
                    differences(h, 0)
                    mod_late(layer, MOD_SLOTS + 3 * h)
                    weigh(h, 0)
                    differences(h, 1)
                    mod_late(layer, MOD_SLOTS + 3 * h + 1)
                    weigh(h, 1)
                    mod_late(layer, MOD_SLOTS + 3 * h + 2)
                    dve.wait_ge(out_mm[layer], 2 * h + 2)
                    groups = [[i for i in (range(3 * g, min(3 * g + 3, 8))) if i % NTB in tbs] for g in range(3)]
                    for step in range(2):
                        for g, ids in enumerate(groups):
                            i0, n = ids[0], len(ids)
                            den = bank[5 + g][:, 0:387].rearrange("p (i e) -> p i e", e=129)[:, i0 % 3:i0 % 3 + n, P]
                            o = dmax[:, i0:i0 + n]
                            if step == 0:
                                mark(V.scalar_tensor_tensor(o, den, -1.0, floorc[:, i0:i0 + n, h], ALU.mult, ALU.max))
                            else:
                                dve.wait_ge(dve_step, steps[0] - 2)
                                mark(V.tensor_tensor(o, den, o, ALU.max))
                    dve.wait_ge(dve_step, steps[0])
                    for d in range(2):
                        link(V.reciprocal(rden[:, d * NTB + b0:(d + 1) * NTB], dmax[:, d * NTB + b0:(d + 1) * NTB]))
                    num = lambda idx: bank[5 + idx // 3][:, (idx % 3) * 129:(idx % 3) * 129 + P]
                    for tb in tbs:
                        mark(V.tensor_scalar(Hs[:, tb, h * P:(h + 1) * P], num(tb), rden[:, tb:tb + 1], None, ALU.mult))
                    last = None
                    for tb in tbs:
                        idx = NTB + tb
                        dve.wait_ge(dve_step, steps[0] - (len(tbs) - 1 - (tb - b0)))
                        last = V.scalar_tensor_tensor(Hs[:, tb, h * P:(h + 1) * P], num(idx), rden[:, idx:idx + 1],
                                                      Hs[:, tb, h * P:(h + 1) * P], ALU.mult, ALU.add)
                    last.then_inc(hs_ready[layer], 1)
                if layer == 0:
                    mod_cols(2 * MOD_SLOTS - 1)
                    amplitudes(1)

            def after_heads(layer):
                lo, hi = cols(layer, False)
                tbs = list(range(NTB)) if layer == 0 else list(range(LTB, NTB))
                b0 = tbs[0]
                for ct in range(2):
                    dve.wait_ge(cmean_mm[layer], ct + 1)
                    V.tensor_tensor(acc2[:, ct, lo:hi], acc2[:, ct, lo:hi], bank[5 + ct][:, lo:hi],
                                    ALU.subtract).then_inc(cdev_ready[layer], 1)
                dve.wait_ge(hs_ready[layer], MH)
                link(V.tensor_tensor(hsq[:, b0:NTB, :], Hs[:, b0:NTB, :], Hs[:, b0:NTB, :], ALU.mult))
                V.tensor_reduce(ss16[:, 4 * b0:16], hsq[:, b0:NTB, :].rearrange("p b (h e) -> p (b h) e", e=P), AX.X,
                                ALU.add).then_inc(ss_ready[layer], 1)
                for ct in range(2):
                    dve.wait_ge(croot_ready[layer], ct + 1)
                    link(V.reciprocal(crs[:, ct, lo:hi], crs[:, ct, lo:hi]))
                    V.tensor_tensor(acc2[:, ct, lo:hi], acc2[:, ct, lo:hi], crs[:, ct, lo:hi],
                                    ALU.mult).then_inc(cnorm_ready[layer], 1)
                dve.wait_ge(hroot_ready[layer], 1)
                link(V.reciprocal(ss16[:, 4 * b0:16], ss16[:, 4 * b0:16]))
                last = None
                for tb in tbs:
                    for h in range(MH):
                        v = Hs[:, tb, h * P:(h + 1) * P]
                        last = V.scalar_tensor_tensor(v, v, ss16[:, 4 * tb + h:4 * tb + h + 1], sigo[:, tb, h * P:(h + 1) * P],
                                                      ALU.mult, ALU.mult)
                last.then_inc(ytok_ready[layer], 1)

            def residual(layer):
                for m in range(KT):
                    dve.wait_ge(wout_mm[layer], m + 1)
                    last = None
                    for s in streams_of(layer):
                        v = xT[:, m, s * 256:(s + 1) * 256]
                        last = V.scalar_tensor_tensor(v, bank[m % 2][:, s * 256:(s + 1) * 256], mod[:, layer, 16 + m, s:s + 1],
                                                      v, ALU.mult, ALU.add)
                    last.then_inc(xo_ready[layer], 1)

            dve.wait_ge(vec_ready, 1)
            for n in range(MOD_SLOTS):
                if n:
                    mod_cols(n - 1)
                mod_rows(n)
                if n < KT:
                    dve.wait_ge(xt_tp, n + 1)
                    V.tensor_copy(xT[:, n, :], bank[5 + n % 2][:, :]).then_inc(xt_ready, 1)
            mod_cols(MOD_SLOTS - 1)
            amplitudes(0)
            for layer in range(LAYERS):
                V.memset(apad[:, :, :, 0:HALF], 0.0)
                V.memset(apad[:, :, :, HALF + CTX:PADW], 0.0)
                at = landed(dve, ("gf", layer, 0))
                if layer:
                    dve.wait_ge(proj_mm[0], 2)
                for g in range(2):
                    src = wslot(at)[:, :, 0:16].rearrange("p k (d g h) -> p k g d h", d=2, g=2)[:, :, g]
                    last = V.tensor_copy(wgate[:, :, g, :].rearrange("p k (d h) -> p k d h", d=2), src)
                last.then_inc(wgate_ready[layer], 1)
                norm(layer, 0)
                dve.wait_ge(xr_ready[layer][0], KT)
                link(V.memset(vtok[:, :, :, P:P + 1], 1.0))
                gates(layer)
                convolution(layer)
                heads(layer)
                after_heads(layer)
                residual(layer)
                norm(layer, 1)
                if layer == 0:
                    for i in range(NHT):
                        dve.wait_ge(sil0_ready, i + 1)
                        dve.wait_ge(gu0_mm, 2 * i + 2)
                        V.tensor_tensor(act0[:, i, :], sil0[:, i % 2, :], bank[2 * (i % 2) + 1][:, :],
                                        ALU.mult).then_inc(act0_ready, 1)
                    dve.wait_ge(down0_mm, len(DOWN))
                    for m in range(KT):
                        last = None
                        for s in range(2):
                            v = xT[:, m, s * 256:(s + 1) * 256]
                            last = V.scalar_tensor_tensor(v, bank[m][:, s * 256:(s + 1) * 256], mod[:, 0, 40 + m, s:s + 1],
                                                          v, ALU.mult, ALU.add)
                        last.then_inc(x2_ready, 1)

            dve.sem_inc(act_ready, 2)
            dve.wait_ge(logit_mm, 1)
            mask = rt[:, 0:16].rearrange("p (b e) -> p b e", b=LTB)
            lg = rt[:, 16:32].rearrange("p (b e) -> p b e", b=LTB)
            hot = rt[:, 32:64].rearrange("p (r b e) -> p r b e", r=2, b=LTB)
            tie = rt[:, 64:80].rearrange("p (b e) -> p b e", b=LTB)
            top = rt[:, 80:84].rearrange("p (r b) -> p r b", r=2)
            tmx = rt[:, 84:86]
            wts = rt[:, 86:90].rearrange("p (r b) -> p r b", r=2)
            down_to = iota[:, 0:NE]
            desc = rt[:, 96:104]
            gat = rt[:, 104:120].rearrange("p (b e) -> p b e", b=LTB)
            cnt = rt[:, 120:128]
            posn = rt[:, 128:144].rearrange("p (b e) -> p b e", b=LTB)
            mxc = rt[:, 144:145]
            link(V.tensor_scalar(desc, down_to, -1.0, float(NE), ALU.mult, ALU.add))
            link(V.tensor_tensor(lg, bank[0][:, 0:16].rearrange("p (b e) -> p b e", b=LTB),
                                 rbias[:, :].unsqueeze(1).to_broadcast([P, LTB, NE]), ALU.add))
            for r in range(2):
                link(V.tensor_reduce(top[:, r, :], lg, AX.X, ALU.max))
                link(V.tensor_tensor(tie, lg, top[:, r, :].unsqueeze(2).to_broadcast([P, LTB, NE]), ALU.is_equal))
                link(V.tensor_tensor(tie, tie, desc.unsqueeze(1).to_broadcast([P, LTB, NE]), ALU.mult))
                link(V.tensor_reduce(tmx, tie, AX.X, ALU.max))
                link(V.tensor_tensor(hot[:, r], desc.unsqueeze(1).to_broadcast([P, LTB, NE]),
                                     tmx.unsqueeze(2).to_broadcast([P, LTB, NE]), ALU.is_equal))
                if r == 0:
                    link(V.scalar_tensor_tensor(lg, hot[:, 0], -3e38, lg, ALU.mult, ALU.add))
            V.tensor_tensor(mask, hot[:, 0], hot[:, 1], ALU.add).then_inc(mask_ready, 1)
            V.tensor_tensor(wts[:, 1, :], top[:, 1, :], top[:, 0, :], ALU.subtract).then_inc(wdiff_ready, 1)
            dve.wait_ge(wexp_ready, 1)
            link(V.tensor_scalar(wts[:, 0, :], wts[:, 1, :], 1.0, None, ALU.add))
            link(V.reciprocal(wts[:, 0, :], wts[:, 0, :]))
            link(V.tensor_tensor(wts[:, 1, :], wts[:, 1, :], wts[:, 0, :], ALU.mult))
            link(V.tensor_tensor(gat, hot[:, 0], wts[:, 0, :].unsqueeze(2).to_broadcast([P, LTB, NE]), ALU.mult))
            link(V.tensor_tensor(tie, hot[:, 1], wts[:, 1, :].unsqueeze(2).to_broadcast([P, LTB, NE]), ALU.mult))
            link(V.memset(gatecol[:, :, :], 0.0))
            link(V.memset(slotpos[:, :, :], -1.0))
            for r in range(2):
                link(V.tensor_tensor(gatecol[:, :, r * NE:(r + 1) * NE], gat, tie, ALU.add))
            dve.wait_ge(pos_mm, 1)
            link(V.scalar_tensor_tensor(posn, bank[1][:, 0:16].rearrange("p (b e) -> p b e", b=LTB), 1.0, mask, ALU.add, ALU.mult))
            for r in range(2):
                link(V.tensor_scalar(slotpos[:, :, r * NE:(r + 1) * NE], posn, -1.0 - P * r, None, ALU.add))
            link(V.tensor_reduce(mxc, bank[1][:, 16:24], AX.X, ALU.max))
            link(V.tensor_scalar(mxc, mxc, float(P), float(NE), ALU.is_gt, ALU.mult))
            link(V.tensor_scalar(nitems[0:1, 0:1], mxc[0:1, :], float(NE), None, ALU.add))
            dve.sem_inc(route_ready, 1)

            def build_pick(item):
                last = None
                for b in range(LTB):
                    last = V.tensor_scalar(pick[:, b, :], iota, slotpos[:, b, bass.ds(item, 1)], None, ALU.is_equal)
                last.then_inc(pick_ready, 1)

            def accumulate(r):
                last = None
                for j in range(4):
                    m = 4 * r + j
                    v = xT[:, m, CTX:TOK]
                    last = V.scalar_tensor_tensor(v, bank[6 + j // 2][:, (j % 2) * LAT:(j % 2 + 1) * LAT],
                                                  mod[:, 1, 40 + m, 1:2], v, ALU.mult, ALU.add)
                last.then_inc(xacc_ready, 1)

            build_pick(0)
            V.memset(ysb, 0.0).then_inc(y_ready, 1)
            V.memset(spread, 0.0).then_inc(spread_ready, 1)
            dve.sem_inc(xacc_ready, 1)
            dve.sem_inc(act_tp, 2)
            n_items = dve.value_load(nitems[0:1, 0:1], min_val=NE, max_val=2 * NE)
            with dve.Fori(0, n_items) as item:
                dve.wait_ge(gather_mm, item + 1)
                build_pick(item + 1)
                for b in range(LTB):
                    last = V.tensor_scalar(wpick[:, b, :], iota, slotpos[:, b, bass.ds(item, 1)],
                                           gatecol[:, b, bass.ds(item, 1)], ALU.is_equal, ALU.mult)
                last.then_inc(wpick_ready, 1)
                for j in range(GU):
                    dve.wait_ge(sil_ready, item * GU + j + 1)
                    dve.wait_ge(act_tp, item * GU + j + (2 if j == 0 else 1))
                    V.tensor_tensor(act[:, j % 2, :], sil[:, j % 2, :], bank[j % 2][:, 256:512], ALU.mult).then_inc(act_ready, 1)
                    if j < 2:
                        dve.wait_ge(scatter_mm, 2 * item + j + 1)
                        dve.wait_ge(xacc_ready, 2 * item + j + 1)
                        accumulate(j)
                    if j == 3:
                        dve.wait_ge(spread_tp, item + 1)
                        V.tensor_copy(spread, bank[3][:, 256:512]).then_inc(spread_ready, 1)
                dve.wait_ge(down_mm, (item + 1) * len(DOWN))
                V.tensor_copy(ysb[:, 0:NCOL], bank[4][:, :])
                V.tensor_copy(ysb[:, NCOL:D], bank[5][:, :]).then_inc(y_ready, 1)
            for r in range(2):
                dve.wait_ge(scatter_mm, 2 * n_items + r + 1)
                dve.wait_ge(xacc_ready, 2 * n_items + r + 1)
                accumulate(r)

            dve.wait_ge(froot_ready, 1)
            dve.wait_ge(xacc_ready, 2 * n_items + 3)
            link(V.reciprocal(rsf, rsf))
            for k in range(KT):
                v = xT[:, k, CTX:TOK]
                V.scalar_tensor_tensor(v, v, vec[:, V_FIN + k:V_FIN + k + 1], rsf, ALU.mult, ALU.mult).then_inc(fin_ready, 1)


_INS = ["x", "c", "ctx", "c_ctx", "norm1_g", "norm2_g", "w_mod", "b_mod", "w_in", "b_gate", "mlstm_norm_g", "conv_dw",
        "conv_db", "conv_norm_g", "conv_norm_b", "w_out", "ffn_w_gate_up", "ffn_w_down", "moe_w_router",
        "moe_b_router", "moe_w_gate_up", "moe_w_down", "final_norm_g"]


def _constants(np):
    t = np.zeros((P, NCONST), np.float32)
    i = np.arange(P)
    t[:, C_ID:C_ID + P] = np.eye(P)
    t[:, C_ONE:C_ONE + P] = 1.0
    t[:, C_GRP:C_GRP + P] = (i[:, None] // 64 == i[None, :] // 64) / 64.0
    t[:, C_UT:C_UT + P] = i[:, None] < i[None, :]
    t[:, C_IOTA:C_IOTA + P] = i[None, :]
    t[:, C_MF:C_MF + P] = np.where(i[:, None] <= i[None, :], 0.0, NEG)
    t[:, C_MB:C_MB + P] = np.where(i[:, None] >= i[None, :], 0.0, NEG)
    n = np.arange(256)
    for b in range(2):
        ang = 2 * np.pi * ((i[:, None] + b * P) * n[None, :] % 256) / 256.0
        t[:, C_COS + b * 256:C_COS + (b + 1) * 256] = np.cos(ang)
        t[:, C_SIN + b * 256:C_SIN + (b + 1) * 256] = -np.sin(ang)
    same = i[:, None] // 64 == i[None, :] // 64
    ang = 2 * np.pi * ((i[:, None] % 64) * (i[None, :] % 64) % 64) / 64.0
    t[:, C_BD:C_BD + P] = np.where(same, np.cos(ang), 0.0) / 128.0
    t[:, C_BD + P:C_BD + 2 * P] = np.where(same, np.sin(ang), 0.0) / 128.0
    t[:, C_EPS] = EPS
    return t


def kernel(**inputs):
    import numpy as _np
    import concourse.bacc as _bacc
    from concourse import mybir as _mybir
    from concourse.bass_utils import run_bass_kernel_spmd as _run

    nc = _bacc.Bacc("TRN2", target_bir_lowering=False, num_devices=1)
    arrays, args = {}, []
    for name in _INS:
        a = _np.ascontiguousarray(inputs[name])
        arrays[f"in_{name}_dram"] = a
        args.append(nc.dram_tensor(f"in_{name}_dram", a.shape, _mybir.dt.from_np(a.dtype), kind="ExternalInput").ap())
    table = _constants(_np)
    arrays["constants_dram"] = table
    args.append(nc.dram_tensor("constants_dram", table.shape, _mybir.dt.float32, kind="ExternalInput").ap())
    args.append(nc.dram_tensor("out_0_dram", (1, LAT, D), _mybir.dt.float32, kind="ExternalOutput").ap())
    build(nc, *args)
    r = _run(nc, [arrays], core_ids=[0])
    return r.results[0]["out_0_dram"]
```

```python
import concourse.bass as bass
from concourse import mybir
from contextlib import ExitStack

P = 128
D = 1024
KT = D // P
CTX = 256
LAT = 256
TOK = CTX + LAT
NTB = TOK // P
LTB = LAT // P
LAYERS = 2
MW = 512
MH = 4
CW = 256
TAPS = 31
HALF = TAPS // 2
PADW = CTX + 2 * HALF
HID = 2816
NHT = HID // P
NE = 8
EPS = 1e-6
PIN = 2832
NCOL = 512
UNITW = 2048
RAW = 6
SPL = 3
GU = HID // 256
DN = NHT // 2
EXP = 2 * GU + DN
TURN = -(-EXP // RAW) * RAW
MODC = 6 * D // NCOL
NEG = -1e30

C_ID, C_ONE, C_GRP, C_UT, C_IOTA, C_MF, C_MB = [P * i for i in range(7)]
C_COS = 7 * P
C_SIN = C_COS + 2 * 256
C_BD = C_SIN + 2 * 256
C_EPS = C_BD + 256
C_PERM = C_EPS + 1
C_PAIR = C_PERM + 16
NCONST = C_PAIR + 2

V_N1, V_N2, V_MG, V_DB, V_CG, V_CB, V_FIN, V_C, V_CC = 0, 16, 32, 40, 44, 48, 52, 60, 68
V_MOD = 76
V_DW = V_MOD + 96
NVEC = V_DW + LAYERS * TAPS * 2


def causal_cols(direction, sb, lat_only):
    if direction == 0:
        full = [((sb + 1) * P, TOK)] if sb < 3 else []
    else:
        full = {0: [(CTX, TOK)], 1: [(0, P), (CTX, TOK)], 2: [], 3: [(CTX, CTX + P)]}[sb]
    diag = sb
    if lat_only:
        full = [(max(a, CTX), b) for a, b in full if b > CTX]
        if sb < 2:
            diag = None
    spans = list(full)
    if diag is not None:
        spans.append((diag * P, diag * P + P))
    spans.sort()
    merged = []
    for a, b in spans:
        if merged and merged[-1][1] == a:
            merged[-1] = (merged[-1][0], b)
        else:
            merged.append((a, b))
    return diag, full, merged


def key_blocks(direction, tb):
    if direction == 0:
        return list(range(tb + 1))
    return {0: [0, 1], 1: [1], 2: [0, 1, 2, 3], 3: [0, 1, 3]}[tb]


def build(nc, x, c, ctx, c_ctx, norm1_g, norm2_g, w_mod, b_mod, w_in, b_gate, mlstm_norm_g, conv_dw, conv_db,
          conv_norm_g, conv_norm_b, w_out, ffn_w_gate_up, ffn_w_down, moe_w_router, moe_b_router,
          moe_w_gate_up, moe_w_down, final_norm_g, const_tab, out):
    f32 = mybir.dt.float32
    i32 = mybir.dt.int32
    ALU = mybir.AluOpType
    ACT = mybir.ActivationFunctionType
    AX = mybir.AxisListType

    es = ExitStack()
    with es:
        def sb(name, shape, dt=f32):
            return es.enter_context(nc.sbuf_tensor(name, shape, dt))

        def sem(name):
            return es.enter_context(nc.semaphore(name))

        def per_layer(name):
            return [sem(f"{name}_{layer}") for layer in range(LAYERS)]

        f32r = mybir.dt.float32r
        base = [nc.sbuf_base]

        def at_byte(name, offset, shape, dt=f32):
            return nc.alloc_sbuf_tensor_at(name, shape, dt, offset=offset)

        def put(name, shape, dt=f32):
            start = -(-base[0] // 32) * 32
            n = 4
            for d in shape[1:]:
                n *= d
            base[0] = start + n
            return at_byte(name, start, shape, dt)

        xT = put("xT", [P, KT, TOK])
        raw = put("raw", [P, RAW, UNITW])
        wH = put("wH", [P, SPL, UNITW], f32r)
        wL = put("wL", [P, SPL, UNITW], f32r)
        const = put("const", [P, NCONST])
        vec = put("vec", [P, NVEC])
        condr = put("condr", [P, 4 * KT + 124], f32r)
        cond = put("cond", [P, KT, 2])
        mod = put("mod", [P, LAYERS, 48, 2])
        amp = put("amp", [P, LAYERS, 2, KT, 2])
        wr = put("wr", [P, KT, NE])
        rbias = put("rbias", [P, NE])
        gbias = put("gbias", [16, LAYERS])
        acol = put("acol", [P, 2, NTB, 8])
        floorc = put("floorc", [P, 2 * NTB, MH])
        dmax = put("dmax", [P, 8])
        rden = put("rden", [P, 8])
        ss16 = put("ss16", [P, 16])
        nitems = put("nitems", [1, 2], i32)
        hH = put("hH", [P, KT, TOK], f32r)
        hL = put("hL", [P, KT, TOK], f32r)
        area = -(-base[0] // 32) * 32
        h_at, l_at = base[0] - 8 * KT * TOK, base[0] - 4 * KT * TOK

        ident = const[:, C_ID:C_ID + P]
        ones = const[:, C_ONE:C_ONE + P]
        grp = const[:, C_GRP:C_GRP + P]
        before = const[:, C_UT:C_UT + P]
        iota = const[:, C_IOTA:C_IOTA + P]
        masks = [const[:, C_MF:C_MF + P], const[:, C_MB:C_MB + P]]
        cosn = const[:, C_COS:C_COS + 512].rearrange("p (b n) -> p b n", b=2)
        sinn = const[:, C_SIN:C_SIN + 512].rearrange("p (b n) -> p b n", b=2)
        dftc = const[:, C_BD:C_BD + 256]
        eps = const[:, C_EPS:C_EPS + 1]
        perm = [const[0:16, C_PERM + 8 * i:C_PERM + 8 * i + 8] for i in range(2)]
        pair = const[0:4, C_PAIR:C_PAIR + 2]

        def u(name, at, shape, dt=f32, region=area):
            return at_byte(name, region + 4 * at, shape, dt)

        xin = u("xin", 0, [P, NTB, D])
        rows = u("rows", 4096, [P, 3, P])
        sq = u("sq", 4096, [P, KT, TOK])
        rstd = u("rstd", 8192, [P, TOK])
        hpre = u("hpre", 8704, [P, 2, TOK])
        qT = u("qT", 0, [P, MH, TOK])
        kT = u("kT", 2048, [P, MH, TOK])
        vtok = u("vtok", 4096, [P, NTB, MH, P + 1])
        fT = u("fT", 6160, [P, 2, TOK])
        apad = u("apad", 7184, [P, 2, 2, PADW])
        Hs = u("Hs", 6160, [P, NTB, MW])
        acc = u("acc", 8328, [P, 2, 2, CTX])
        acc2 = acc.rearrange("p c s t -> p c (s t)")
        sigc = u("sigc", 8328, [P, 2, TOK])
        dm = u("dm", 8328, [P, NTB, P])
        modrow = u("modrow", 12600, [4, NCOL])
        rowsg = [u(f"rowsg{r}", 9352 + 512 * r, [8, TOK]) for r in range(6)]
        gates16 = u("gates16", 9352 + 4 * 512, [16, TOK])
        sigo = u("sigo", 9352, [P, NTB, MW])
        prob = u("prob", 0, [P, 2, NTB, TOK], region=h_at)
        fab = u("fab", 0, [P, NTB, 2, 256], region=h_at)
        csq = u("csq", 2048, [P, 2, TOK], region=h_at)
        crs = u("crs", 3072, [P, 2, TOK], region=h_at)
        hsq = u("hsq", 0, [P, NTB, MW], region=h_at)
        y1 = [u(f"y1{x}", 2048 * i, [P, MH, TOK], f32r) for i, x in enumerate("HL")]
        y2 = [u(f"y2{x}", 2048 * i, [P, MH, TOK], f32r, region=l_at) for i, x in enumerate("HL")]
        act0 = u("act0", 0, [P, NHT, TOK])
        sil0 = u("sil0", NHT * TOK, [P, 2, TOK])
        a0 = [u(f"a0{x}", 0, [P, 4, TOK], f32r, region=r) for x, r in (("H", h_at), ("L", l_at))]
        hlat = u("hlat", 0, [P, KT, LAT], region=l_at)
        hxtok = u("hxtok", 0, [P, LTB, D])
        hTe = [u(f"hTe{x}", 2048 + 1024 * i, [P, KT, P], f32r) for i, x in enumerate("HL")]
        sil = u("sil", 4096, [P, 2, 256])
        act = u("act", 4608, [P, 2, 256])
        ysb = u("ysb", 5120, [P, D])
        pick = u("pick", 6144, [P, LTB, P])
        wpick = u("wpick", 6400, [P, LTB, P])
        spread = u("spread", 6656, [P, LAT])
        NITEM = 2 * NE
        slotpos = u("slotpos", 6912, [P, LTB, 24])
        gatecol = u("gatecol", 6960, [P, LTB, 24])
        rt = u("rt", 7008, [P, 160])
        actT = [u(f"actT{x}", 7168 + 2816 * i, [P, NHT, P], f32r) for i, x in enumerate("HL")]
        outsb = u("outsb", 0, [P, LTB, D], region=h_at)
        sqf = u("sqf", 0, [P, KT, LAT], region=l_at)
        rsf = u("rsf", 2048, [P, LAT], region=l_at)

        def f(ap):
            return ap.bitcast(f32)

        bank = [es.enter_context(nc.psum_tensor(f"bank{i}", [P, NCOL], f32)) for i in range(8)]

        const_in = sem("const_in")
        rows_in = sem("rows_in")
        x_in = sem("x_in")
        small_in = sem("small_in")
        raw_in = [sem(f"raw_in{r}") for r in range(RAW)]
        high_ready = sem("high_ready")
        unit_ready = sem("unit_ready")
        dve_step = sem("dve_step")
        act_step = sem("act_step")
        vec_tp = sem("vec_tp")
        vec_ready = sem("vec_ready")
        cond_ready = sem("cond_ready")
        xt_tp = sem("xt_tp")
        xt_ready = sem("xt_ready")
        mod_mm = sem("mod_mm")
        mod_row = sem("mod_row")
        mod_tp = sem("mod_tp")
        mod_col = sem("mod_col")
        mod_half = sem("mod_half")
        condh_ready = sem("condh_ready")
        condr_ready = sem("condr_ready")
        amp_ready = [[sem(f"amp_ready_{a}{b}") for b in range(2)] for a in range(LAYERS)]
        sq_ready = [[sem(f"sq_ready_{a}{b}") for b in range(2)] for a in range(LAYERS)]
        ssq_done = sem("ssq_done")
        root_ready = sem("root_ready")
        xr_ready = [[sem(f"xr_ready_{a}{b}") for b in range(2)] for a in range(LAYERS)]
        hh_ready = [[sem(f"hh_ready_{a}{b}") for b in range(2)] for a in range(LAYERS)]
        h_ready = [[sem(f"h_ready_{a}{b}") for b in range(2)] for a in range(LAYERS)]
        proj_mm = per_layer("proj_mm")
        proj_ready = per_layer("proj_ready")
        nabs_ready = per_layer("nabs_ready")
        ln_ready = sem("ln_ready")
        gate_rows = sem("gate_rows")
        gate_tp = sem("gate_tp")
        gate_cols = per_layer("gate_cols")
        fab_mm = per_layer("fab_mm")
        fab_ready = per_layer("fab_ready")
        fy_mm = per_layer("fy_mm")
        fyh_ready = per_layer("fyh_ready")
        csil_ready = per_layer("csil_ready")
        yh_ready = per_layer("yh_ready")
        score_mm = per_layer("score_mm")
        mbc_mm = per_layer("mbc_mm")
        dm_ready = per_layer("dm_ready")
        e_ready = per_layer("e_ready")
        p_ready = per_layer("p_ready")
        out_mm = per_layer("out_mm")
        hs_ready = per_layer("hs_ready")
        ss_ready = sem("ss_ready")
        hroot_ready = sem("hroot_ready")
        ytok_ready = sem("ytok_ready")
        yt_tp = per_layer("yt_tp")
        pad_ready = sem("pad_ready")
        conv_ready = sem("conv_ready")
        cmean_mm = per_layer("cmean_mm")
        cdev_ready = per_layer("cdev_ready")
        csq_ready = per_layer("csq_ready")
        cvar_mm = per_layer("cvar_mm")
        croot_ready = per_layer("croot_ready")
        cnorm_ready = per_layer("cnorm_ready")
        ycat_ready = per_layer("ycat_ready")
        wout_mm = per_layer("wout_mm")
        xo_ready = per_layer("xo_ready")
        gu0_half = sem("gu0_half")
        gu0_mm = sem("gu0_mm")
        a0h_ready = sem("a0h_ready")
        a0_ready = sem("a0_ready")
        sil0_ready = sem("sil0_ready")
        act0_ready = sem("act0_ready")
        down0_mm = sem("down0_mm")
        x2_ready = sem("x2_ready")
        logit_mm = sem("logit_mm")
        hxtok_tp = sem("hxtok_tp")
        hxtok_ready = sem("hxtok_ready")
        mask_ready = sem("mask_ready")
        wdiff_ready = sem("wdiff_ready")
        wexp_ready = sem("wexp_ready")
        pos_mm = sem("pos_mm")
        route_ready = sem("route_ready")
        pick_ready = sem("pick_ready")
        gather_mm = sem("gather_mm")
        hteh_ready = sem("hteh_ready")
        hte_ready = sem("hte_ready")
        gu_mm = sem("gu_mm")
        sil_ready = sem("sil_ready")
        act_ready = sem("act_ready")
        act_tp = sem("act_tp")
        actTh_ready = sem("actTh_ready")
        actT_ready = sem("actT_ready")
        wpick_ready = sem("wpick_ready")
        spread_tp = sem("spread_tp")
        spread_ready = sem("spread_ready")
        down_mm = sem("down_mm")
        y_ready = sem("y_ready")
        scatter_mm = sem("scatter_mm")
        xacc_ready = sem("xacc_ready")
        fsq_ready = sem("fsq_ready")
        fssq_mm = sem("fssq_mm")
        froot_ready = sem("froot_ready")
        fin_ready = sem("fin_ready")
        fin_tp = sem("fin_tp")
        out_ready = sem("out_ready")
        out_stored = sem("out_stored")

        def ksplit(w):
            return w.rearrange("(k p) n -> p k n", p=P)

        def expert_unit(gate_up, down, p):
            if p < 2 * GU:
                j, half = divmod(p, 2)
                v = ksplit(gate_up)[:, 4 * half:4 * half + 4, :]
                return [(0, v[:, :, j * 256:j * 256 + 256]), (256, v[:, :, HID + j * 256:HID + j * 256 + 256])]
            i = p - 2 * GU
            return [(0, ksplit(down)[:, 2 * i:2 * i + 2, :])]

        def view(t, slot, name, p=0):
            k = 4 if name == "mod" or (name == "mlp" and p < 2 * GU) else 2 if name == "mlp" else KT
            return t[:, slot, :].rearrange("p (k c) -> p k c", k=k)

        stream = []
        MODS = [(0, n) for n in range(MODC)] + [(1, n) for n in range(MODC)]
        EARLY = 4

        def mod_stream(lo, hi):
            for layer, n in MODS[lo:hi]:
                for half in range(2):
                    v = ksplit(w_mod[layer])[:, 4 * half:4 * half + 4, n * NCOL:(n + 1) * NCOL]
                    stream.append(("mod", layer, 2 * n + half, [(0, v)]))

        O_G = 4 * MW
        O_F = O_G + 16
        IN_UNITS = [("g", 0, O_G, P), ("f", 0, O_F, 256), ("cu", 0, O_F + 256, 256), ("cg", 0, O_F + 512, 256)]
        IN_UNITS += [(name, i, at + 256 * i, 256) for name, at in (("q", 0), ("k", MW), ("v", 2 * MW), ("o", 3 * MW))
                     for i in range(2)]
        mod_stream(0, EARLY)
        for layer in range(LAYERS):
            for name, i, at, w in IN_UNITS:
                stream.append((name, layer, i, [(0, ksplit(w_in[layer])[:, :, at:at + w])]))
            if layer == 0:
                mod_stream(EARLY, 2 * MODC)
            for n in range(4):
                stream.append(("wout", layer, n, [(0, ksplit(w_out[layer])[:, :, n * 256:(n + 1) * 256])]))
            if layer == 0:
                for p in range(EXP):
                    stream.append(("mlp", 0, p, expert_unit(ffn_w_gate_up[0], ffn_w_down[0], p)))
        place = {(name, layer, i): n for n, (name, layer, i, _) in enumerate(stream)}
        BASE = len(stream)

        def load(eng, n, name, p, pieces):
            for off, src in pieces:
                dst = view(raw, n % RAW, name, p)[:, :, off:off + src.shape[2]]
                eng.dma_start(dst, src).then_inc(raw_in[n % RAW], 32 // len(pieces))

        def unit_cols(t, slot, name):
            return view(t, slot, name)[:, :, 0:P] if name == "g" else t[:, slot, :]

        def halves(eng, name, layer, i):
            n = place[name, layer, i]
            eng.wait_ge(unit_ready, n + 1)
            return [view(t, n % SPL, name, i) for t in (wH, wL)]

        def proj_outputs(layer):
            tbs = range(NTB) if layer == 0 else range(LTB, NTB)
            units = [("g", 0), ("f", 0), ("f", 1), ("gi", 0), ("gf", 0), ("cu", 0), ("cu", 1), ("cg", 0), ("cg", 1)]
            units += [("q", h) for h in range(MH)] + [("k", h) for h in range(MH)]
            units += [("v", (half, b)) for half in range(2) for b in range(NTB)]
            units += [("o", (half, b)) for half in range(2) for b in tbs]
            return units

        outputs_of = [proj_outputs(layer) for layer in range(LAYERS)]

        def unit_of(kind, i):
            if kind in ("gi", "gf"):
                return None
            return (kind, i[0]) if kind in ("v", "o") else (kind, i // 2) if kind in ("q", "k") else (kind, 0)

        def output_count(layer, kind, i):
            return outputs_of[layer].index((kind, i)) + 1

        def mod_index(layer, n):
            return layer * MODC + n

        def mod_bank(g):
            return bank[7] if g < EARLY and g % 2 else bank[4]

        def consumed(n):
            name, layer, i, _ = stream[n]
            if name == "mod":
                g = mod_index(layer, i // 2)
                return (mod_mm if i % 2 else mod_half), g + 1
            if name == "wout":
                return wout_mm[layer], 2 * (i + 1)
            if name == "mlp" and i < 2 * GU:
                return (gu0_mm, 4 * (i // 2 + 1)) if i % 2 else (gu0_half, i // 2 + 1)
            if name == "mlp":
                return down0_mm, 2 * (i - 2 * GU + 1)
            return proj_mm[layer], max(m + 1 for m, (kind, j) in enumerate(outputs_of[layer]) if unit_of(kind, j) == (name, i))

        def cols(layer, both):
            return (0, TOK) if layer == 0 or both else (CTX, TOK)

        def sum_bank(layer, i):
            return bank[0] if layer == 1 and i == 0 else bank[6]

        def streams_of(layer, both=False):
            return (0, 1) if layer == 0 or both else (1,)

        block = es.enter_context(nc.Block())

        @block.sync
        def _(sp):
            sp.dma_start(const[:, :], const_tab).then_inc(const_in, 16)
            r0, r1, r2 = rows[:, 0, :], rows[:, 1, :], rows[:, 2, :]
            flat = [(V_N1, norm1_g.rearrange("l (k p) -> (l k) p", p=P)), (V_N2, norm2_g.rearrange("l (k p) -> (l k) p", p=P)),
                    (V_MG, mlstm_norm_g.rearrange("l (k p) -> (l k) p", p=P)), (V_DB, conv_db.rearrange("l (k p) -> (l k) p", p=P)),
                    (V_CG, conv_norm_g.rearrange("l (k p) -> (l k) p", p=P)), (V_CB, conv_norm_b.rearrange("l (k p) -> (l k) p", p=P)),
                    (V_FIN, final_norm_g.rearrange("(k p) -> k p", p=P)), (V_C, c[0].rearrange("(k p) -> k p", p=P)),
                    (V_CC, c_ctx.rearrange("(k p) -> k p", p=P))]
            for at, src in flat:
                sp.dma_start(r0[at:at + src.shape[0], :], src).then_inc(rows_in, 16)
            sp.dma_start(r1[0:96, :], b_mod.rearrange("l (k p) -> (l k) p", p=P)).then_inc(rows_in, 16)
            sp.dma_start(r2[0:124, :], conv_dw.rearrange("l t (k p) -> (l t k) p", p=P)).then_inc(rows_in, 16)
            for n in range(2):
                load(sp, n, stream[n][0], stream[n][2], stream[n][3])
            sp.dma_start(xin[:, 0:2, :], ctx[0].rearrange("(b p) d -> p b d", p=P)).then_inc(x_in, 16)
            sp.dma_start(xin[:, 2:4, :], x[0].rearrange("(b p) d -> p b d", p=P)).then_inc(x_in, 16)
            for n in range(2, RAW):
                load(sp, n, stream[n][0], stream[n][2], stream[n][3])
            with nc.allow_non_contiguous_dma(reason="a few small vectors"):
                sp.dma_start(gbias[:, :], b_gate.rearrange("l r -> r l")).then_inc(small_in, 16)
                sp.dma_start(wr[:, :, :], moe_w_router[0].rearrange("(k p) e -> p k e", p=P)).then_inc(small_in, 16)
                sp.dma_start(rbias[:, :], moe_b_router.to_broadcast([P, NE])).then_inc(small_in, 16)
            for n in range(RAW, BASE):
                sp.wait_ge(unit_ready, n - RAW + 1)
                load(sp, n, stream[n][0], stream[n][2], stream[n][3])

            def expert(item, e, first, count=EXP):
                for p in range(count):
                    if p >= RAW:
                        sp.wait_ge(unit_ready, item * EXP + (BASE + p - RAW + 1))
                    elif first:
                        sp.wait_ge(unit_ready, BASE + p - RAW + 1)
                    else:
                        back = TURN - RAW if p + TURN - RAW < EXP else TURN - 2 * RAW
                        sp.wait_ge(unit_ready, item * EXP + (BASE + p + back - EXP + 1))
                    load(sp, BASE + p, "mlp", p, expert_unit(moe_w_gate_up[0, e], moe_w_down[0, e], p))

            expert(0, 0, True)
            sp.wait_ge(route_ready, 1)
            n_items = sp.value_load(nitems[0:1, 0:1], min_val=NE, max_val=2 * NE)
            with sp.Fori(1, n_items) as item:
                expert(item, item % NE, False)
            expert(n_items, 0, False, 2)
            for b in range(LTB):
                sp.wait_ge(out_ready, 2 * (b + 1))
                sp.dma_start(out[0, b * P:(b + 1) * P, :], outsb[:, b, :]).then_inc(out_stored, 16)
            sp.wait_ge(out_stored, 16 * LTB)

        @block.tensor
        def _(pe):
            mm = nc.tensor.matmul
            tp = nc.tensor.transpose

            def exact(o, stationary, moving, start, stop):
                mm(o, stationary[0], moving[0], start=start, stop=False)
                mm(o, stationary[0], moving[1], start=False, stop=False)
                return mm(o, stationary[1], moving[0], start=False, stop=stop)

            def mod_transposes(g):
                pe.wait_ge(mod_row, g + 1)
                for j in range(4):
                    last = mm(mod_bank(g)[:, 2 * j:2 * j + 2], modrow[0:4, j * P:(j + 1) * P], pair, start=True, stop=True)
                last.then_inc(mod_tp, 1)

            def mod_chunk(g):
                if g not in (0, EARLY):
                    mod_transposes(g - 1)
                before_it = g if mod_bank(g) is mod_bank(g - 1) else g - 1
                if before_it >= 1:
                    pe.wait_ge(mod_col, before_it)
                layer, n = MODS[g]
                for half in range(2):
                    w = halves(pe, "mod", layer, 2 * n + half)
                    for j in range(4):
                        k = 4 * half + j
                        for m in range(2):
                            last = mm(mod_bank(g)[:, :], condr[:, 4 * k:4 * k + P], w[m][:, j, :],
                                      start=k == 0 and m == 0, stop=k == KT - 1 and m == 1)
                    last.then_inc(mod_mm if half else mod_half, 1)

            def norm_sum(layer, i, lo, hi):
                for k in range(KT):
                    pe.wait_ge(sq_ready[layer][i], k + 1)
                    last = mm(sum_bank(layer, i)[:, lo:hi], ones, sq[:, k, lo:hi], start=k == 0, stop=k == KT - 1)
                last.then_inc(ssq_done, 1)

            def projections(layer):
                for n, (kind, i) in enumerate(outputs_of[layer]):
                    b = bank[n % 2]
                    if n >= 2:
                        pe.wait_ge(proj_ready[layer], n - 1)
                    lo, hi = cols(layer, kind in ("g", "k"))
                    if kind in ("gi", "gf"):
                        pe.wait_ge(proj_ready[layer], output_count(layer, "g", 0))
                        last = mm(b[0:8, :], perm[0 if kind == "gi" else 1], gates16[:, :], start=True, stop=True)
                        last.then_inc(proj_mm[layer], 1)
                        continue
                    w = halves(pe, unit_of(kind, i)[0], layer, unit_of(kind, i)[1])
                    for k in range(KT):
                        if n == 0:
                            pe.wait_ge(h_ready[layer][0], k + 1)
                        if kind in ("v", "o"):
                            tok = slice(i[1] * P, (i[1] + 1) * P)
                            last = exact(b[:, 0:256], [t[:, k, tok] for t in (hH, hL)], [t[:, k, :] for t in w],
                                         k == 0, k == KT - 1)
                        else:
                            j = (i % 2) * P
                            last = exact(b[:, lo:hi], [t[:, k, j:j + P] for t in w], [t[:, k, lo:hi] for t in (hH, hL)],
                                         k == 0, k == KT - 1)
                    last.then_inc(proj_mm[layer], 1)
                    if (kind, i) == ("k", MH - 1):
                        gate_transposes(layer)

            def gate_transposes(layer):
                pe.wait_ge(gate_rows, layer + 1)
                for d in range(2):
                    for b in range(NTB):
                        at = (d * NTB + b) * 8
                        tp(bank[7][:, at:at + 8], rowsg[d][:, b * P:(b + 1) * P], ident[0:8, 0:8])
                        last = tp(bank[7][:, 64 + at:72 + at], rowsg[2 + d][:, b * P:(b + 1) * P], ident[0:8, 0:8])
                last.then_inc(gate_tp, 1)

            def fourier_channels(layer):
                fb = [2, 3, 5, 6]
                for s in streams_of(layer):
                    for ct in range(2):
                        b = bank[fb[s * 2 + ct]]
                        for j in range(2):
                            tb = 2 * s + j
                            last = mm(b[:, j * 256:(j + 1) * 256], fT[:, ct, tb * P:(tb + 1) * P], dftc, start=True, stop=True)
                        last.then_inc(fab_mm[layer], 1)

            def fourier_positions(layer):
                pe.wait_ge(fab_ready[layer], 2 * len(streams_of(layer)))
                for ct in range(2):
                    for s in streams_of(layer):
                        for j in range(2):
                            tb = 2 * s + j
                            o = bank[2 + ct][:, s * 256:(s + 1) * 256]
                            mm(o, fab[:, tb, ct, 0:P], cosn[:, j, :], start=j == 0, stop=False)
                            last = mm(o, fab[:, tb, ct, P:2 * P], sinn[:, j, :], start=False, stop=j == 1)
                    last.then_inc(fy_mm[layer], 1)

            def heads(layer):
                lo, hi = cols(layer, False)
                tbs = range(NTB) if layer == 0 else range(LTB, NTB)

                def running_max(h, d):
                    if h or d:
                        pe.wait_ge(e_ready[layer], 2 * h + d)
                    mm(bank[3][:, lo:hi], ident[0:8, d * MH + h:d * MH + h + 1].to_broadcast([8, P]),
                       rowsg[4 + d][:, lo:hi], start=True, stop=True).then_inc(mbc_mm[layer], 1)

                def read_values(h, d):
                    pe.wait_ge(p_ready[layer], 2 * h + d + 1)
                    for j, tb in enumerate(tbs):
                        idx = d * NTB + tb
                        b = bank[5 + idx // 3]
                        o = b[:, (idx % 3) * 129:(idx % 3) * 129 + 129]
                        keys = key_blocks(d, tb)
                        for n, s in enumerate(keys):
                            last = mm(o, prob[:, d, s, tb * P:(tb + 1) * P], vtok[:, s, h, :],
                                      start=n == 0, stop=n == len(keys) - 1)
                    last.then_inc(out_mm[layer], 1)

                pe.wait_ge(gate_cols[layer], 2)
                pe.wait_ge(ycat_ready[layer], 2)
                pe.wait_ge(croot_ready[layer], 2)
                for h in range(MH):
                    if h:
                        pe.wait_ge(p_ready[layer], 2 * h)
                    for s in range(NTB):
                        a, z = (lo, hi) if s < 2 else (CTX, TOK)
                        o = bank[s][:, a:z] if s < 2 else bank[2][:, (s - 2) * LAT:(s - 1) * LAT]
                        last = mm(o, kT[:, h, s * P:(s + 1) * P], qT[:, h, a:z], start=True, stop=True)
                    last.then_inc(score_mm[layer], 1)
                    running_max(h, 0)
                    late_mod(layer, EARLY + 4 + 4 * h)
                    running_max(h, 1)
                    late_mod(layer, EARLY + 5 + 4 * h)
                    if h:
                        pe.wait_ge(hs_ready[layer], h)
                    read_values(h, 0)
                    late_mod(layer, EARLY + 6 + 4 * h)
                    read_values(h, 1)
                    late_mod(layer, EARLY + 7 + 4 * h)
                if layer == 0:
                    mod_transposes(2 * MODC - 1)

            def conv_mean(layer):
                lo, hi = cols(layer, False)
                pe.wait_ge(conv_ready, layer + 1)
                pe.wait_ge(proj_ready[layer], len(outputs_of[layer]))
                for ct in range(2):
                    last = mm(bank[ct][:, lo:hi], grp, acc2[:, ct, lo:hi], start=True, stop=True)
                    last.then_inc(cmean_mm[layer], 1)

            def conv_variance(layer):
                lo, hi = cols(layer, False)
                for ct in range(2):
                    pe.wait_ge(csq_ready[layer], ct + 1)
                    last = mm(bank[ct][:, lo:hi], grp, csq[:, ct, lo:hi], start=True, stop=True)
                    last.then_inc(cvar_mm[layer], 1)

            def late_mod(layer, g):
                if layer == 0:
                    mod_chunk(g)

            def y_transposes(layer):
                tbs = range(NTB) if layer == 0 else range(LTB, NTB)
                pe.wait_ge(p_ready[layer], 2 * MH)
                pe.wait_ge(e_ready[layer], 2 * MH)
                pe.wait_ge(ytok_ready, layer + 1)
                for h in range(MH):
                    for tb in tbs:
                        last = tp(bank[h][:, tb * P:(tb + 1) * P], Hs[:, tb, h * P:(h + 1) * P], ident)
                    last.then_inc(yt_tp[layer], 1)

            def out_projection(layer):
                lo, hi = cols(layer, False)
                pe.wait_ge(ycat_ready[layer], 8)
                for m in range(KT):
                    if m >= 2:
                        pe.wait_ge(xo_ready[layer], m - 1)
                    w = halves(pe, "wout", layer, m // 2)
                    for n, k in enumerate([4, 5, 6, 7, 0, 1, 2, 3]):
                        y = [t[:, k % 4, lo:hi] for t in (y1 if k < 4 else y2)]
                        last = exact(bank[m % 2][:, lo:hi], [t[:, k, (m % 2) * P:(m % 2 + 1) * P] for t in w], y,
                                     n == 0, n == KT - 1)
                    last.then_inc(wout_mm[layer], 1)

            def dense_mixer():
                for j in range(GU):
                    if j >= 2:
                        pe.wait_ge(act0_ready, 2 * (j - 1))
                    for half in range(2):
                        w = halves(pe, "mlp", 0, 2 * j + half)
                        for t in range(4):
                            off = (t % 2) * 256 + (t // 2) * P
                            for i in range(4):
                                k = 4 * half + i
                                if j == 0 and t == 0:
                                    pe.wait_ge(h_ready[0][1], k + 1)
                                last = exact(bank[4 * (j % 2) + t][:, :], [v[:, i, off:off + P] for v in w],
                                             [v[:, k, :] for v in (hH, hL)], k == 0, k == KT - 1)
                            if half:
                                last.then_inc(gu0_mm, 1)
                        if not half:
                            last.then_inc(gu0_half, 1)
                for n in range(DN):
                    w = halves(pe, "mlp", 0, 2 * GU + n)
                    for j in range(2):
                        i = 2 * n + j
                        pe.wait_ge(a0_ready, i + 1)
                        for m in range(KT):
                            last = exact(bank[m][:, :], [v[:, j, m * P:(m + 1) * P] for v in w],
                                         [v[:, i % 4, :] for v in a0], i == 0, i == NHT - 1)
                        last.then_inc(down0_mm, 1)

            pe.wait_ge(const_in, 16)
            pe.wait_ge(rows_in, 16 * 11)
            for r, (at, n) in enumerate(((0, 76), (V_MOD, 96), (V_DW, 124))):
                last = tp(bank[0][:, at:at + n], rows[0:n, r, :], ident[0:n, 0:n])
            last.then_inc(vec_tp, 1)
            pe.wait_ge(condr_ready, 1)
            for n in range(KT):
                if n == 0:
                    pe.wait_ge(x_in, 32)
                if n >= 2:
                    pe.wait_ge(xt_ready, n - 1)
                for b in range(NTB):
                    last = tp(bank[5 + n % 2][:, b * P:(b + 1) * P], xin[:, b, n * P:(n + 1) * P], ident)
                last.then_inc(xt_tp, 1)
            for g in range(EARLY):
                mod_chunk(g)
            mod_transposes(EARLY - 1)

            for layer in range(LAYERS):
                norm_sum(layer, 0, 0, TOK)
                projections(layer)
                fourier_channels(layer)
                late_mod(layer, EARLY)
                conv_mean(layer)
                late_mod(layer, EARLY + 1)
                fourier_positions(layer)
                late_mod(layer, EARLY + 2)
                conv_variance(layer)
                late_mod(layer, EARLY + 3)
                heads(layer)
                y_transposes(layer)
                out_projection(layer)
                norm_sum(layer, 1, *cols(layer, False))
                if layer == 0:
                    dense_mixer()

            pe.wait_ge(hh_ready[1][1], KT)
            pe.wait_ge(small_in, 16 * 3)
            for b in range(LTB):
                for k in range(KT):
                    last = mm(bank[0][:, b * NE:(b + 1) * NE], hlat[:, k, b * P:(b + 1) * P], wr[:, k, :],
                              start=k == 0, stop=k == KT - 1)
            last.then_inc(logit_mm, 1)
            for b in range(LTB):
                for half in range(2):
                    for j in range(4):
                        k = 4 * half + j
                        last = tp(bank[2 + 2 * b + half][:, j * P:(j + 1) * P], hlat[:, k, b * P:(b + 1) * P], ident)
                    last.then_inc(hxtok_tp, 1)
            pe.wait_ge(mask_ready, 1)
            mask = rt[:, 0:16].rearrange("p (b e) -> p b e", b=LTB)
            mm(bank[1][:, 0:8], before, mask[:, 0, :], start=True, stop=True)
            mm(bank[1][:, 8:16], ones, mask[:, 0, :], start=True, stop=False)
            mm(bank[1][:, 8:16], before, mask[:, 1, :], start=False, stop=True)
            mm(bank[1][:, 16:24], ones, mask[:, 0, :], start=True, stop=False)
            mm(bank[1][:, 16:24], ones, mask[:, 1, :], start=False, stop=True).then_inc(pos_mm, 1)

            def gather():
                for k in range(KT):
                    for b in range(LTB):
                        last = mm(bank[6 + k // 4][:, (k % 4) * P:(k % 4 + 1) * P], hxtok[:, b, k * P:(k + 1) * P],
                                  pick[:, b, :], start=b == 0, stop=b == LTB - 1)
                last.then_inc(gather_mm, 1)

            def scatter(r):
                for j in range(4):
                    m = 4 * r + j
                    last = mm(bank[6 + j // 2][:, (j % 2) * LAT:(j % 2 + 1) * LAT], ysb[:, m * P:(m + 1) * P], spread[:, :],
                              start=True, stop=True)
                last.then_inc(scatter_mm, 1)

            def transposes(item, j):
                cnt = GU * item + j
                pe.wait_ge(act_ready, cnt + 3)
                pe.wait_ge(actT_ready, cnt + (2 if j == 0 else 1))
                for i in range(2):
                    last = tp(bank[2 + j % 2][:, i * P:(i + 1) * P], act[:, j % 2, i * P:(i + 1) * P], ident)
                last.then_inc(act_tp, 1)

            def expert_halves(item, p):
                pe.wait_ge(unit_ready, item * EXP + (BASE + p + 1))
                return [view(t, (BASE + p) % SPL, "mlp", p) for t in (wH, wL)]

            pe.wait_ge(hxtok_ready, 4)
            pe.wait_ge(pick_ready, 1)
            gather()
            pe.sem_inc(down_mm, 1)
            n_items = pe.value_load(nitems[0:1, 0:1], min_val=NE, max_val=2 * NE)
            with pe.Fori(0, n_items) as item:
                pe.wait_ge(hte_ready, item + 1)
                for j in range(GU):
                    pe.wait_ge(act_ready, item * GU + j + (2 if j == 0 else 1))
                    for half in range(2):
                        w = expert_halves(item, 2 * j + half)
                        for i in range(4):
                            k = 4 * half + i
                            last = exact(bank[j % 2][:, :], [t[:, k, :] for t in hTe], [t[:, i, :] for t in w],
                                         k == 0, k == KT - 1)
                        last.then_inc(gu_mm, 1)
                    if j < 2:
                        if j == 0:
                            pe.wait_ge(y_ready, item + 1)
                            pe.wait_ge(spread_ready, item + 1)
                        pe.wait_ge(xacc_ready, 2 * item + j + 1)
                        scatter(j)
                    if j == 4:
                        pe.wait_ge(spread_ready, item + 2)
                    if j >= 1:
                        transposes(item, j - 1)
                    if j == 3:
                        pe.wait_ge(wpick_ready, item + 1)
                        pe.wait_ge(actT_ready, item * GU + 4)
                        for b in range(LTB):
                            last = tp(bank[3][:, 256 + b * P:256 + (b + 1) * P], wpick[:, b, :], ident)
                        last.then_inc(spread_tp, 1)
                pe.wait_ge(pick_ready, item + 2)
                pe.wait_ge(xacc_ready, 2 * item + 3)
                gather()
                transposes(item, GU - 1)
                for n in range(DN):
                    w = expert_halves(item, 2 * GU + n)
                    pe.wait_ge(actT_ready, item * GU + n + 3)
                    for j in range(2):
                        i = 2 * n + j
                        for half in range(2):
                            last = exact(bank[4 + half][:, :], [t[:, i, :] for t in actT],
                                         [t[:, j, half * NCOL:(half + 1) * NCOL] for t in w], i == 0, i == NHT - 1)
                    last.then_inc(down_mm, 1)
            pe.wait_ge(y_ready, n_items + 1)
            pe.wait_ge(spread_ready, n_items + 1)
            for r in range(2):
                pe.wait_ge(xacc_ready, 2 * n_items + r + 1)
                if r == 0:
                    pe.wait_ge(hte_ready, n_items + 1)
                scatter(r)

            for k in range(KT):
                pe.wait_ge(fsq_ready, k + 1)
                last = mm(bank[0][:, 0:LAT], ones, sqf[:, k, :], start=k == 0, stop=k == KT - 1)
            last.then_inc(fssq_mm, 1)
            for b in range(LTB):
                for half in range(2):
                    for j in range(4):
                        k = 4 * half + j
                        if b == 0:
                            pe.wait_ge(fin_ready, k + 1)
                        last = tp(bank[2 + 2 * b + half][:, j * P:(j + 1) * P], xT[:, k, CTX + b * P:CTX + (b + 1) * P], ident)
                    last.then_inc(fin_tp, 1)

        @block.scalar
        def _(sc):
            act_fn = nc.scalar.activation

            split = [0]

            def high_to(n):
                while split[0] < min(n, BASE + 2):
                    m = split[0]
                    name = stream[m][0] if m < BASE else "mlp"
                    sc.wait_ge(raw_in[m % RAW], 32 * (m // RAW + 1))
                    if m >= SPL:
                        sc.wait_ge(*consumed(m - SPL))
                    act_fn(unit_cols(wH, m % SPL, name), unit_cols(raw, m % RAW, name), ACT.Copy).then_inc(high_ready, 1)
                    split[0] += 1

            def late_mod(layer, g):
                if layer == 0:
                    high_to(place["mod", MODS[g][0], 2 * MODS[g][1] + 1] + SPL)

            def norm(layer, i):
                lo, hi = cols(layer, i == 0)
                for k in range(KT):
                    if layer == 0 and i == 0:
                        sc.wait_ge(xt_ready, k + 1)
                    elif i == 1:
                        sc.wait_ge(xo_ready[layer], k + 1)
                    else:
                        sc.wait_ge(x2_ready, k + 1)
                    act_fn(sq[:, k, lo:hi], xT[:, k, lo:hi], ACT.Square).then_inc(sq_ready[layer][i], 1)
                sc.wait_ge(ssq_done, 2 * layer + i + 1)
                act_fn(rstd[:, lo:hi], sum_bank(layer, i)[:, lo:hi], ACT.Sqrt, bias=eps, scale=1.0 / D).then_inc(root_ready, 1)
                for k in range(KT):
                    sc.wait_ge(xr_ready[layer][i], k + 1)
                    for s in streams_of(layer, i == 0):
                        if layer == 1 and i == 1:
                            o = hlat[:, k, :]
                        else:
                            o = hH[:, k, s * 256:(s + 1) * 256]
                        last = act_fn(o, hpre[:, k % 2, s * 256:(s + 1) * 256], ACT.Identity,
                                      bias=mod[:, layer, 24 * i + k, s:s + 1])
                    last.then_inc(hh_ready[layer][i], 1)

            def mixer(layer):
                lo, hi = cols(layer, False)
                for n, (kind, i) in enumerate(outputs_of[layer]):
                    b = bank[n % 2]
                    if unit_of(kind, i):
                        name, part = unit_of(kind, i)
                        high_to(place[name, layer, part] + SPL)
                    sc.wait_ge(proj_mm[layer], n + 1)
                    if n == 0:
                        sc.wait_ge(small_in, 16 * 3)
                        o = act_fn(gates16[:, :], b[0:16, :], ACT.Identity, bias=gbias[:, layer:layer + 1])
                    elif kind in ("gi", "gf"):
                        o = act_fn(rowsg[0 if kind == "gi" else 1][:, :], b[0:8, :], ACT.Copy)
                    elif kind == "f":
                        o = act_fn(fT[:, i, lo:hi], b[:, lo:hi], ACT.Copy)
                    elif kind == "cu":
                        ss = slice(0, 2) if layer == 0 else slice(1, 2)
                        sc.wait_ge(pad_ready, layer + 1)
                        o = act_fn(apad[:, i, ss, HALF:HALF + CTX], b[:, lo:hi].rearrange("p (s t) -> p s t", t=CTX), ACT.Copy)
                    elif kind == "cg":
                        o = act_fn(sigc[:, i, lo:hi], b[:, lo:hi], ACT.Sigmoid)
                    elif kind == "q":
                        o = act_fn(qT[:, i, lo:hi], b[:, lo:hi], ACT.Copy)
                    elif kind == "k":
                        o = act_fn(kT[:, i, :], b[:, :], ACT.Copy, scale=float(P) ** -0.5)
                    elif kind == "v":
                        half, tb = i
                        o = act_fn(vtok[:, tb, 2 * half:2 * half + 2, 0:P], b[:, 0:256].rearrange("p (h e) -> p h e", h=2), ACT.Copy)
                    else:
                        half, tb = i
                        o = act_fn(sigo[:, tb, half * 256:(half + 1) * 256], b[:, 0:256], ACT.Sigmoid)
                    o.then_inc(proj_ready[layer], 1)
                    if kind == "gf":
                        sc.wait_ge(nabs_ready[layer], 1)
                        act_fn(rowsg[2][:, :], rowsg[2][:, :], ACT.Exp).then_inc(nabs_ready[layer], 1)
                        sc.wait_ge(nabs_ready[layer], 2)
                        act_fn(rowsg[2][:, :], rowsg[2][:, :], ACT.Ln, bias=1.0).then_inc(ln_ready, 1)
                    if (kind, i) == ("k", MH - 1):
                        sc.wait_ge(gate_tp, layer + 1)
                        act_fn(acol[:, :, :, :], bank[7][:, 0:64].rearrange("p (d b r) -> p d b r", d=2, b=NTB),
                               ACT.Copy).then_inc(gate_cols[layer], 1)
                        for d in range(2):
                            m = bank[7][:, 64 + 32 * d:96 + 32 * d].rearrange("p (b r) -> p b r", b=NTB)
                            last = act_fn(floorc[:, d * NTB:(d + 1) * NTB, :], m[:, :, d * MH:(d + 1) * MH], ACT.Exp)
                        last.then_inc(gate_cols[layer], 1)
                fb = [2, 3, 5, 6]
                n = 0
                for s in streams_of(layer):
                    for ct in range(2):
                        n += 1
                        sc.wait_ge(fab_mm[layer], n)
                        act_fn(fab[:, 2 * s:2 * s + 2, ct, :], bank[fb[s * 2 + ct]][:, :].rearrange("p (b f) -> p b f", b=2),
                               ACT.Copy).then_inc(fab_ready[layer], 1)
                late_mod(layer, EARLY)
                for ct in range(2):
                    sc.wait_ge(cdev_ready[layer], ct + 1)
                    act_fn(csq[:, ct, lo:hi], acc2[:, ct, lo:hi], ACT.Square).then_inc(csq_ready[layer], 1)
                late_mod(layer, EARLY + 1)
                for ct in range(2):
                    sc.wait_ge(fy_mm[layer], ct + 1)
                    act_fn(y2[0][:, ct, lo:hi], bank[2 + ct][:, lo:hi], ACT.Copy).then_inc(fyh_ready[layer], 1)
                late_mod(layer, EARLY + 2)
                for ct in range(2):
                    sc.wait_ge(cvar_mm[layer], ct + 1)
                    act_fn(crs[:, ct, lo:hi], bank[ct][:, lo:hi], ACT.Sqrt, bias=eps).then_inc(croot_ready[layer], 1)
                late_mod(layer, EARLY + 3)
                for ct in range(2):
                    sc.wait_ge(cnorm_ready[layer], ct + 1)
                    w = layer * 2 + ct
                    act_fn(acc2[:, ct, lo:hi], acc2[:, ct, lo:hi], ACT.Silu, bias=vec[:, V_CB + w:V_CB + w + 1],
                           scale=vec[:, V_CG + w:V_CG + w + 1]).then_inc(csil_ready[layer], 1)
                sc.wait_ge(gate_cols[layer], 2)
                sc.wait_ge(ycat_ready[layer], 4)
                for h in range(MH):
                    for d in range(2):
                        sc.wait_ge(mbc_mm[layer], 2 * h + d + 1)
                        if h:
                            sc.wait_ge(out_mm[layer], 2 * (h - 1) + d + 1)
                        sc.wait_ge(dm_ready[layer], 2 * h + d + 1)
                        last = None
                        for s in range(NTB):
                            diag, full, _ = causal_cols(d, s, layer == 1)
                            bias = acol[:, d, s, d * MH + h:d * MH + h + 1]
                            for a, z in full:
                                last = act_fn(prob[:, d, s, a:z], bank[3][:, a:z], ACT.Exp, bias=bias, scale=-1.0)
                            if diag is not None:
                                last = act_fn(prob[:, d, s, diag * P:(diag + 1) * P], dm[:, diag, :], ACT.Exp, bias=bias)
                        last.then_inc(e_ready[layer], 1)
                        late_mod(layer, EARLY + 4 + 4 * h + d)
                    late_mod(layer, EARLY + 7 + 4 * h)
                sc.wait_ge(ss_ready, layer + 1)
                act_fn(ss16[:, :], ss16[:, :], ACT.Sqrt, bias=eps, scale=1.0 / P).then_inc(hroot_ready, 1)
                for h in range(MH):
                    sc.wait_ge(yt_tp[layer], h + 1)
                    w = V_MG + layer * MH + h
                    act_fn(y1[0][:, h, lo:hi], bank[h][:, lo:hi], ACT.Copy, scale=vec[:, w:w + 1]).then_inc(yh_ready[layer], 1)
                for n in range(4):
                    high_to(place["wout", layer, n] + SPL)

            sc.wait_ge(vec_tp, 1)
            act_fn(vec[:, :], bank[0][:, 0:NVEC], ACT.Copy).then_inc(vec_ready, 1)
            sc.wait_ge(vec_ready, 1)
            act_fn(cond[:, :, 0], vec[:, V_CC:V_CC + KT], ACT.Silu).then_inc(cond_ready, 1)
            act_fn(cond[:, :, 1], vec[:, V_C:V_C + KT], ACT.Silu).then_inc(cond_ready, 1)
            high_to(SPL)
            sc.wait_ge(cond_ready, 2)
            condv = condr[:, 0:4 * KT].rearrange("p (k m s) -> p k m s", k=KT, m=2)
            sc.wait_ge(condh_ready, 1)
            act_fn(condv[:, :, 0, :], cond[:, :, :], ACT.Copy).then_inc(condh_ready, 1)
            for g in range(EARLY):
                late_mod(0, g)
            for layer in range(LAYERS):
                norm(layer, 0)
                mixer(layer)
                norm(layer, 1)
                if layer == 0:
                    for j in range(GU):
                        high_to(place["mlp", 0, 2 * j + 1] + SPL)
                        for t in range(2):
                            i = 2 * j + t
                            sc.wait_ge(gu0_mm, 4 * j + 2 * t + 1)
                            if i >= 2:
                                sc.wait_ge(act0_ready, i - 1)
                            act_fn(sil0[:, t, :], bank[4 * (j % 2) + 2 * t][:, :], ACT.Silu).then_inc(sil0_ready, 1)

                    def hidden_high(i):
                        if i >= 4:
                            sc.wait_ge(down0_mm, i - 3)
                        act_fn(a0[0][:, i % 4, :], act0[:, i, :], ACT.Copy).then_inc(a0h_ready, 1)

                    sc.wait_ge(act0_ready, NHT)
                    hidden_high(0)
                    hidden_high(1)
                    for n in range(DN):
                        if n < DN - 1:
                            hidden_high(2 * n + 2)
                            hidden_high(2 * n + 3)
                        high_to(place["mlp", 0, 2 * GU + n] + SPL)
            for n in range(4):
                sc.wait_ge(hxtok_tp, n + 1)
                b, half = n // 2, n % 2
                act_fn(hxtok[:, b, half * NCOL:(half + 1) * NCOL], bank[2 + n][:, :], ACT.Copy).then_inc(hxtok_ready, 1)

            sc.wait_ge(wdiff_ready, 1)
            act_fn(rt[:, 88:90], rt[:, 88:90], ACT.Exp).then_inc(wexp_ready, 1)

            def gathered():
                for half in range(2):
                    last = act_fn(hTe[0][:, 4 * half:4 * half + 4, :], bank[6 + half][:, :].rearrange("p (k t) -> p k t", k=4), ACT.Copy)
                last.then_inc(hteh_ready, 1)

            def transposed(item, j):
                sc.wait_ge(act_tp, item * GU + j + 3)
                act_fn(actT[0][:, 2 * j:2 * j + 2, :], bank[2 + j % 2][:, 0:256].rearrange("p (i t) -> p i t", i=2),
                       ACT.Copy).then_inc(actTh_ready, 1)

            def high(item, p, ahead=False):
                n = BASE + p
                uses = TURN // RAW if p % RAW < EXP - (TURN - RAW) else TURN // RAW - 1
                before = (BASE - 1 - n % RAW) // RAW + 1
                if ahead:
                    sc.wait_ge(raw_in[n % RAW], item * (32 * uses) + 32 * (before + uses + p // RAW + 1))
                    sc.wait_ge(down_mm, item * DN + (DN - 3 + p + 2))
                else:
                    sc.wait_ge(raw_in[n % RAW], item * (32 * uses) + 32 * (before + p // RAW + 1))
                    if p == 2:
                        sc.wait_ge(down_mm, item * DN + 1)
                    elif p - SPL < 2 * GU:
                        sc.wait_ge(gu_mm, item * (2 * GU) + p - SPL + 1)
                    else:
                        sc.wait_ge(down_mm, item * DN + (p - SPL - 2 * GU + 2))
                act_fn(wH[:, n % SPL, :], raw[:, n % RAW, :], ACT.Copy).then_inc(high_ready, 1)

            sc.wait_ge(gather_mm, 1)
            gathered()
            sc.wait_ge(*consumed(BASE - 1))
            sc.wait_ge(route_ready, 1)
            n_items = sc.value_load(nitems[0:1, 0:1], min_val=NE, max_val=2 * NE)
            with sc.Fori(0, n_items) as item:
                for j in range(GU):
                    high(item, 2 * j + 2)
                    high(item, 2 * j + 3)
                    sc.wait_ge(gu_mm, item * (2 * GU) + 2 * j + 2)
                    sc.wait_ge(act_ready, item * GU + j + (2 if j == 0 else 1))
                    act_fn(sil[:, j % 2, :], bank[j % 2][:, 0:256], ACT.Silu).then_inc(sil_ready, 1)
                    if j == 1:
                        sc.wait_ge(y_ready, item + 1)
                    if j >= 1:
                        transposed(item, j - 1)
                sc.wait_ge(gather_mm, item + 2)
                gathered()
                transposed(item, GU - 1)
                for p in range(2 * GU + 2, EXP):
                    high(item, p)
                for p in range(2):
                    high(item, p, ahead=True)
                sc.wait_ge(down_mm, item * DN + DN + 1)
                act_fn(ysb[:, 0:NCOL], bank[4][:, :], ACT.Copy)
                act_fn(ysb[:, NCOL:D], bank[5][:, :], ACT.Copy).then_inc(y_ready, 1)
            for k in range(KT):
                sc.wait_ge(xacc_ready, 2 * n_items + 3)
                act_fn(sqf[:, k, :], xT[:, k, CTX:TOK], ACT.Square).then_inc(fsq_ready, 1)
            sc.wait_ge(fssq_mm, 1)
            act_fn(rsf[:, :], bank[0][:, 0:LAT], ACT.Sqrt, bias=eps, scale=1.0 / D).then_inc(froot_ready, 1)
            for n in range(4):
                sc.wait_ge(fin_tp, n + 1)
                b, half = n // 2, n % 2
                act_fn(outsb[:, b, half * NCOL:(half + 1) * NCOL], bank[2 + n][:, :], ACT.Copy).then_inc(out_ready, 1)

        @block.vector
        def _(dve):
            V = nc.vector
            steps = [0]

            def link(ins):
                steps[0] += 1
                ins.then_inc(dve_step, 1)
                dve.wait_ge(dve_step, steps[0])

            def mark(ins):
                steps[0] += 1
                ins.then_inc(dve_step, 1)
                return steps[0]

            split = [0]

            def low_to(n):
                while split[0] < min(n, BASE + 2):
                    m = split[0]
                    name = stream[m][0] if m < BASE else "mlp"
                    dve.wait_ge(high_ready, m + 1)
                    V.tensor_tensor(unit_cols(wL, m % SPL, name), unit_cols(raw, m % RAW, name),
                                    f(unit_cols(wH, m % SPL, name)), ALU.subtract).then_inc(unit_ready, 1)
                    split[0] += 1

            def mod_rows(g):
                dve.wait_ge(mod_mm, g + 1)
                if g:
                    dve.wait_ge(mod_tp, g)
                V.tensor_copy(modrow[:, :], mod_bank(g)[0:4, :]).then_inc(mod_row, 1)

            def mod_cols(g):
                layer, n = MODS[g]
                dve.wait_ge(mod_tp, g + 1)
                at = V_MOD + layer * 48 + 4 * n
                V.tensor_tensor(mod[:, layer, 4 * n:4 * n + 4, :], mod_bank(g)[:, 0:8].rearrange("p (j s) -> p j s", s=2),
                                vec[:, at:at + 4].unsqueeze(2).to_broadcast([P, 4, 2]), ALU.add).then_inc(mod_col, 1)

            def late_mod(layer, g):
                if layer == 0:
                    if g not in (0, EARLY):
                        mod_cols(g - 1)
                    low_to(place["mod", MODS[g][0], 2 * MODS[g][1] + 1] + SPL)
                    mod_rows(g)

            def amplitude(layer, i):
                dve.wait_ge(mod_col, EARLY if layer == 0 and i == 0 else 2 * MODC)
                sc1 = mod[:, layer, 24 * i + 8:24 * i + 16, :]
                g = vec[:, 16 * i + 8 * layer:16 * i + 8 * layer + 8].unsqueeze(2).to_broadcast([P, KT, 2])
                link(V.tensor_scalar(amp[:, layer, i], sc1, 1.0, None, ALU.add))
                V.tensor_tensor(amp[:, layer, i], amp[:, layer, i], g, ALU.mult).then_inc(amp_ready[layer][i], 1)

            def norm(layer, i):
                lo, hi = cols(layer, i == 0)
                dve.wait_ge(amp_ready[layer][i], 1)
                dve.wait_ge(root_ready, 2 * layer + i + 1)
                link(V.reciprocal(rstd[:, lo:hi], rstd[:, lo:hi]))
                ss = streams_of(layer, i == 0)
                latent_only = layer == 1 and i == 1

                def low(k):
                    dve.wait_ge(hh_ready[layer][i], k + 1)
                    for s in ss:
                        c = slice(s * 256, (s + 1) * 256)
                        last = V.scalar_tensor_tensor(hL[:, k, c], hpre[:, k % 2, c], mod[:, layer, 24 * i + k, s:s + 1],
                                                      f(hH[:, k, c]), ALU.add, ALU.subtract)
                    last.then_inc(h_ready[layer][i], 1)

                for k in range(KT):
                    if latent_only:
                        if k >= 2:
                            dve.wait_ge(hh_ready[layer][i], k - 1)
                    elif k >= 2:
                        low(k - 2)
                        dve.wait_ge(h_ready[layer][i], k - 1)
                    for s in ss:
                        c = slice(s * 256, (s + 1) * 256)
                        last = V.scalar_tensor_tensor(hpre[:, k % 2, c], xT[:, k, c], amp[:, layer, i, k, s:s + 1],
                                                      rstd[:, c], ALU.mult, ALU.mult)
                    last.then_inc(xr_ready[layer][i], 1)
                if not latent_only:
                    low(KT - 2)
                    low(KT - 1)

            def gates(layer):
                R = [r[:, :] for r in rowsg]
                dve.wait_ge(proj_ready[layer], output_count(layer, "gf", 0))
                ins = V.scalar_tensor_tensor(R[2], R[1], -1.0, R[1], ALU.mult, ALU.min)
                ins.then_inc(nabs_ready[layer], 1)
                dve.wait_ge(ln_ready, layer + 1)
                link(V.scalar_tensor_tensor(R[1], R[1], 0.0, R[2], ALU.min, ALU.subtract))
                onesrow = ones[0:8, 0:1].to_broadcast([8, TOK])

                def run(d, o, src, first, kind):
                    if d == 0:
                        spans = [slice(0, TOK)]
                    else:
                        spans = [slice(CTX - 1, None, -1), slice(TOK - 1, CTX - 1, -1)]
                    init = first
                    for s in spans:
                        a = src[:, s]
                        if kind == "sum":
                            link(V.tensor_tensor_scan(o[:, s], onesrow[:, s], a, init, ALU.mult, ALU.add))
                        else:
                            link(V.tensor_tensor_scan(o[:, s], a, a, init, ALU.max, ALU.max))
                        init = o[:, 0:1]

                dve.wait_ge(proj_mm[layer], output_count(layer, "gf", 0))
                for d in range(2):
                    run(d, R[2 + d], R[1], 0.0, "sum")
                link(V.tensor_tensor(R[1], R[0], R[3], ALU.subtract))
                link(V.tensor_tensor(R[0], R[0], R[2], ALU.subtract))
                for d in range(2):
                    run(d, R[4 + d], R[d], NEG, "max")
                for d in range(2):
                    ins = V.scalar_tensor_tensor(R[2 + d], R[2 + d], -1.0, R[4 + d], ALU.mult, ALU.subtract)
                    if d == 0:
                        link(ins)
                    else:
                        ins.then_inc(gate_rows, 1)

            def convolution(layer):
                ss = slice(0, 2) if layer == 0 else slice(1, 2)
                lo, hi = cols(layer, False)
                n0 = place["g", layer, 0]
                dve.wait_ge(proj_ready[layer], output_count(layer, "cg", 1))
                for ct in range(2):
                    v = apad[:, ct, ss, HALF:HALF + CTX]
                    link(V.tensor_tensor(v, v, sigc[:, ct, lo:hi].rearrange("p (s t) -> p s t", t=CTX), ALU.mult))
                ahead = 6
                for t in range(TAPS):
                    if t % 4 == 3:
                        ahead += 1
                        low_to(n0 + ahead)
                    for ct in range(2):
                        at = V_DW + layer * 2 * TAPS + t * 2 + ct
                        src = apad[:, ct, ss, t:t + CTX]
                        if t == 0:
                            db = vec[:, V_DB + 2 * layer + ct:V_DB + 2 * layer + ct + 1]
                            mark(V.tensor_scalar(acc[:, ct, ss, :], src, vec[:, at:at + 1], db, ALU.mult, ALU.add))
                        else:
                            dve.wait_ge(dve_step, steps[0] - 1)
                            mark(V.scalar_tensor_tensor(acc[:, ct, ss, :], src, vec[:, at:at + 1], acc[:, ct, ss, :],
                                                        ALU.mult, ALU.add))
                dve.wait_ge(dve_step, steps[0])
                dve.sem_inc(conv_ready, 1)
                low_to(place["o", layer, 1] + SPL)

            def conv_finish(layer):
                lo, hi = cols(layer, False)
                late_mod(layer, EARLY)
                for ct in range(2):
                    dve.wait_ge(cmean_mm[layer], ct + 1)
                    V.tensor_tensor(acc2[:, ct, lo:hi], acc2[:, ct, lo:hi], bank[ct][:, lo:hi],
                                    ALU.subtract).then_inc(cdev_ready[layer], 1)
                late_mod(layer, EARLY + 1)
                for ct in range(2):
                    dve.wait_ge(fyh_ready[layer], ct + 1)
                    V.tensor_tensor(y2[1][:, ct, lo:hi], bank[2 + ct][:, lo:hi], f(y2[0][:, ct, lo:hi]),
                                    ALU.subtract).then_inc(ycat_ready[layer], 1)
                late_mod(layer, EARLY + 2)
                for ct in range(2):
                    dve.wait_ge(croot_ready[layer], ct + 1)
                    link(V.reciprocal(crs[:, ct, lo:hi], crs[:, ct, lo:hi]))
                    V.tensor_tensor(acc2[:, ct, lo:hi], acc2[:, ct, lo:hi], crs[:, ct, lo:hi],
                                    ALU.mult).then_inc(cnorm_ready[layer], 1)
                late_mod(layer, EARLY + 3)
                for ct in range(2):
                    dve.wait_ge(csil_ready[layer], ct + 1)
                    link(V.tensor_copy(y2[0][:, 2 + ct, lo:hi], acc2[:, ct, lo:hi]))
                    V.tensor_tensor(y2[1][:, 2 + ct, lo:hi], acc2[:, ct, lo:hi], f(y2[0][:, 2 + ct, lo:hi]),
                                    ALU.subtract).then_inc(ycat_ready[layer], 1)

            def heads(layer):
                tbs = list(range(NTB)) if layer == 0 else list(range(LTB, NTB))
                b0 = tbs[0]

                def differences(h, d):
                    dve.wait_ge(mbc_mm[layer], 2 * h + d + 1)
                    V.tensor_tensor(dm[:, b0:NTB, :], masks[d].unsqueeze(1).to_broadcast([P, NTB - b0, P]),
                                    bank[3][:, b0 * P:TOK].rearrange("p (b t) -> p b t", t=P),
                                    ALU.subtract).then_inc(dm_ready[layer], 1)

                def weigh(h, d):
                    dve.wait_ge(e_ready[layer], 2 * h + d + 1)
                    dve.wait_ge(score_mm[layer], h + 1)
                    last = None
                    for s in range(NTB):
                        for a, z in causal_cols(d, s, layer == 1)[2]:
                            sco = bank[s][:, a:z] if s < 2 else bank[2][:, (s - 2) * LAT + a - CTX:(s - 2) * LAT + z - CTX]
                            last = V.tensor_tensor(prob[:, d, s, a:z], prob[:, d, s, a:z], sco, ALU.mult)
                    last.then_inc(p_ready[layer], 1)

                dve.wait_ge(ycat_ready[layer], 4)
                for h in range(MH):
                    differences(h, 0)
                    late_mod(layer, EARLY + 4 + 4 * h)
                    weigh(h, 0)
                    differences(h, 1)
                    late_mod(layer, EARLY + 5 + 4 * h)
                    weigh(h, 1)
                    late_mod(layer, EARLY + 6 + 4 * h)
                    dve.wait_ge(out_mm[layer], 2 * h + 2)
                    groups = [[i for i in (range(3 * g, min(3 * g + 3, 8))) if i % NTB in tbs] for g in range(3)]
                    for step in range(2):
                        for g, ids in enumerate(groups):
                            i0, n = ids[0], len(ids)
                            den = bank[5 + g][:, 0:387].rearrange("p (i e) -> p i e", e=129)[:, i0 % 3:i0 % 3 + n, P]
                            o = dmax[:, i0:i0 + n]
                            if step == 0:
                                mark(V.scalar_tensor_tensor(o, den, -1.0, floorc[:, i0:i0 + n, h], ALU.mult, ALU.max))
                            else:
                                dve.wait_ge(dve_step, steps[0] - 2)
                                mark(V.tensor_tensor(o, den, o, ALU.max))
                    dve.wait_ge(dve_step, steps[0])
                    for d in range(2):
                        link(V.reciprocal(rden[:, d * NTB + b0:(d + 1) * NTB], dmax[:, d * NTB + b0:(d + 1) * NTB]))
                    num = lambda idx: bank[5 + idx // 3][:, (idx % 3) * 129:(idx % 3) * 129 + P]
                    for tb in tbs:
                        mark(V.tensor_scalar(Hs[:, tb, h * P:(h + 1) * P], num(tb), rden[:, tb:tb + 1], None, ALU.mult))
                    last = None
                    for tb in tbs:
                        idx = NTB + tb
                        dve.wait_ge(dve_step, steps[0] - (len(tbs) - 1 - (tb - b0)))
                        last = V.scalar_tensor_tensor(Hs[:, tb, h * P:(h + 1) * P], num(idx), rden[:, idx:idx + 1],
                                                      Hs[:, tb, h * P:(h + 1) * P], ALU.mult, ALU.add)
                    last.then_inc(hs_ready[layer], 1)
                    late_mod(layer, EARLY + 7 + 4 * h)
                if layer == 0:
                    mod_cols(2 * MODC - 1)
                    amplitude(0, 1)
                    amplitude(1, 0)
                    amplitude(1, 1)

            def after_heads(layer):
                lo, hi = cols(layer, False)
                tbs = list(range(NTB)) if layer == 0 else list(range(LTB, NTB))
                b0 = tbs[0]
                dve.wait_ge(hs_ready[layer], MH)
                link(V.tensor_tensor(hsq[:, b0:NTB, :], Hs[:, b0:NTB, :], Hs[:, b0:NTB, :], ALU.mult))
                V.tensor_reduce(ss16[:, 4 * b0:16], hsq[:, b0:NTB, :].rearrange("p b (h e) -> p (b h) e", e=P), AX.X,
                                ALU.add).then_inc(ss_ready, 1)
                dve.wait_ge(hroot_ready, layer + 1)
                link(V.reciprocal(ss16[:, 4 * b0:16], ss16[:, 4 * b0:16]))
                last = None
                for tb in tbs:
                    for h in range(MH):
                        v = Hs[:, tb, h * P:(h + 1) * P]
                        last = V.scalar_tensor_tensor(v, v, ss16[:, 4 * tb + h:4 * tb + h + 1], sigo[:, tb, h * P:(h + 1) * P],
                                                      ALU.mult, ALU.mult)
                last.then_inc(ytok_ready, 1)
                for h in range(MH):
                    dve.wait_ge(yh_ready[layer], h + 1)
                    w = V_MG + layer * MH + h
                    V.scalar_tensor_tensor(y1[1][:, h, lo:hi], bank[h][:, lo:hi], vec[:, w:w + 1], f(y1[0][:, h, lo:hi]),
                                           ALU.mult, ALU.subtract).then_inc(ycat_ready[layer], 1)

            def residual(layer):
                for m in range(KT):
                    low_to(place["wout", layer, m // 2] + SPL)
                    dve.wait_ge(wout_mm[layer], m + 1)
                    last = None
                    for s in streams_of(layer):
                        v = xT[:, m, s * 256:(s + 1) * 256]
                        last = V.scalar_tensor_tensor(v, bank[m % 2][:, s * 256:(s + 1) * 256], mod[:, layer, 16 + m, s:s + 1],
                                                      v, ALU.mult, ALU.add)
                    last.then_inc(xo_ready[layer], 1)

            dve.wait_ge(vec_ready, 1)
            V.memset(f(condr[:, :]), 0.0).then_inc(condh_ready, 1)
            dve.wait_ge(condh_ready, 2)
            condv = condr[:, 0:4 * KT].rearrange("p (k m s) -> p k m s", k=KT, m=2)
            V.tensor_tensor(condv[:, :, 1, :], cond[:, :, :], f(condv[:, :, 0, :]), ALU.subtract).then_inc(condr_ready, 1)
            low_to(2)
            for n in range(KT):
                dve.wait_ge(xt_tp, n + 1)
                V.tensor_copy(xT[:, n, :], bank[5 + n % 2][:, :]).then_inc(xt_ready, 1)
            for g in range(EARLY):
                late_mod(0, g)
            mod_cols(EARLY - 1)
            amplitude(0, 0)
            for layer in range(LAYERS):
                norm(layer, 0)
                dve.wait_ge(h_ready[layer][0], KT)
                V.memset(apad[:, :, :, 0:HALF], 0.0)
                V.memset(apad[:, :, :, HALF + CTX:PADW], 0.0).then_inc(pad_ready, 1)
                link(V.memset(vtok[:, :, :, P:P + 1], 1.0))
                n0 = place["g", layer, 0]
                low_to(n0 + SPL + 1)
                gates(layer)
                low_to(n0 + SPL + 3)
                convolution(layer)
                conv_finish(layer)
                heads(layer)
                after_heads(layer)
                residual(layer)
                norm(layer, 1)
                if layer == 0:
                    for j in range(GU):
                        low_to(place["mlp", 0, 2 * j + 1] + SPL)
                        for t in range(2):
                            i = 2 * j + t
                            dve.wait_ge(sil0_ready, i + 1)
                            dve.wait_ge(gu0_mm, 4 * j + 2 * t + 2)
                            V.tensor_tensor(act0[:, i, :], sil0[:, t, :], bank[4 * (j % 2) + 2 * t + 1][:, :],
                                            ALU.mult).then_inc(act0_ready, 1)

                    def hidden_low(i):
                        dve.wait_ge(a0h_ready, i + 1)
                        V.tensor_tensor(a0[1][:, i % 4, :], act0[:, i, :], f(a0[0][:, i % 4, :]),
                                        ALU.subtract).then_inc(a0_ready, 1)

                    hidden_low(0)
                    hidden_low(1)
                    for n in range(DN):
                        if n < DN - 1:
                            hidden_low(2 * n + 2)
                            hidden_low(2 * n + 3)
                        low_to(place["mlp", 0, 2 * GU + n] + SPL)
                    dve.wait_ge(down0_mm, NHT)
                    for m in range(KT):
                        last = None
                        for s in range(2):
                            v = xT[:, m, s * 256:(s + 1) * 256]
                            last = V.scalar_tensor_tensor(v, bank[m][:, s * 256:(s + 1) * 256], mod[:, 0, 40 + m, s:s + 1],
                                                          v, ALU.mult, ALU.add)
                        last.then_inc(x2_ready, 1)

            dve.sem_inc(act_ready, 2)
            dve.wait_ge(logit_mm, 1)
            mask = rt[:, 0:16].rearrange("p (b e) -> p b e", b=LTB)
            lg = rt[:, 16:32].rearrange("p (b e) -> p b e", b=LTB)
            hot = rt[:, 32:64].rearrange("p (r b e) -> p r b e", r=2, b=LTB)
            tie = rt[:, 64:80].rearrange("p (b e) -> p b e", b=LTB)
            top = rt[:, 80:84].rearrange("p (r b) -> p r b", r=2)
            tmx = rt[:, 84:86]
            wts = rt[:, 86:90].rearrange("p (r b) -> p r b", r=2)
            down_to = iota[:, 0:NE]
            desc = rt[:, 96:104]
            gat = rt[:, 104:120].rearrange("p (b e) -> p b e", b=LTB)
            cnt = rt[:, 120:128]
            posn = rt[:, 128:144].rearrange("p (b e) -> p b e", b=LTB)
            mxc = rt[:, 144:145]
            link(V.tensor_scalar(desc, down_to, -1.0, float(NE), ALU.mult, ALU.add))
            link(V.tensor_tensor(lg, bank[0][:, 0:16].rearrange("p (b e) -> p b e", b=LTB),
                                 rbias[:, :].unsqueeze(1).to_broadcast([P, LTB, NE]), ALU.add))
            for r in range(2):
                link(V.tensor_reduce(top[:, r, :], lg, AX.X, ALU.max))
                link(V.tensor_tensor(tie, lg, top[:, r, :].unsqueeze(2).to_broadcast([P, LTB, NE]), ALU.is_equal))
                link(V.tensor_tensor(tie, tie, desc.unsqueeze(1).to_broadcast([P, LTB, NE]), ALU.mult))
                link(V.tensor_reduce(tmx, tie, AX.X, ALU.max))
                link(V.tensor_tensor(hot[:, r], desc.unsqueeze(1).to_broadcast([P, LTB, NE]),
                                     tmx.unsqueeze(2).to_broadcast([P, LTB, NE]), ALU.is_equal))
                if r == 0:
                    link(V.scalar_tensor_tensor(lg, hot[:, 0], -3e38, lg, ALU.mult, ALU.add))
            V.tensor_tensor(mask, hot[:, 0], hot[:, 1], ALU.add).then_inc(mask_ready, 1)
            V.tensor_tensor(wts[:, 1, :], top[:, 1, :], top[:, 0, :], ALU.subtract).then_inc(wdiff_ready, 1)
            dve.wait_ge(wexp_ready, 1)
            link(V.tensor_scalar(wts[:, 0, :], wts[:, 1, :], 1.0, None, ALU.add))
            link(V.reciprocal(wts[:, 0, :], wts[:, 0, :]))
            link(V.tensor_tensor(wts[:, 1, :], wts[:, 1, :], wts[:, 0, :], ALU.mult))
            link(V.tensor_tensor(gat, hot[:, 0], wts[:, 0, :].unsqueeze(2).to_broadcast([P, LTB, NE]), ALU.mult))
            link(V.tensor_tensor(tie, hot[:, 1], wts[:, 1, :].unsqueeze(2).to_broadcast([P, LTB, NE]), ALU.mult))
            link(V.memset(gatecol[:, :, :], 0.0))
            link(V.memset(slotpos[:, :, :], -1.0))
            for r in range(2):
                link(V.tensor_tensor(gatecol[:, :, r * NE:(r + 1) * NE], gat, tie, ALU.add))
            dve.wait_ge(pos_mm, 1)
            link(V.scalar_tensor_tensor(posn, bank[1][:, 0:16].rearrange("p (b e) -> p b e", b=LTB), 1.0, mask, ALU.add, ALU.mult))
            for r in range(2):
                link(V.tensor_scalar(slotpos[:, :, r * NE:(r + 1) * NE], posn, -1.0 - P * r, None, ALU.add))
            link(V.tensor_reduce(mxc, bank[1][:, 16:24], AX.X, ALU.max))
            link(V.tensor_scalar(mxc, mxc, float(P), float(NE), ALU.is_gt, ALU.mult))
            link(V.tensor_scalar(nitems[0:1, 0:1], mxc[0:1, :], float(NE), None, ALU.add))
            dve.sem_inc(route_ready, 1)

            def build_pick(item):
                last = None
                for b in range(LTB):
                    last = V.tensor_scalar(pick[:, b, :], iota, slotpos[:, b, bass.ds(item, 1)], None, ALU.is_equal)
                last.then_inc(pick_ready, 1)

            def accumulate(r):
                last = None
                for j in range(4):
                    m = 4 * r + j
                    v = xT[:, m, CTX:TOK]
                    last = V.scalar_tensor_tensor(v, bank[6 + j // 2][:, (j % 2) * LAT:(j % 2 + 1) * LAT],
                                                  mod[:, 1, 40 + m, 1:2], v, ALU.mult, ALU.add)
                last.then_inc(xacc_ready, 1)

            def low(item, p, ahead=False):
                n = BASE + p
                dve.wait_ge(high_ready, item * EXP + (BASE + p + 1 + (EXP if ahead else 0)))
                V.tensor_tensor(wL[:, n % SPL, :], raw[:, n % RAW, :], f(wH[:, n % SPL, :]), ALU.subtract).then_inc(unit_ready, 1)

            def gathered_low(count):
                dve.wait_ge(hteh_ready, count + 1)
                for half in range(2):
                    ks = slice(4 * half, 4 * half + 4)
                    last = V.tensor_tensor(hTe[1][:, ks, :], bank[6 + half][:, :].rearrange("p (k t) -> p k t", k=4),
                                           f(hTe[0][:, ks, :]), ALU.subtract)
                last.then_inc(hte_ready, 1)

            def transposed_low(item, j):
                dve.wait_ge(actTh_ready, item * GU + j + 1)
                ks = slice(2 * j, 2 * j + 2)
                V.tensor_tensor(actT[1][:, ks, :], bank[2 + j % 2][:, 0:256].rearrange("p (i t) -> p i t", i=2),
                                f(actT[0][:, ks, :]), ALU.subtract).then_inc(actT_ready, 1)

            build_pick(0)
            V.memset(ysb[:, :], 0.0).then_inc(y_ready, 1)
            V.memset(spread[:, :], 0.0).then_inc(spread_ready, 1)
            dve.sem_inc(xacc_ready, 1)
            dve.sem_inc(act_tp, 2)
            dve.sem_inc(actT_ready, 2)
            gathered_low(0)
            n_items = dve.value_load(nitems[0:1, 0:1], min_val=NE, max_val=2 * NE)
            with dve.Fori(0, n_items) as item:
                dve.wait_ge(gather_mm, item + 1)
                build_pick(item + 1)
                for b in range(LTB):
                    last = V.tensor_scalar(wpick[:, b, :], iota, slotpos[:, b, bass.ds(item, 1)],
                                           gatecol[:, b, bass.ds(item, 1)], ALU.is_equal, ALU.mult)
                last.then_inc(wpick_ready, 1)
                for j in range(GU):
                    low(item, 2 * j + 2)
                    low(item, 2 * j + 3)
                    dve.wait_ge(sil_ready, item * GU + j + 1)
                    dve.wait_ge(act_tp, item * GU + j + (2 if j == 0 else 1))
                    V.tensor_tensor(act[:, j % 2, :], sil[:, j % 2, :], bank[j % 2][:, 256:512], ALU.mult).then_inc(act_ready, 1)
                    if j < 2:
                        dve.wait_ge(scatter_mm, 2 * item + j + 1)
                        dve.wait_ge(xacc_ready, 2 * item + j + 1)
                        accumulate(j)
                    if j >= 1:
                        transposed_low(item, j - 1)
                    if j == 3:
                        dve.wait_ge(spread_tp, item + 1)
                        V.tensor_copy(spread[:, :], bank[3][:, 256:512]).then_inc(spread_ready, 1)
                gathered_low(item + 1)
                transposed_low(item, GU - 1)
                for p in range(2 * GU + 2, EXP):
                    low(item, p)
                for p in range(2):
                    low(item, p, ahead=True)
            for r in range(2):
                dve.wait_ge(scatter_mm, 2 * n_items + r + 1)
                dve.wait_ge(xacc_ready, 2 * n_items + r + 1)
                accumulate(r)

            dve.wait_ge(froot_ready, 1)
            dve.wait_ge(xacc_ready, 2 * n_items + 3)
            link(V.reciprocal(rsf[:, :], rsf[:, :]))
            for k in range(KT):
                v = xT[:, k, CTX:TOK]
                V.scalar_tensor_tensor(v, v, vec[:, V_FIN + k:V_FIN + k + 1], rsf[:, :], ALU.mult, ALU.mult).then_inc(fin_ready, 1)


_INS = ["x", "c", "ctx", "c_ctx", "norm1_g", "norm2_g", "w_mod", "b_mod", "w_in", "b_gate", "mlstm_norm_g", "conv_dw",
        "conv_db", "conv_norm_g", "conv_norm_b", "w_out", "ffn_w_gate_up", "ffn_w_down", "moe_w_router",
        "moe_b_router", "moe_w_gate_up", "moe_w_down", "final_norm_g"]


def _constants(np):
    t = np.zeros((P, NCONST), np.float32)
    i = np.arange(P)
    t[:, C_ID:C_ID + P] = np.eye(P)
    t[:, C_ONE:C_ONE + P] = 1.0
    t[:, C_GRP:C_GRP + P] = (i[:, None] // 64 == i[None, :] // 64) / 64.0
    t[:, C_UT:C_UT + P] = i[:, None] < i[None, :]
    t[:, C_IOTA:C_IOTA + P] = i[None, :]
    t[:, C_MF:C_MF + P] = np.where(i[:, None] <= i[None, :], 0.0, NEG)
    t[:, C_MB:C_MB + P] = np.where(i[:, None] >= i[None, :], 0.0, NEG)
    n = np.arange(256)
    for b in range(2):
        ang = 2 * np.pi * ((i[:, None] + b * P) * n[None, :] % 256) / 256.0
        t[:, C_COS + b * 256:C_COS + (b + 1) * 256] = np.cos(ang)
        t[:, C_SIN + b * 256:C_SIN + (b + 1) * 256] = -np.sin(ang)
    same = i[:, None] // 64 == i[None, :] // 64
    ang = 2 * np.pi * ((i[:, None] % 64) * (i[None, :] % 64) % 64) / 64.0
    t[:, C_BD:C_BD + P] = np.where(same, np.cos(ang), 0.0) / 128.0
    t[:, C_BD + P:C_BD + 2 * P] = np.where(same, np.sin(ang), 0.0) / 128.0
    t[:, C_EPS] = EPS
    for g in range(2):
        for m in range(8):
            t[(2 * (m // MH) + g) * MH + m % MH, C_PERM + 8 * g + m] = 1.0
    for m in range(4):
        t[m, C_PAIR + m % 2] = 1.0
    return t


def kernel(**inputs):
    import numpy as _np
    import concourse.bacc as _bacc
    from concourse import mybir as _mybir
    from concourse.bass_utils import run_bass_kernel_spmd as _run

    nc = _bacc.Bacc("TRN2", target_bir_lowering=False, num_devices=1)
    arrays, args = {}, []
    for name in _INS:
        a = _np.ascontiguousarray(inputs[name])
        arrays[f"in_{name}_dram"] = a
        args.append(nc.dram_tensor(f"in_{name}_dram", a.shape, _mybir.dt.from_np(a.dtype), kind="ExternalInput").ap())
    table = _constants(_np)
    arrays["constants_dram"] = table
    args.append(nc.dram_tensor("constants_dram", table.shape, _mybir.dt.float32, kind="ExternalInput").ap())
    args.append(nc.dram_tensor("out_0_dram", (1, LAT, D), _mybir.dt.float32, kind="ExternalOutput").ap())
    build(nc, *args)
    r = _run(nc, [arrays], core_ids=[0])
    return r.results[0]["out_0_dram"]
```

```python
import concourse.bass as bass
from concourse import mybir
from contextlib import ExitStack

P = 128
D = 1024
KT = D // P
CTX = 256
LAT = 256
TOK = CTX + LAT
NTB = TOK // P
LTB = LAT // P
LAYERS = 2
MW = 512
MH = 4
CW = 256
TAPS = 31
HALF = TAPS // 2
PADW = CTX + 2 * HALF
HID = 2816
NHT = HID // P
NE = 8
EPS = 1e-6
PIN = 2832
NCOL = 512
UNITW = 2048
RAW = 6
SPL = 3
GU = HID // 256
DN = NHT // 2
EXP = 2 * GU + DN
TURN = -(-EXP // RAW) * RAW
MODC = 6 * D // NCOL
GROUPS = [(0, 4), (4, 16), (16, 24)]
ROWS = 4 * max(b - a for a, b in GROUPS)
CONDW = 2 * ROWS - 4
NEG = -1e30

C_ID, C_ONE, C_GRP, C_UT, C_IOTA, C_MF, C_MB = [P * i for i in range(7)]
C_EPS = 7 * P
C_PERM = C_EPS + 1
C_PAIR = C_PERM + 16
C_COS = C_PAIR + 2 * 12
C_SIN = C_COS + 2 * 256
C_BD = C_SIN + 2 * 256
NCONST = C_BD + 256

V_N1, V_N2, V_MG, V_DB, V_CG, V_CB, V_FIN, V_C, V_CC = 0, 16, 32, 40, 44, 48, 52, 60, 68
V_MOD = 76
V_DW = V_MOD + 96
NVEC = V_DW + LAYERS * TAPS * 2


def causal_cols(direction, sb, lat_only):
    if direction == 0:
        full = [((sb + 1) * P, TOK)] if sb < 3 else []
    else:
        full = {0: [(CTX, TOK)], 1: [(0, P), (CTX, TOK)], 2: [], 3: [(CTX, CTX + P)]}[sb]
    diag = sb
    if lat_only:
        full = [(max(a, CTX), b) for a, b in full if b > CTX]
        if sb < 2:
            diag = None
    spans = list(full)
    if diag is not None:
        spans.append((diag * P, diag * P + P))
    spans.sort()
    merged = []
    for a, b in spans:
        if merged and merged[-1][1] == a:
            merged[-1] = (merged[-1][0], b)
        else:
            merged.append((a, b))
    return diag, full, merged


def key_blocks(direction, tb):
    if direction == 0:
        return list(range(tb + 1))
    return {0: [0, 1], 1: [1], 2: [0, 1, 2, 3], 3: [0, 1, 3]}[tb]


def build(nc, x, c, ctx, c_ctx, norm1_g, norm2_g, w_mod, b_mod, w_in, b_gate, mlstm_norm_g, conv_dw, conv_db,
          conv_norm_g, conv_norm_b, w_out, ffn_w_gate_up, ffn_w_down, moe_w_router, moe_b_router,
          moe_w_gate_up, moe_w_down, final_norm_g, const_tab, out):
    f32 = mybir.dt.float32
    i32 = mybir.dt.int32
    ALU = mybir.AluOpType
    ACT = mybir.ActivationFunctionType
    AX = mybir.AxisListType

    es = ExitStack()
    with es:
        def sb(name, shape, dt=f32):
            return es.enter_context(nc.sbuf_tensor(name, shape, dt))

        def sem(name):
            return es.enter_context(nc.semaphore(name))

        def per_layer(name):
            return [sem(f"{name}_{layer}") for layer in range(LAYERS)]

        f32r = mybir.dt.float32r
        base = [nc.sbuf_base]

        def at_byte(name, offset, shape, dt=f32):
            return nc.alloc_sbuf_tensor_at(name, shape, dt, offset=offset)

        def put(name, shape, dt=f32):
            start = -(-base[0] // 32) * 32
            n = 4
            for d in shape[1:]:
                n *= d
            base[0] = start + n
            return at_byte(name, start, shape, dt)

        xT = put("xT", [P, KT, TOK])
        raw = put("raw", [P, RAW, UNITW])
        wH = put("wH", [P, SPL, UNITW], f32r)
        wL = put("wL", [P, SPL, UNITW], f32r)
        const = put("const", [P, NCONST])
        vec = put("vec", [P, NVEC])
        cond = put("cond", [P, KT, 2])
        mod = put("mod", [P, LAYERS, 48, 2])
        amp = put("amp", [P, LAYERS, 2, KT, 2])
        wr = put("wr", [P, KT, NE])
        rbias = put("rbias", [P, NE])
        gbias = put("gbias", [16, LAYERS])
        acol = put("acol", [P, 2, NTB, 8])
        floorc = put("floorc", [P, 2 * NTB, MH])
        dmax = put("dmax", [P, 8])
        rden = put("rden", [P, 8])
        ss16 = put("ss16", [P, 16])
        nitems = put("nitems", [1, 2], i32)
        scrap = put("scrap", [1, 1])
        hH = put("hH", [P, KT, TOK], f32r)
        hL = put("hL", [P, KT, TOK], f32r)
        area = -(-base[0] // 32) * 32
        h_at, l_at = base[0] - 8 * KT * TOK, base[0] - 4 * KT * TOK

        ident = const[:, C_ID:C_ID + P]
        ones = const[:, C_ONE:C_ONE + P]
        grp = const[:, C_GRP:C_GRP + P]
        before = const[:, C_UT:C_UT + P]
        iota = const[:, C_IOTA:C_IOTA + P]
        masks = [const[:, C_MF:C_MF + P], const[:, C_MB:C_MB + P]]
        cosn = const[:, C_COS:C_COS + 512].rearrange("p (b n) -> p b n", b=2)
        sinn = const[:, C_SIN:C_SIN + 512].rearrange("p (b n) -> p b n", b=2)
        dftc = const[:, C_BD:C_BD + 256]
        eps = const[:, C_EPS:C_EPS + 1]
        perm = [const[0:16, C_PERM + 8 * i:C_PERM + 8 * i + 8] for i in range(2)]
        pair = const[0:ROWS, C_PAIR:C_PAIR + ROWS // 2]

        def u(name, at, shape, dt=f32, region=area):
            return at_byte(name, region + 4 * at, shape, dt)

        xin = u("xin", 0, [P, NTB, D])
        rows = u("rows", 4096, [P, 3, P])
        sq = u("sq", 4096, [P, KT, TOK])
        rstd = u("rstd", 8192, [P, TOK])
        hpre = u("hpre", 8704, [P, 2, TOK])
        qT = u("qT", 0, [P, MH, TOK])
        kT = u("kT", 2048, [P, MH, TOK])
        vtok = u("vtok", 4096, [P, NTB, MH, P + 1])
        fT = u("fT", 6160, [P, 2, TOK])
        apad = u("apad", 7184, [P, 2, 2, PADW])
        Hs = u("Hs", 6160, [P, NTB, MW])
        acc = u("acc", 8328, [P, 2, 2, CTX])
        acc2 = acc.rearrange("p c s t -> p c (s t)")
        sigc = u("sigc", 8328, [P, 2, TOK])
        dm = u("dm", 8328, [P, NTB, P])
        modrow = u("modrow", 8840, [ROWS, NCOL])
        hsq = u("hsq", 8840, [P, NTB, P])
        condz = u("condz", 12424, [P, KT, CONDW], f32r)
        rowsg = [u(f"rowsg{r}", 9352 + 512 * r, [8, TOK]) for r in range(6)]
        gates16 = u("gates16", 9352 + 4 * 512, [16, TOK])
        sigo = u("sigo", 9352, [P, NTB, MW])
        prob = u("prob", 0, [P, 2, NTB, TOK], region=h_at)
        fab = u("fab", 0, [P, NTB, 2, 256], region=h_at)
        csq = u("csq", 7184, [P, 2, TOK])
        hsq_last = u("hsq_last", 0, [P, NTB, P], region=h_at)
        y1 = [u(f"y1{x}", 2048 * i, [P, MH, TOK], f32r) for i, x in enumerate("HL")]
        y2 = [u(f"y2{x}", 2048 * i, [P, MH, TOK], f32r, region=l_at) for i, x in enumerate("HL")]
        act0 = u("act0", 0, [P, NHT, TOK])
        sil0 = u("sil0", NHT * TOK, [P, 2, TOK])
        a0 = [u(f"a0{x}", 0, [P, 4, TOK], f32r, region=r) for x, r in (("H", h_at), ("L", l_at))]
        hlat = u("hlat", 0, [P, KT, LAT], region=l_at)
        hxtok = u("hxtok", 0, [P, LTB, D])
        hTe = [u(f"hTe{x}", 2048 + 1024 * i, [P, KT, P], f32r) for i, x in enumerate("HL")]
        sil = u("sil", 4096, [P, 2, 256])
        act = u("act", 4608, [P, 2, 256])
        ysb = u("ysb", 5120, [P, D])
        pick = u("pick", 6144, [P, LTB, P])
        wpick = u("wpick", 6400, [P, LTB, P])
        spread = u("spread", 6656, [P, LAT])
        slotpos = u("slotpos", 6912, [P, LTB, 24])
        gatecol = u("gatecol", 6960, [P, LTB, 24])
        rt = u("rt", 7008, [P, 160])
        actT = [u(f"actT{x}", 7168 + 2816 * i, [P, NHT, P], f32r) for i, x in enumerate("HL")]
        outsb = u("outsb", 0, [P, LTB, D], region=h_at)
        sqf = u("sqf", 0, [P, KT, LAT], region=l_at)
        rsf = u("rsf", 2048, [P, LAT], region=l_at)

        def f(ap):
            return ap.bitcast(f32)

        bank = [es.enter_context(nc.psum_tensor(f"bank{i}", [P, NCOL], f32)) for i in range(8)]

        const_in = sem("const_in")
        rows_in = sem("rows_in")
        x_in = sem("x_in")
        small_in = sem("small_in")
        raw_in = [sem(f"raw_in{r}") for r in range(RAW)]
        high_ready = sem("high_ready")
        unit_ready = sem("unit_ready")
        dve_step = sem("dve_step")
        vec_tp = sem("vec_tp")
        vec_ready = sem("vec_ready")
        cond_ready = sem("cond_ready")
        xt_tp = sem("xt_tp")
        xt_ready = sem("xt_ready")
        mod_mm = sem("mod_mm")
        mod_row = sem("mod_row")
        mod_tp = sem("mod_tp")
        mod_col = sem("mod_col")
        mod_half = sem("mod_half")
        condh_ready = sem("condh_ready")
        condz_ready = sem("condz_ready")
        amp_ready = [[sem(f"amp_ready_{a}{b}") for b in range(2)] for a in range(LAYERS)]
        sq_ready = [[sem(f"sq_ready_{a}{b}") for b in range(2)] for a in range(LAYERS)]
        ssq_done = sem("ssq_done")
        root_ready = sem("root_ready")
        xr_ready = [[sem(f"xr_ready_{a}{b}") for b in range(2)] for a in range(LAYERS)]
        hh_ready = [[sem(f"hh_ready_{a}{b}") for b in range(2)] for a in range(LAYERS)]
        h_ready = [[sem(f"h_ready_{a}{b}") for b in range(2)] for a in range(LAYERS)]
        proj_mm = per_layer("proj_mm")
        proj_ready = per_layer("proj_ready")
        nabs_ready = per_layer("nabs_ready")
        ln_ready = sem("ln_ready")
        gate_rows = sem("gate_rows")
        gate_tp = sem("gate_tp")
        gate_cols = per_layer("gate_cols")
        fab_mm = per_layer("fab_mm")
        fab_ready = per_layer("fab_ready")
        fy_mm = per_layer("fy_mm")
        fyh_ready = per_layer("fyh_ready")
        csil_ready = per_layer("csil_ready")
        yh_ready = per_layer("yh_ready")
        score_mm = per_layer("score_mm")
        mbc_mm = per_layer("mbc_mm")
        dm_ready = per_layer("dm_ready")
        e_ready = per_layer("e_ready")
        p_ready = per_layer("p_ready")
        out_mm = per_layer("out_mm")
        hs_ready = per_layer("hs_ready")
        hsq_ready = sem("hsq_ready")
        ss_ready = sem("ss_ready")
        hroot_ready = sem("hroot_ready")
        ytok_ready = sem("ytok_ready")
        yt_tp = per_layer("yt_tp")
        pad_ready = sem("pad_ready")
        conv_ready = sem("conv_ready")
        cmean_mm = per_layer("cmean_mm")
        cdev_ready = per_layer("cdev_ready")
        csq_ready = per_layer("csq_ready")
        cvar_mm = per_layer("cvar_mm")
        croot_ready = per_layer("croot_ready")
        cnorm_ready = per_layer("cnorm_ready")
        ycat_ready = per_layer("ycat_ready")
        wout_mm = per_layer("wout_mm")
        xo_ready = per_layer("xo_ready")
        gu0_half = sem("gu0_half")
        gu0_mm = sem("gu0_mm")
        a0h_ready = sem("a0h_ready")
        a0_ready = sem("a0_ready")
        sil0_ready = sem("sil0_ready")
        act0_ready = sem("act0_ready")
        down0_mm = sem("down0_mm")
        x2_ready = sem("x2_ready")
        logit_mm = sem("logit_mm")
        hxtok_tp = sem("hxtok_tp")
        hxtok_ready = sem("hxtok_ready")
        mask_ready = sem("mask_ready")
        wdiff_ready = sem("wdiff_ready")
        wexp_ready = sem("wexp_ready")
        pos_mm = sem("pos_mm")
        route_ready = sem("route_ready")
        pick_ready = sem("pick_ready")
        gather_mm = sem("gather_mm")
        hteh_ready = sem("hteh_ready")
        hte_ready = sem("hte_ready")
        gu_mm = sem("gu_mm")
        sil_ready = sem("sil_ready")
        act_ready = sem("act_ready")
        act_tp = sem("act_tp")
        actTh_ready = sem("actTh_ready")
        actT_ready = sem("actT_ready")
        wpick_ready = sem("wpick_ready")
        spread_tp = sem("spread_tp")
        spread_ready = sem("spread_ready")
        down_mm = sem("down_mm")
        y_ready = sem("y_ready")
        scatter_mm = sem("scatter_mm")
        xacc_ready = sem("xacc_ready")
        fsq_ready = sem("fsq_ready")
        fssq_mm = sem("fssq_mm")
        froot_ready = sem("froot_ready")
        fin_ready = sem("fin_ready")
        fin_tp = sem("fin_tp")
        out_ready = sem("out_ready")
        out_stored = sem("out_stored")

        def ksplit(w):
            return w.rearrange("(k p) n -> p k n", p=P)

        def expert_unit(gate_up, down, p):
            if p < 2 * GU:
                j, half = divmod(p, 2)
                v = ksplit(gate_up)[:, 4 * half:4 * half + 4, :]
                return [(0, v[:, :, j * 256:j * 256 + 256]), (256, v[:, :, HID + j * 256:HID + j * 256 + 256])]
            i = p - 2 * GU
            return [(0, ksplit(down)[:, 2 * i:2 * i + 2, :])]

        def view(t, slot, name, p=0):
            k = 4 if name == "mod" or (name == "mlp" and p < 2 * GU) else 2 if name == "mlp" else KT
            return t[:, slot, :].rearrange("p (k c) -> p k c", k=k)

        stream = []

        def mod_stream(group):
            for g in range(*GROUPS[group]):
                layer, n = divmod(g, MODC)
                for half in range(2):
                    v = ksplit(w_mod[layer])[:, 4 * half:4 * half + 4, n * NCOL:(n + 1) * NCOL]
                    stream.append(("mod", layer, 2 * n + half, [(0, v)]))

        O_G = 4 * MW
        O_F = O_G + 16
        IN_UNITS = [("g", 0, O_G, P), ("f", 0, O_F, 256), ("cu", 0, O_F + 256, 256), ("cg", 0, O_F + 512, 256)]
        IN_UNITS += [(name, i, at + 256 * i, 256) for name, at in (("q", 0), ("k", MW), ("v", 2 * MW), ("o", 3 * MW))
                     for i in range(2)]
        mod_stream(0)
        for layer in range(LAYERS):
            for name, i, at, w in IN_UNITS:
                stream.append((name, layer, i, [(0, ksplit(w_in[layer])[:, :, at:at + w])]))
            mod_stream(layer + 1)
            for n in range(4):
                stream.append(("wout", layer, n, [(0, ksplit(w_out[layer])[:, :, n * 256:(n + 1) * 256])]))
            if layer == 0:
                for p in range(EXP):
                    stream.append(("mlp", 0, p, expert_unit(ffn_w_gate_up[0], ffn_w_down[0], p)))
        place = {(name, layer, i): n for n, (name, layer, i, _) in enumerate(stream)}
        BASE = len(stream)

        def load(eng, n, name, p, pieces):
            for off, src in pieces:
                dst = view(raw, n % RAW, name, p)[:, :, off:off + src.shape[2]]
                eng.dma_start(dst, src).then_inc(raw_in[n % RAW], 32 // len(pieces))

        def unit_cols(t, slot, name):
            return view(t, slot, name)[:, :, 0:P] if name == "g" else t[:, slot, :]

        def halves(eng, name, layer, i):
            n = place[name, layer, i]
            eng.wait_ge(unit_ready, n + 1)
            return [view(t, n % SPL, name, i) for t in (wH, wL)]

        def proj_outputs(layer):
            tbs = range(NTB) if layer == 0 else range(LTB, NTB)
            units = [("g", 0), ("f", 0), ("f", 1), ("gi", 0), ("gf", 0), ("cu", 0), ("cu", 1), ("cg", 0), ("cg", 1)]
            units += [("q", h) for h in range(MH)] + [("k", h) for h in range(MH)]
            units += [("v", (half, b)) for half in range(2) for b in range(NTB)]
            units += [("o", (half, b)) for half in range(2) for b in tbs]
            return units

        outputs_of = [proj_outputs(layer) for layer in range(LAYERS)]

        def unit_of(kind, i):
            if kind in ("gi", "gf"):
                return None
            return (kind, i[0]) if kind in ("v", "o") else (kind, i // 2) if kind in ("q", "k") else (kind, 0)

        def output_count(layer, kind, i):
            return outputs_of[layer].index((kind, i)) + 1

        def mod_place(g, half):
            return place["mod", g // MODC, 2 * (g % MODC) + half]

        mod_bank = bank[4]
        CHUNK0 = GROUPS[1][0]

        def head_unit(layer, t, which):
            return GROUPS[layer + 1][1] - 2 * MH + t, which

        def consumed(n):
            name, layer, i, _ = stream[n]
            if name == "mod":
                g = layer * MODC + i // 2
                return (mod_mm if i % 2 else mod_half), g + 1
            if name == "wout":
                return wout_mm[layer], 2 * (i + 1)
            if name == "mlp" and i < 2 * GU:
                return (gu0_mm, 4 * (i // 2 + 1)) if i % 2 else (gu0_half, i // 2 + 1)
            if name == "mlp":
                n = i - 2 * GU
                return down0_mm, 2 * (n + 1) if n < DN - 1 else NHT - 2 + KT
            return proj_mm[layer], max(m + 1 for m, (kind, j) in enumerate(outputs_of[layer]) if unit_of(kind, j) == (name, i))

        def cols(layer, both):
            return (0, TOK) if layer == 0 or both else (CTX, TOK)

        def sum_bank(layer, i):
            return bank[7] if layer == 0 and i == 0 else bank[0]

        def proj_bank(n):
            return bank[2] if n == 2 else bank[n % 2]

        def head_bank(h):
            return bank[4 + h]

        def fab_bank(layer, s, ct):
            return bank[(5 if layer == 0 and s == 1 else 2) + ct]

        def last_bank(q):
            return bank[(6 + q) % 8]

        def streams_of(layer, both=False):
            return (0, 1) if layer == 0 or both else (1,)

        block = es.enter_context(nc.Block())

        @block.sync
        def _(sp):
            sp.dma_start(const[:, 0:C_COS], const_tab[:, 0:C_COS]).then_inc(const_in, 16)
            r0, r1, r2 = rows[:, 0, :], rows[:, 1, :], rows[:, 2, :]
            flat = [(V_N1, norm1_g.rearrange("l (k p) -> (l k) p", p=P)), (V_N2, norm2_g.rearrange("l (k p) -> (l k) p", p=P)),
                    (V_MG, mlstm_norm_g.rearrange("l (k p) -> (l k) p", p=P)), (V_DB, conv_db.rearrange("l (k p) -> (l k) p", p=P)),
                    (V_CG, conv_norm_g.rearrange("l (k p) -> (l k) p", p=P)), (V_CB, conv_norm_b.rearrange("l (k p) -> (l k) p", p=P)),
                    (V_FIN, final_norm_g.rearrange("(k p) -> k p", p=P)), (V_C, c[0].rearrange("(k p) -> k p", p=P)),
                    (V_CC, c_ctx.rearrange("(k p) -> k p", p=P))]
            for at, src in flat:
                sp.dma_start(r0[at:at + src.shape[0], :], src).then_inc(rows_in, 16)
            sp.dma_start(r1[0:96, :], b_mod.rearrange("l (k p) -> (l k) p", p=P)).then_inc(rows_in, 16)
            sp.dma_start(r2[0:124, :], conv_dw.rearrange("l t (k p) -> (l t k) p", p=P)).then_inc(rows_in, 16)
            sp.dma_start(xin[:, 0:2, :], ctx[0].rearrange("(b p) d -> p b d", p=P)).then_inc(x_in, 16)
            sp.dma_start(xin[:, 2:4, :], x[0].rearrange("(b p) d -> p b d", p=P)).then_inc(x_in, 16)
            for n in range(RAW):
                load(sp, n, stream[n][0], stream[n][2], stream[n][3])
            sp.dma_start(const[:, C_COS:NCONST], const_tab[:, C_COS:NCONST]).then_inc(const_in, 16)
            with nc.allow_non_contiguous_dma(reason="a few small vectors"):
                sp.dma_start(gbias[:, :], b_gate.rearrange("l r -> r l")).then_inc(small_in, 16)
                sp.dma_start(wr[:, :, :], moe_w_router[0].rearrange("(k p) e -> p k e", p=P)).then_inc(small_in, 16)
                sp.dma_start(rbias[:, :], moe_b_router.to_broadcast([P, NE])).then_inc(small_in, 16)
            for n in range(RAW, BASE):
                sp.wait_ge(unit_ready, n - RAW + 1)
                load(sp, n, stream[n][0], stream[n][2], stream[n][3])

            def expert(item, e, first, count=EXP):
                for p in range(count):
                    if p >= RAW:
                        sp.wait_ge(unit_ready, item * EXP + (BASE + p - RAW + 1))
                    elif first:
                        sp.wait_ge(unit_ready, BASE + p - RAW + 1)
                    else:
                        back = TURN - RAW if p + TURN - RAW < EXP else TURN - 2 * RAW
                        sp.wait_ge(unit_ready, item * EXP + (BASE + p + back - EXP + 1))
                    load(sp, BASE + p, "mlp", p, expert_unit(moe_w_gate_up[0, e], moe_w_down[0, e], p))

            expert(0, 0, True)
            sp.wait_ge(route_ready, 1)
            n_items = sp.value_load(nitems[0:1, 0:1], min_val=NE, max_val=2 * NE)
            with sp.Fori(1, n_items) as item:
                expert(item, item % NE, False)
            expert(n_items, 0, False, 2)
            for b in range(LTB):
                sp.wait_ge(out_ready, 2 * (b + 1))
                sp.dma_start(out[0, b * P:(b + 1) * P, :], outsb[:, b, :]).then_inc(out_stored, 16)
            sp.wait_ge(out_stored, 16 * LTB)

        @block.tensor
        def _(pe):
            mm = nc.tensor.matmul
            tp = nc.tensor.transpose

            def exact(o, stationary, moving, start, stop):
                mm(o, stationary[0], moving[0], start=start, stop=False)
                mm(o, stationary[0], moving[1], start=False, stop=False)
                return mm(o, stationary[1], moving[0], start=False, stop=stop)

            def mod_transposes(group):
                n = GROUPS[group][1] - GROUPS[group][0]
                pe.wait_ge(mod_row, group + 1)
                for j in range(4):
                    last = mm(mod_bank[:, j * 2 * n:(j + 1) * 2 * n], modrow[0:4 * n, j * P:(j + 1) * P],
                              pair[0:4 * n, 0:2 * n], start=True, stop=True)
                last.then_inc(mod_tp, 1)

            def mod_half_chunk(g, half):
                group = next(i for i, (a, b) in enumerate(GROUPS) if a <= g < b)
                first, end = GROUPS[group]
                if g == first and half == 0 and group:
                    pe.wait_ge(mod_col, group)
                w = halves(pe, "mod", g // MODC, 2 * (g % MODC) + half)
                at = ROWS - 4 - 4 * (g - first)
                for j in range(4):
                    k = 4 * half + j
                    for m in range(2):
                        last = mm(mod_bank[0:ROWS, :], condz[:, k, at:at + ROWS], w[m][:, j, :],
                                  start=g == first and k == 0 and m == 0, stop=g == end - 1 and k == KT - 1 and m == 1)
                last.then_inc(mod_mm if half else mod_half, 1)

            def mod_chunk(layer, g):
                if layer == 0:
                    mod_half_chunk(g, 0)
                    mod_half_chunk(g, 1)

            def norm_sum(layer, i, tiles):
                lo, hi = cols(layer, i == 0)
                for k in tiles:
                    pe.wait_ge(sq_ready[layer][i], k + 1)
                    last = mm(sum_bank(layer, i)[:, lo:hi], ones, sq[:, k, lo:hi], start=k == 0, stop=k == KT - 1)
                    if k == KT - 1:
                        last.then_inc(ssq_done, 1)

            def projections(layer):
                def share(n, w, k):
                    kind, i = outputs_of[layer][n]
                    if kind in ("v", "o"):
                        tok = slice(i[1] * P, (i[1] + 1) * P)
                        return exact(proj_bank(n)[:, 0:256], [t[:, k, tok] for t in (hH, hL)], [t[:, k, :] for t in w],
                                     k == 0, k == KT - 1)
                    lo, hi = cols(layer, kind in ("g", "k"))
                    j = (i % 2) * P
                    return exact(proj_bank(n)[:, lo:hi], [t[:, k, j:j + P] for t in w], [t[:, k, lo:hi] for t in (hH, hL)],
                                 k == 0, k == KT - 1)

                w = [halves(pe, unit_of(kind, i)[0], layer, unit_of(kind, i)[1]) for kind, i in outputs_of[layer][:3]]
                for k in range(KT):
                    pe.wait_ge(h_ready[layer][0], k + 1)
                    for n in range(3):
                        last = share(n, w[n], k)
                        if k == KT - 1:
                            last.then_inc(proj_mm[layer], 1)
                first_o = output_count(layer, *next(v for v in outputs_of[layer] if v[0] == "o")) - 1
                for n in range(3, len(outputs_of[layer])):
                    kind, i = outputs_of[layer][n]
                    if n == first_o:
                        conv_mean(layer)
                    if n == first_o + 2:
                        conv_variance(layer)
                    pe.wait_ge(proj_ready[layer], n - 1)
                    if kind in ("gi", "gf"):
                        pe.wait_ge(proj_ready[layer], output_count(layer, "g", 0))
                        last = mm(proj_bank(n)[0:8, :], perm[0 if kind == "gi" else 1], gates16[:, :], start=True, stop=True)
                        last.then_inc(proj_mm[layer], 1)
                        continue
                    w = halves(pe, unit_of(kind, i)[0], layer, unit_of(kind, i)[1])
                    for k in range(KT):
                        last = share(n, w, k)
                    last.then_inc(proj_mm[layer], 1)
                    if (kind, i) == ("k", MH - 1):
                        gate_transposes(layer)

            def gate_transposes(layer):
                pe.wait_ge(gate_rows, layer + 1)
                for d in range(2):
                    for b in range(NTB):
                        at = (d * NTB + b) * 8
                        tp(bank[7][:, at:at + 8], rowsg[d][:, b * P:(b + 1) * P], ident[0:8, 0:8])
                        last = tp(bank[7][:, 64 + at:72 + at], rowsg[2 + d][:, b * P:(b + 1) * P], ident[0:8, 0:8])
                last.then_inc(gate_tp, 1)

            def fourier_channels(layer):
                pe.wait_ge(const_in, 32)
                for s in streams_of(layer):
                    if layer == 0 and s == 1:
                        pe.wait_ge(croot_ready[layer], 2)
                    for ct in range(2):
                        b = fab_bank(layer, s, ct)
                        for j in range(2):
                            tb = 2 * s + j
                            last = mm(b[:, j * 256:(j + 1) * 256], fT[:, ct, tb * P:(tb + 1) * P], dftc, start=True, stop=True)
                        last.then_inc(fab_mm[layer], 1)

            def fourier_positions(layer):
                pe.wait_ge(fab_ready[layer], 2 * len(streams_of(layer)))
                for ct in range(2):
                    for s in streams_of(layer):
                        for j in range(2):
                            tb = 2 * s + j
                            o = bank[2 + ct][:, s * 256:(s + 1) * 256]
                            mm(o, fab[:, tb, ct, 0:P], cosn[:, j, :], start=j == 0, stop=False)
                            last = mm(o, fab[:, tb, ct, P:2 * P], sinn[:, j, :], start=False, stop=j == 1)
                    last.then_inc(fy_mm[layer], 1)

            def heads(layer):
                lo, hi = cols(layer, False)
                tbs = range(NTB) if layer == 0 else range(LTB, NTB)

                def scores(h):
                    for s in range(NTB):
                        a, z = (lo, hi) if s < 2 else (CTX, TOK)
                        o = bank[s][:, a:z] if s < 2 else bank[2][:, (s - 2) * LAT:(s - 1) * LAT]
                        last = mm(o, kT[:, h, s * P:(s + 1) * P], qT[:, h, a:z], start=True, stop=True)
                    last.then_inc(score_mm[layer], 1)

                def running_max(t):
                    h, d = divmod(t, 2)
                    mm(bank[3][:, lo:hi], ident[0:8, d * MH + h:d * MH + h + 1].to_broadcast([8, P]),
                       rowsg[4 + d][:, lo:hi], start=True, stop=True).then_inc(mbc_mm[layer], 1)

                def read_values(t):
                    h, d = divmod(t, 2)
                    for tb in tbs:
                        idx = d * NTB + tb
                        b = bank[5 + idx // 3]
                        o = b[:, (idx % 3) * 129:(idx % 3) * 129 + 129]
                        keys = key_blocks(d, tb)
                        for n, s in enumerate(keys):
                            last = mm(o, prob[:, d, s, tb * P:(tb + 1) * P], vtok[:, s, h, :],
                                      start=n == 0, stop=n == len(keys) - 1)
                    last.then_inc(out_mm[layer], 1)

                pe.wait_ge(gate_cols[layer], 2)
                pe.wait_ge(ycat_ready[layer], 4)
                pe.wait_ge(proj_ready[layer], len(outputs_of[layer]))
                scores(0)
                running_max(0)
                mod_chunk(layer, CHUNK0 + 2)
                mod_chunk(layer, CHUNK0 + 3)
                for t in range(2 * MH):
                    if t < 2 * MH - 1:
                        pe.wait_ge(e_ready[layer], t + 1)
                        running_max(t + 1)
                    mod_half_chunk(*head_unit(layer, t, 0))
                    pe.wait_ge(p_ready[layer], t + 1)
                    if t % 2 and t < 2 * MH - 1:
                        scores(t // 2 + 1)
                    mod_half_chunk(*head_unit(layer, t, 1))
                    if t % 2 == 0 and t:
                        pe.wait_ge(hs_ready[layer], t // 2)
                    read_values(t)

            def conv_mean(layer):
                lo, hi = cols(layer, False)
                pe.wait_ge(conv_ready, layer + 1)
                for ct in range(2):
                    last = mm(bank[5 + ct][:, lo:hi], grp, acc2[:, ct, lo:hi], start=True, stop=True)
                    last.then_inc(cmean_mm[layer], 1)

            def conv_variance(layer):
                lo, hi = cols(layer, False)
                for ct in range(2):
                    pe.wait_ge(csq_ready[layer], ct + 1)
                    last = mm(bank[5 + ct][:, lo:hi], grp, csq[:, ct, lo:hi], start=True, stop=True)
                    last.then_inc(cvar_mm[layer], 1)

            def out_projection(layer):
                lo, hi = cols(layer, False)
                tbs = range(NTB) if layer == 0 else range(LTB, NTB)

                def share(m, k, start, stop):
                    w = halves(pe, "wout", layer, m // 2)
                    y = [t[:, k % 4, lo:hi] for t in (y1 if k < 4 else y2)]
                    return exact(bank[m][:, lo:hi], [t[:, k, (m % 2) * P:(m % 2 + 1) * P] for t in w], y, start, stop)

                pe.wait_ge(ycat_ready[layer], 4)
                pe.wait_ge(p_ready[layer], 2 * MH)
                pe.wait_ge(e_ready[layer], 2 * MH)
                for m in range(4):
                    for k in range(4, KT):
                        share(m, k, k == 4, False)
                    if m == 1:
                        mod_transposes(layer + 1)
                pe.wait_ge(hs_ready[layer], MH)
                pe.wait_ge(mod_col, layer + 2)
                for h in range(MH):
                    pe.wait_ge(ytok_ready, MH * layer + h + 1)
                    for tb in tbs:
                        last = tp(head_bank(h)[:, tb * P:(tb + 1) * P], Hs[:, tb, h * P:(h + 1) * P], ident)
                    last.then_inc(yt_tp[layer], 1)
                for h in range(MH):
                    pe.wait_ge(ycat_ready[layer], 4 + h + 1)
                    for m in range(4):
                        last = share(m, h, False, h == MH - 1)
                        if h == MH - 1:
                            last.then_inc(wout_mm[layer], 1)
                for m in range(4, KT):
                    for n, k in enumerate([4, 5, 6, 7, 0, 1, 2, 3]):
                        last = share(m, k, n == 0, n == KT - 1)
                    last.then_inc(wout_mm[layer], 1)
                    if m == KT - 2:
                        norm_sum(layer, 1, range(KT - 2))
                norm_sum(layer, 1, [KT - 2, KT - 1])

            def dense_mixer():
                for j in range(GU):
                    if j >= 2:
                        pe.wait_ge(act0_ready, 2 * (j - 1))
                    for half in range(2):
                        w = halves(pe, "mlp", 0, 2 * j + half)
                        order = [(t, i) for t in range(4) for i in range(4)]
                        if j == 0:
                            order = [(t, i) for i in range(4) for t in range(4)]
                        for t, i in order:
                            off = (t % 2) * 256 + (t // 2) * P
                            k = 4 * half + i
                            if j == 0 and t == 0:
                                pe.wait_ge(h_ready[0][1], k + 1)
                            last = exact(bank[4 * (j % 2) + t][:, :], [v[:, i, off:off + P] for v in w],
                                         [v[:, k, :] for v in (hH, hL)], k == 0, k == KT - 1)
                            if half and i == 3:
                                last.then_inc(gu0_mm, 1)
                        if not half:
                            last.then_inc(gu0_half, 1)
                for n in range(DN - 1):
                    w = halves(pe, "mlp", 0, 2 * GU + n)
                    for j in range(2):
                        i = 2 * n + j
                        pe.wait_ge(a0_ready, i + 1)
                        for m in range(KT):
                            last = exact(bank[m][:, :], [v[:, j, m * P:(m + 1) * P] for v in w],
                                         [v[:, i % 4, :] for v in a0], i == 0, False)
                        last.then_inc(down0_mm, 1)
                w = halves(pe, "mlp", 0, 2 * GU + DN - 1)
                pe.wait_ge(a0_ready, NHT)
                for m in range(KT):
                    for i in range(NHT - 2, NHT):
                        last = exact(bank[m][:, :], [t[:, i % 2, m * P:(m + 1) * P] for t in w],
                                     [t[:, i % 4, :] for t in a0], False, i == NHT - 1)
                    last.then_inc(down0_mm, 1)
                    if m == KT - 2:
                        norm_sum(1, 0, range(KT - 3))
                norm_sum(1, 0, range(KT - 3, KT))

            pe.wait_ge(const_in, 16)
            pe.wait_ge(rows_in, 16 * 11)
            for r, (at, n) in enumerate(((0, 76), (V_MOD, 96), (V_DW, 124))):
                last = tp(bank[0][:, at:at + n], rows[0:n, r, :], ident[0:n, 0:n])
            last.then_inc(vec_tp, 1)
            for n in range(KT):
                if n == 0:
                    pe.wait_ge(x_in, 32)
                if n >= 2:
                    pe.wait_ge(xt_ready, n - 1)
                for b in range(NTB):
                    last = tp(bank[5 + n % 2][:, b * P:(b + 1) * P], xin[:, b, n * P:(n + 1) * P], ident)
                last.then_inc(xt_tp, 1)
            norm_sum(0, 0, range(KT))
            pe.wait_ge(condz_ready, 1)
            for g in range(*GROUPS[0]):
                mod_half_chunk(g, 0)
                mod_half_chunk(g, 1)
            mod_transposes(0)

            for layer in range(LAYERS):
                projections(layer)
                fourier_channels(layer)
                mod_chunk(layer, CHUNK0)
                fourier_positions(layer)
                mod_chunk(layer, CHUNK0 + 1)
                heads(layer)
                out_projection(layer)
                if layer == 0:
                    dense_mixer()

            pe.wait_ge(small_in, 16 * 3)
            for k in range(KT):
                pe.wait_ge(hh_ready[1][1], k + 1)
                for b in range(LTB):
                    last = mm(bank[b][:, 0:NE], hlat[:, k, b * P:(b + 1) * P], wr[:, k, :], start=k == 0, stop=k == KT - 1)
            last.then_inc(logit_mm, 1)
            for b in range(LTB):
                for half in range(2):
                    for j in range(4):
                        k = 4 * half + j
                        last = tp(bank[2 + 2 * b + half][:, j * P:(j + 1) * P], hlat[:, k, b * P:(b + 1) * P], ident)
                    last.then_inc(hxtok_tp, 1)
            pe.wait_ge(mask_ready, 1)
            mask = rt[:, 0:16].rearrange("p (b e) -> p b e", b=LTB)
            mm(bank[1][:, 0:8], before, mask[:, 0, :], start=True, stop=True)
            mm(bank[1][:, 8:16], ones, mask[:, 0, :], start=True, stop=False)
            mm(bank[1][:, 8:16], before, mask[:, 1, :], start=False, stop=True)
            mm(bank[1][:, 16:24], ones, mask[:, 0, :], start=True, stop=False)
            mm(bank[1][:, 16:24], ones, mask[:, 1, :], start=False, stop=True).then_inc(pos_mm, 1)

            def gather():
                for k in range(KT):
                    for b in range(LTB):
                        last = mm(bank[6 + k // 4][:, (k % 4) * P:(k % 4 + 1) * P], hxtok[:, b, k * P:(k + 1) * P],
                                  pick[:, b, :], start=b == 0, stop=b == LTB - 1)
                last.then_inc(gather_mm, 1)

            def scatter(r):
                for j in range(4):
                    m = 4 * r + j
                    last = mm(bank[6 + j // 2][:, (j % 2) * LAT:(j % 2 + 1) * LAT], ysb[:, m * P:(m + 1) * P], spread[:, :],
                              start=True, stop=True)
                last.then_inc(scatter_mm, 1)

            def transposes(item, j):
                cnt = GU * item + j
                pe.wait_ge(act_ready, cnt + 3)
                pe.wait_ge(actT_ready, cnt + (2 if j == 0 else 1))
                for i in range(2):
                    last = tp(bank[2 + j % 2][:, i * P:(i + 1) * P], act[:, j % 2, i * P:(i + 1) * P], ident)
                last.then_inc(act_tp, 1)

            def expert_halves(item, p):
                pe.wait_ge(unit_ready, item * EXP + (BASE + p + 1))
                return [view(t, (BASE + p) % SPL, "mlp", p) for t in (wH, wL)]

            pe.wait_ge(hxtok_ready, 4)
            pe.wait_ge(pick_ready, 1)
            gather()
            pe.sem_inc(down_mm, 1)
            pe.wait_ge(route_ready, 1)
            n_items = pe.value_load(nitems[0:1, 0:1], min_val=NE, max_val=2 * NE)
            with pe.Fori(0, n_items) as item:
                pe.wait_ge(hte_ready, item + 1)
                for j in range(GU):
                    pe.wait_ge(act_ready, item * GU + j + (2 if j == 0 else 1))
                    for half in range(2):
                        w = expert_halves(item, 2 * j + half)
                        for i in range(4):
                            k = 4 * half + i
                            last = exact(bank[j % 2][:, :], [t[:, k, :] for t in hTe], [t[:, i, :] for t in w],
                                         k == 0, k == KT - 1)
                        last.then_inc(gu_mm, 1)
                    if j < 2:
                        if j == 0:
                            pe.wait_ge(y_ready, item + 1)
                            pe.wait_ge(spread_ready, item + 1)
                        pe.wait_ge(xacc_ready, 2 * item + j + 1)
                        scatter(j)
                    if j == 4:
                        pe.wait_ge(spread_ready, item + 2)
                    if j >= 1:
                        transposes(item, j - 1)
                    if j == 3:
                        pe.wait_ge(wpick_ready, item + 1)
                        pe.wait_ge(actT_ready, item * GU + 4)
                        for b in range(LTB):
                            last = tp(bank[3][:, 256 + b * P:256 + (b + 1) * P], wpick[:, b, :], ident)
                        last.then_inc(spread_tp, 1)
                pe.wait_ge(pick_ready, item + 2)
                pe.wait_ge(xacc_ready, 2 * item + 3)
                gather()
                transposes(item, GU - 1)
                for n in range(DN):
                    w = expert_halves(item, 2 * GU + n)
                    pe.wait_ge(actT_ready, item * GU + n + 3)
                    for j in range(2):
                        i = 2 * n + j
                        for half in range(2):
                            last = exact(bank[4 + half][:, :], [t[:, i, :] for t in actT],
                                         [t[:, j, half * NCOL:(half + 1) * NCOL] for t in w], i == 0, i == NHT - 1)
                    last.then_inc(down_mm, 1)
            pe.wait_ge(y_ready, n_items + 1)
            pe.wait_ge(spread_ready, n_items + 1)
            pe.wait_ge(xacc_ready, 2 * n_items + 1)
            pe.wait_ge(hte_ready, n_items + 1)
            for q in range(4):
                for j in range(2):
                    m = 2 * q + j
                    last = mm(last_bank(q)[:, j * LAT:(j + 1) * LAT], ysb[:, m * P:(m + 1) * P], spread[:, :],
                              start=True, stop=True)
                last.then_inc(scatter_mm, 1)

            for k in range(KT):
                pe.wait_ge(fsq_ready, k + 1)
                last = mm(bank[4][:, 0:LAT], ones, sqf[:, k, :], start=k == 0, stop=k == KT - 1)
            last.then_inc(fssq_mm, 1)
            for b in range(LTB):
                for half in range(2):
                    for j in range(4):
                        k = 4 * half + j
                        if b == 0:
                            pe.wait_ge(fin_ready, k + 1)
                        last = tp(bank[2 + 2 * b + half][:, j * P:(j + 1) * P], xT[:, k, CTX + b * P:CTX + (b + 1) * P], ident)
                    last.then_inc(fin_tp, 1)

        @block.scalar
        def _(sc):
            act_fn = nc.scalar.activation

            split = [0]

            def high_to(n):
                while split[0] < min(n, BASE + 2):
                    m = split[0]
                    name = stream[m][0] if m < BASE else "mlp"
                    sc.wait_ge(raw_in[m % RAW], 32 * (m // RAW + 1))
                    if m >= SPL:
                        sc.wait_ge(*consumed(m - SPL))
                    act_fn(unit_cols(wH, m % SPL, name), unit_cols(raw, m % RAW, name), ACT.Copy).then_inc(high_ready, 1)
                    split[0] += 1

            def mod_high(layer, g):
                if layer == 0:
                    high_to(mod_place(g, 1) + SPL)

            def warm(func):
                act_fn(scrap[:, :], eps[0:1, :], func)

            def norm_squares(layer, i):
                lo, hi = cols(layer, i == 0)
                warm(ACT.Sqrt)
                for k in range(KT):
                    if layer == 0 and i == 0:
                        sc.wait_ge(xt_ready, k + 1)
                    elif i == 1:
                        sc.wait_ge(xo_ready[layer], k + 1)
                    else:
                        sc.wait_ge(x2_ready, k + 1)
                    act_fn(sq[:, k, lo:hi], xT[:, k, lo:hi], ACT.Square).then_inc(sq_ready[layer][i], 1)
                    if i == 1 and k % 2 == 0 and k:
                        high_to(place["wout", layer, k // 2] + SPL)

            def norm(layer, i):
                lo, hi = cols(layer, i == 0)
                sc.wait_ge(ssq_done, 2 * layer + i + 1)
                act_fn(rstd[:, lo:hi], sum_bank(layer, i)[:, lo:hi], ACT.Sqrt, bias=eps, scale=1.0 / D).then_inc(root_ready, 1)
                if layer == 0 and i == 0:
                    for g in range(*GROUPS[0]):
                        mod_high(0, g)
                for k in range(KT):
                    sc.wait_ge(xr_ready[layer][i], k + 1)
                    for s in streams_of(layer, i == 0):
                        if layer == 1 and i == 1:
                            o = hlat[:, k, :]
                        else:
                            o = hH[:, k, s * 256:(s + 1) * 256]
                        last = act_fn(o, hpre[:, k % 2, s * 256:(s + 1) * 256], ACT.Identity,
                                      bias=mod[:, layer, 24 * i + k, s:s + 1])
                    last.then_inc(hh_ready[layer][i], 1)

            def mixer(layer):
                lo, hi = cols(layer, False)
                first_o = output_count(layer, *next(v for v in outputs_of[layer] if v[0] == "o")) - 1
                for n, (kind, i) in enumerate(outputs_of[layer]):
                    b = proj_bank(n)
                    if unit_of(kind, i):
                        name, part = unit_of(kind, i)
                        high_to(place[name, layer, part] + SPL)
                    sc.wait_ge(proj_mm[layer], n + 1)
                    if n == 0:
                        sc.wait_ge(small_in, 16 * 3)
                        o = act_fn(gates16[:, :], b[0:16, :], ACT.Identity, bias=gbias[:, layer:layer + 1])
                    elif kind in ("gi", "gf"):
                        o = act_fn(rowsg[0 if kind == "gi" else 1][:, :], b[0:8, :], ACT.Copy)
                    elif kind == "f":
                        o = act_fn(fT[:, i, lo:hi], b[:, lo:hi], ACT.Copy)
                    elif kind == "cu":
                        ss = slice(0, 2) if layer == 0 else slice(1, 2)
                        sc.wait_ge(pad_ready, layer + 1)
                        o = act_fn(apad[:, i, ss, HALF:HALF + CTX], b[:, lo:hi].rearrange("p (s t) -> p s t", t=CTX), ACT.Copy)
                    elif kind == "cg":
                        o = act_fn(sigc[:, i, lo:hi], b[:, lo:hi], ACT.Sigmoid)
                    elif kind == "q":
                        o = act_fn(qT[:, i, lo:hi], b[:, lo:hi], ACT.Copy)
                    elif kind == "k":
                        o = act_fn(kT[:, i, :], b[:, :], ACT.Copy, scale=float(P) ** -0.5)
                    elif kind == "v":
                        half, tb = i
                        o = act_fn(vtok[:, tb, 2 * half:2 * half + 2, 0:P], b[:, 0:256].rearrange("p (h e) -> p h e", h=2), ACT.Copy)
                    else:
                        half, tb = i
                        o = act_fn(sigo[:, tb, half * 256:(half + 1) * 256], b[:, 0:256], ACT.Sigmoid)
                    o.then_inc(proj_ready[layer], 1)
                    if n == first_o:
                        for ct in range(2):
                            sc.wait_ge(cdev_ready[layer], ct + 1)
                            act_fn(csq[:, ct, lo:hi], acc2[:, ct, lo:hi], ACT.Square).then_inc(csq_ready[layer], 1)
                    if n == first_o + 2:
                        for ct in range(2):
                            sc.wait_ge(cvar_mm[layer], ct + 1)
                            act_fn(csq[:, ct, lo:hi], bank[5 + ct][:, lo:hi], ACT.Sqrt, bias=eps).then_inc(croot_ready[layer], 1)
                    if kind == "gf":
                        sc.wait_ge(nabs_ready[layer], 1)
                        act_fn(rowsg[2][:, :], rowsg[2][:, :], ACT.Exp).then_inc(nabs_ready[layer], 1)
                        sc.wait_ge(nabs_ready[layer], 2)
                        act_fn(rowsg[2][:, :], rowsg[2][:, :], ACT.Ln, bias=1.0).then_inc(ln_ready, 1)
                    if (kind, i) == ("k", MH - 1):
                        sc.wait_ge(gate_tp, layer + 1)
                        act_fn(acol[:, :, :, :], bank[7][:, 0:64].rearrange("p (d b r) -> p d b r", d=2, b=NTB),
                               ACT.Copy).then_inc(gate_cols[layer], 1)
                        for d in range(2):
                            m = bank[7][:, 64 + 32 * d:96 + 32 * d].rearrange("p (b r) -> p b r", b=NTB)
                            last = act_fn(floorc[:, d * NTB:(d + 1) * NTB, :], m[:, :, d * MH:(d + 1) * MH], ACT.Exp)
                        last.then_inc(gate_cols[layer], 1)
                n = 0
                for s in streams_of(layer):
                    for ct in range(2):
                        n += 1
                        sc.wait_ge(fab_mm[layer], n)
                        act_fn(fab[:, 2 * s:2 * s + 2, ct, :], fab_bank(layer, s, ct)[:, :].rearrange("p (b f) -> p b f", b=2),
                               ACT.Copy).then_inc(fab_ready[layer], 1)
                for ct in range(2):
                    sc.wait_ge(cnorm_ready[layer], ct + 1)
                    w = layer * 2 + ct
                    act_fn(acc2[:, ct, lo:hi], acc2[:, ct, lo:hi], ACT.Silu, bias=vec[:, V_CB + w:V_CB + w + 1],
                           scale=vec[:, V_CG + w:V_CG + w + 1]).then_inc(csil_ready[layer], 1)
                mod_high(layer, CHUNK0)
                for ct in range(2):
                    sc.wait_ge(csil_ready[layer], ct + 1)
                    act_fn(y2[0][:, 2 + ct, lo:hi], acc2[:, ct, lo:hi], ACT.Copy).then_inc(csil_ready[layer], 1)
                for ct in range(2):
                    sc.wait_ge(fy_mm[layer], ct + 1)
                    act_fn(y2[0][:, ct, lo:hi], bank[2 + ct][:, lo:hi], ACT.Copy).then_inc(fyh_ready[layer], 1)
                mod_high(layer, CHUNK0 + 1)
                warm(ACT.Exp)
                sc.wait_ge(gate_cols[layer], 2)
                sc.wait_ge(fy_mm[layer], 2)

                def decay(t):
                    h, d = divmod(t, 2)
                    sc.wait_ge(mbc_mm[layer], t + 1)
                    if h:
                        sc.wait_ge(out_mm[layer], t - 1)
                    sc.wait_ge(dm_ready[layer], t + 1)
                    for s in range(NTB):
                        diag, full, _ = causal_cols(d, s, layer == 1)
                        bias = acol[:, d, s, d * MH + h:d * MH + h + 1]
                        for a, z in full:
                            last = act_fn(prob[:, d, s, a:z], bank[3][:, a:z], ACT.Exp, bias=bias, scale=-1.0)
                        if diag is not None:
                            last = act_fn(prob[:, d, s, diag * P:(diag + 1) * P], dm[:, diag, :], ACT.Exp, bias=bias)
                    last.then_inc(e_ready[layer], 1)

                b0 = 0 if layer == 0 else LTB
                if layer == 0:
                    high_to(mod_place(CHUNK0 + 2, 0) + SPL)
                decay(0)
                mod_high(layer, CHUNK0 + 2)
                mod_high(layer, CHUNK0 + 3)
                for t in range(2 * MH):
                    if t < 2 * MH - 1:
                        decay(t + 1)
                    high_to(mod_place(*head_unit(layer, t, 0)) + SPL)
                    high_to(mod_place(*head_unit(layer, t, 1)) + SPL)
                    if t % 2 == 0 and t:
                        h = t // 2 - 1
                        sc.wait_ge(hs_ready[layer], h + 1)
                        if h:
                            sc.wait_ge(ss_ready, MH * layer + h)
                        act_fn(hsq[:, b0:NTB, :], Hs[:, b0:NTB, h * P:(h + 1) * P], ACT.Square).then_inc(hsq_ready, 1)
                sc.wait_ge(hs_ready[layer], MH)
                sc.wait_ge(out_mm[layer], 2 * MH)
                act_fn(hsq_last[:, b0:NTB, :], Hs[:, b0:NTB, (MH - 1) * P:MH * P], ACT.Square).then_inc(hsq_ready, 1)
                warm(ACT.Sqrt)
                sc.wait_ge(ss_ready, MH * (layer + 1))
                act_fn(ss16[:, :], ss16[:, :], ACT.Sqrt, bias=eps, scale=1.0 / P).then_inc(hroot_ready, 1)
                high_to(place["wout", layer, 0] + SPL)
                for h in range(MH):
                    sc.wait_ge(yt_tp[layer], h + 1)
                    w = V_MG + layer * MH + h
                    act_fn(y1[0][:, h, lo:hi], head_bank(h)[:, lo:hi], ACT.Copy, scale=vec[:, w:w + 1]).then_inc(yh_ready[layer], 1)

            sc.wait_ge(vec_tp, 1)
            act_fn(vec[:, :], bank[0][:, 0:NVEC], ACT.Copy).then_inc(vec_ready, 1)
            sc.wait_ge(vec_ready, 1)
            act_fn(cond[:, :, 0], vec[:, V_CC:V_CC + KT], ACT.Silu).then_inc(cond_ready, 1)
            act_fn(cond[:, :, 1], vec[:, V_C:V_C + KT], ACT.Silu).then_inc(cond_ready, 1)
            sc.wait_ge(cond_ready, 2)
            sc.wait_ge(condh_ready, 1)
            act_fn(condz[:, :, ROWS - 4:ROWS - 2], cond[:, :, :], ACT.Copy).then_inc(condh_ready, 1)
            for layer in range(LAYERS):
                norm_squares(layer, 0)
                if layer == 0:
                    high_to(SPL)
                norm(layer, 0)
                mixer(layer)
                norm_squares(layer, 1)
                norm(layer, 1)
                if layer == 0:
                    for j in range(GU):
                        high_to(place["mlp", 0, 2 * j + 1] + SPL)
                        for t in range(2):
                            i = 2 * j + t
                            sc.wait_ge(gu0_mm, 4 * j + 2 * t + 1)
                            if i >= 2:
                                sc.wait_ge(act0_ready, i - 1)
                            act_fn(sil0[:, t, :], bank[4 * (j % 2) + 2 * t][:, :], ACT.Silu).then_inc(sil0_ready, 1)

                    def hidden_high(i):
                        if i >= 4:
                            sc.wait_ge(down0_mm, i - 3)
                        act_fn(a0[0][:, i % 4, :], act0[:, i, :], ACT.Copy).then_inc(a0h_ready, 1)

                    sc.wait_ge(act0_ready, NHT)
                    hidden_high(0)
                    hidden_high(1)
                    for n in range(DN):
                        if n < DN - 1:
                            hidden_high(2 * n + 2)
                            hidden_high(2 * n + 3)
                        high_to(place["mlp", 0, 2 * GU + n] + SPL)
            warm(ACT.Exp)
            for n in range(4):
                sc.wait_ge(hxtok_tp, n + 1)
                b, half = n // 2, n % 2
                act_fn(hxtok[:, b, half * NCOL:(half + 1) * NCOL], bank[2 + n][:, :], ACT.Copy).then_inc(hxtok_ready, 1)

            sc.wait_ge(wdiff_ready, 1)
            act_fn(rt[:, 88:90], rt[:, 88:90], ACT.Exp).then_inc(wexp_ready, 1)

            def gathered():
                for half in range(2):
                    last = act_fn(hTe[0][:, 4 * half:4 * half + 4, :], bank[6 + half][:, :].rearrange("p (k t) -> p k t", k=4), ACT.Copy)
                last.then_inc(hteh_ready, 1)

            def transposed(item, j):
                sc.wait_ge(act_tp, item * GU + j + 3)
                act_fn(actT[0][:, 2 * j:2 * j + 2, :], bank[2 + j % 2][:, 0:256].rearrange("p (i t) -> p i t", i=2),
                       ACT.Copy).then_inc(actTh_ready, 1)

            def high(item, p, ahead=False):
                n = BASE + p
                uses = TURN // RAW if p % RAW < EXP - (TURN - RAW) else TURN // RAW - 1
                before = (BASE - 1 - n % RAW) // RAW + 1
                if ahead:
                    sc.wait_ge(raw_in[n % RAW], item * (32 * uses) + 32 * (before + uses + p // RAW + 1))
                    sc.wait_ge(down_mm, item * DN + (DN - 3 + p + 2))
                else:
                    sc.wait_ge(raw_in[n % RAW], item * (32 * uses) + 32 * (before + p // RAW + 1))
                    if p == 2:
                        sc.wait_ge(down_mm, item * DN + 1)
                    elif p - SPL < 2 * GU:
                        sc.wait_ge(gu_mm, item * (2 * GU) + p - SPL + 1)
                    else:
                        sc.wait_ge(down_mm, item * DN + (p - SPL - 2 * GU + 2))
                act_fn(wH[:, n % SPL, :], raw[:, n % RAW, :], ACT.Copy).then_inc(high_ready, 1)

            sc.wait_ge(gather_mm, 1)
            gathered()
            sc.wait_ge(*consumed(BASE - 1))
            sc.wait_ge(route_ready, 1)
            n_items = sc.value_load(nitems[0:1, 0:1], min_val=NE, max_val=2 * NE)
            with sc.Fori(0, n_items) as item:
                for j in range(GU):
                    high(item, 2 * j + 2)
                    high(item, 2 * j + 3)
                    sc.wait_ge(gu_mm, item * (2 * GU) + 2 * j + 2)
                    sc.wait_ge(act_ready, item * GU + j + (2 if j == 0 else 1))
                    act_fn(sil[:, j % 2, :], bank[j % 2][:, 0:256], ACT.Silu).then_inc(sil_ready, 1)
                    if j == 1:
                        sc.wait_ge(y_ready, item + 1)
                    if j >= 1:
                        transposed(item, j - 1)
                sc.wait_ge(gather_mm, item + 2)
                gathered()
                transposed(item, GU - 1)
                for p in range(2 * GU + 2, EXP):
                    high(item, p)
                for p in range(2):
                    high(item, p, ahead=True)
                sc.wait_ge(down_mm, item * DN + DN + 1)
                act_fn(ysb[:, 0:NCOL], bank[4][:, :], ACT.Copy)
                act_fn(ysb[:, NCOL:D], bank[5][:, :], ACT.Copy).then_inc(y_ready, 1)
            warm(ACT.Sqrt)
            for k in range(KT):
                sc.wait_ge(xacc_ready, 2 * n_items + (k // 2 + 2))
                act_fn(sqf[:, k, :], xT[:, k, CTX:TOK], ACT.Square).then_inc(fsq_ready, 1)
            sc.wait_ge(fssq_mm, 1)
            act_fn(rsf[:, :], bank[4][:, 0:LAT], ACT.Sqrt, bias=eps, scale=1.0 / D).then_inc(froot_ready, 1)
            for n in range(4):
                sc.wait_ge(fin_tp, n + 1)
                b, half = n // 2, n % 2
                act_fn(outsb[:, b, half * NCOL:(half + 1) * NCOL], bank[2 + n][:, :], ACT.Copy).then_inc(out_ready, 1)

        @block.vector
        def _(dve):
            V = nc.vector
            steps = [0]

            def link(ins):
                steps[0] += 1
                ins.then_inc(dve_step, 1)
                dve.wait_ge(dve_step, steps[0])

            def mark(ins):
                steps[0] += 1
                ins.then_inc(dve_step, 1)
                return steps[0]

            split = [0]

            def low_to(n):
                while split[0] < min(n, BASE + 2):
                    m = split[0]
                    name = stream[m][0] if m < BASE else "mlp"
                    dve.wait_ge(high_ready, m + 1)
                    V.tensor_tensor(unit_cols(wL, m % SPL, name), unit_cols(raw, m % RAW, name),
                                    f(unit_cols(wH, m % SPL, name)), ALU.subtract).then_inc(unit_ready, 1)
                    split[0] += 1

            def mod_rows(group):
                dve.wait_ge(mod_mm, GROUPS[group][1])
                n = 4 * (GROUPS[group][1] - GROUPS[group][0])
                if group:
                    dve.wait_ge(ss_ready, MH * group - 1)
                V.tensor_copy(modrow[0:n, :], mod_bank[0:n, :]).then_inc(mod_row, 1)

            def mod_cols(group):
                first, end = GROUPS[group]
                n = end - first
                dve.wait_ge(mod_tp, group + 1)
                o = mod.rearrange("p l t s -> p (l t) s")[:, 4 * first:4 * end, :].rearrange("p (g j) s -> p g j s", j=4)
                rows_of = mod_bank[:, 0:8 * n].rearrange("p (j g s) -> p g j s", j=4, s=2)
                bias = vec[:, V_MOD + 4 * first:V_MOD + 4 * end].rearrange("p (g j) -> p g j", j=4)
                for s in range(2):
                    last = V.tensor_tensor(o[:, :, :, s], rows_of[:, :, :, s], bias, ALU.add)
                last.then_inc(mod_col, 1)

            def mod_low(layer, g):
                if layer == 0:
                    low_to(mod_place(g, 1) + SPL)

            def amplitude(layer, i):
                dve.wait_ge(mod_col, 1 + layer + i)
                sc1 = mod[:, layer, 24 * i + 8:24 * i + 16, :]
                g = vec[:, 16 * i + 8 * layer:16 * i + 8 * layer + 8].unsqueeze(2).to_broadcast([P, KT, 2])
                link(V.tensor_scalar(amp[:, layer, i], sc1, 1.0, None, ALU.add))
                V.tensor_tensor(amp[:, layer, i], amp[:, layer, i], g, ALU.mult).then_inc(amp_ready[layer][i], 1)

            def norm(layer, i):
                lo, hi = cols(layer, i == 0)
                dve.wait_ge(root_ready, 2 * layer + i + 1)
                link(V.reciprocal(rstd[:, lo:hi], rstd[:, lo:hi]))
                if layer == 0 and i == 0:
                    for g in range(*GROUPS[0]):
                        mod_low(0, g)
                    mod_rows(0)
                    mod_cols(0)
                    amplitude(0, 0)
                dve.wait_ge(amp_ready[layer][i], 1)
                ss = streams_of(layer, i == 0)
                latent_only = layer == 1 and i == 1

                def low(k):
                    dve.wait_ge(hh_ready[layer][i], k + 1)
                    for s in ss:
                        c = slice(s * 256, (s + 1) * 256)
                        last = V.scalar_tensor_tensor(hL[:, k, c], hpre[:, k % 2, c], mod[:, layer, 24 * i + k, s:s + 1],
                                                      f(hH[:, k, c]), ALU.add, ALU.subtract)
                    last.then_inc(h_ready[layer][i], 1)

                for k in range(KT):
                    if latent_only:
                        if k >= 2:
                            dve.wait_ge(hh_ready[layer][i], k - 1)
                    elif k >= 2:
                        low(k - 2)
                        dve.wait_ge(h_ready[layer][i], k - 1)
                    for s in ss:
                        c = slice(s * 256, (s + 1) * 256)
                        last = V.scalar_tensor_tensor(hpre[:, k % 2, c], xT[:, k, c], amp[:, layer, i, k, s:s + 1],
                                                      rstd[:, c], ALU.mult, ALU.mult)
                    last.then_inc(xr_ready[layer][i], 1)
                if not latent_only:
                    low(KT - 2)
                    low(KT - 1)

            def gates(layer):
                R = [r[:, :] for r in rowsg]
                dve.wait_ge(proj_ready[layer], output_count(layer, "gf", 0))
                ins = V.scalar_tensor_tensor(R[2], R[1], -1.0, R[1], ALU.mult, ALU.min)
                ins.then_inc(nabs_ready[layer], 1)
                dve.wait_ge(ln_ready, layer + 1)
                link(V.scalar_tensor_tensor(R[1], R[1], 0.0, R[2], ALU.min, ALU.subtract))
                onesrow = ones[0:8, 0:1].to_broadcast([8, TOK])

                def run(d, o, src, first, kind):
                    if d == 0:
                        spans = [slice(0, TOK)]
                    else:
                        spans = [slice(CTX - 1, None, -1), slice(TOK - 1, CTX - 1, -1)]
                    init = first
                    for s in spans:
                        a = src[:, s]
                        if kind == "sum":
                            link(V.tensor_tensor_scan(o[:, s], onesrow[:, s], a, init, ALU.mult, ALU.add))
                        else:
                            link(V.tensor_tensor_scan(o[:, s], a, a, init, ALU.max, ALU.max))
                        init = o[:, 0:1]

                dve.wait_ge(proj_mm[layer], output_count(layer, "gf", 0))
                for d in range(2):
                    run(d, R[2 + d], R[1], 0.0, "sum")
                link(V.tensor_tensor(R[1], R[0], R[3], ALU.subtract))
                link(V.tensor_tensor(R[0], R[0], R[2], ALU.subtract))
                for d in range(2):
                    run(d, R[4 + d], R[d], NEG, "max")
                for d in range(2):
                    ins = V.scalar_tensor_tensor(R[2 + d], R[2 + d], -1.0, R[4 + d], ALU.mult, ALU.subtract)
                    if d == 0:
                        link(ins)
                    else:
                        ins.then_inc(gate_rows, 1)

            def convolution(layer):
                ss = slice(0, 2) if layer == 0 else slice(1, 2)
                lo, hi = cols(layer, False)
                n0 = place["g", layer, 0]
                dve.wait_ge(proj_ready[layer], output_count(layer, "cg", 1))
                for ct in range(2):
                    v = apad[:, ct, ss, HALF:HALF + CTX]
                    link(V.tensor_tensor(v, v, sigc[:, ct, lo:hi].rearrange("p (s t) -> p s t", t=CTX), ALU.mult))
                ahead = 6
                for t in range(TAPS):
                    if t % 7 == 6:
                        ahead += 1
                        low_to(n0 + ahead)
                    for ct in range(2):
                        at = V_DW + layer * 2 * TAPS + t * 2 + ct
                        src = apad[:, ct, ss, t:t + CTX]
                        if t == 0:
                            db = vec[:, V_DB + 2 * layer + ct:V_DB + 2 * layer + ct + 1]
                            mark(V.tensor_scalar(acc[:, ct, ss, :], src, vec[:, at:at + 1], db, ALU.mult, ALU.add))
                        else:
                            dve.wait_ge(dve_step, steps[0] - 1)
                            mark(V.scalar_tensor_tensor(acc[:, ct, ss, :], src, vec[:, at:at + 1], acc[:, ct, ss, :],
                                                        ALU.mult, ALU.add))
                dve.wait_ge(dve_step, steps[0])
                dve.sem_inc(conv_ready, 1)
                low_to(place["o", layer, 0] + SPL)

            def conv_norm(layer):
                lo, hi = cols(layer, False)
                for ct in range(2):
                    dve.wait_ge(cmean_mm[layer], ct + 1)
                    V.tensor_tensor(acc2[:, ct, lo:hi], acc2[:, ct, lo:hi], bank[5 + ct][:, lo:hi],
                                    ALU.subtract).then_inc(cdev_ready[layer], 1)
                for ct in range(2):
                    dve.wait_ge(croot_ready[layer], ct + 1)
                    link(V.reciprocal(csq[:, ct, lo:hi], csq[:, ct, lo:hi]))
                    V.tensor_tensor(acc2[:, ct, lo:hi], acc2[:, ct, lo:hi], csq[:, ct, lo:hi],
                                    ALU.mult).then_inc(cnorm_ready[layer], 1)
                low_to(place["o", layer, 1] + SPL)

            def mixer_low(layer):
                lo, hi = cols(layer, False)
                mod_low(layer, CHUNK0)
                for ct in range(2):
                    dve.wait_ge(csil_ready[layer], 2 + ct + 1)
                    V.tensor_tensor(y2[1][:, 2 + ct, lo:hi], acc2[:, ct, lo:hi], f(y2[0][:, 2 + ct, lo:hi]),
                                    ALU.subtract).then_inc(ycat_ready[layer], 1)
                for ct in range(2):
                    dve.wait_ge(fyh_ready[layer], ct + 1)
                    V.tensor_tensor(y2[1][:, ct, lo:hi], bank[2 + ct][:, lo:hi], f(y2[0][:, ct, lo:hi]),
                                    ALU.subtract).then_inc(ycat_ready[layer], 1)
                mod_low(layer, CHUNK0 + 1)

            def heads(layer):
                tbs = list(range(NTB)) if layer == 0 else list(range(LTB, NTB))
                b0 = tbs[0]

                def differences(h, d):
                    dve.wait_ge(mbc_mm[layer], 2 * h + d + 1)
                    V.tensor_tensor(dm[:, b0:NTB, :], masks[d].unsqueeze(1).to_broadcast([P, NTB - b0, P]),
                                    bank[3][:, b0 * P:TOK].rearrange("p (b t) -> p b t", t=P),
                                    ALU.subtract).then_inc(dm_ready[layer], 1)

                def weigh(h, d):
                    dve.wait_ge(e_ready[layer], 2 * h + d + 1)
                    dve.wait_ge(score_mm[layer], h + 1)
                    last = None
                    for s in range(NTB):
                        for a, z in causal_cols(d, s, layer == 1)[2]:
                            sco = bank[s][:, a:z] if s < 2 else bank[2][:, (s - 2) * LAT + a - CTX:(s - 2) * LAT + z - CTX]
                            last = V.tensor_tensor(prob[:, d, s, a:z], prob[:, d, s, a:z], sco, ALU.mult)
                    last.then_inc(p_ready[layer], 1)

                def normalise(h):
                    dve.wait_ge(out_mm[layer], 2 * h + 2)
                    groups = [[i for i in (range(3 * g, min(3 * g + 3, 8))) if i % NTB in tbs] for g in range(3)]
                    for step in range(2):
                        for g, ids in enumerate(groups):
                            i0, n = ids[0], len(ids)
                            den = bank[5 + g][:, 0:387].rearrange("p (i e) -> p i e", e=129)[:, i0 % 3:i0 % 3 + n, P]
                            o = dmax[:, i0:i0 + n]
                            if step == 0:
                                mark(V.scalar_tensor_tensor(o, den, -1.0, floorc[:, i0:i0 + n, h], ALU.mult, ALU.max))
                            else:
                                dve.wait_ge(dve_step, steps[0] - 2)
                                mark(V.tensor_tensor(o, den, o, ALU.max))
                    dve.wait_ge(dve_step, steps[0])
                    for d in range(2):
                        link(V.reciprocal(rden[:, d * NTB + b0:(d + 1) * NTB], dmax[:, d * NTB + b0:(d + 1) * NTB]))
                    num = lambda idx: bank[5 + idx // 3][:, (idx % 3) * 129:(idx % 3) * 129 + P]
                    for tb in tbs:
                        mark(V.tensor_scalar(Hs[:, tb, h * P:(h + 1) * P], num(tb), rden[:, tb:tb + 1], None, ALU.mult))
                    last = None
                    for tb in tbs:
                        idx = NTB + tb
                        dve.wait_ge(dve_step, steps[0] - (len(tbs) - 1 - (tb - b0)))
                        last = V.scalar_tensor_tensor(Hs[:, tb, h * P:(h + 1) * P], num(idx), rden[:, idx:idx + 1],
                                                      Hs[:, tb, h * P:(h + 1) * P], ALU.mult, ALU.add)
                    last.then_inc(hs_ready[layer], 1)

                def sum_squares(h):
                    dve.wait_ge(hsq_ready, MH * layer + h + 1)
                    V.tensor_reduce(ss16.rearrange("p (b h) -> p b h", h=MH)[:, b0:NTB, h],
                                    (hsq_last if h == MH - 1 else hsq)[:, b0:NTB, :], AX.X, ALU.add).then_inc(ss_ready, 1)

                dve.wait_ge(ycat_ready[layer], 4)
                differences(0, 0)
                mod_low(layer, CHUNK0 + 2)
                weigh(0, 0)
                mod_low(layer, CHUNK0 + 3)
                for t in range(2 * MH):
                    if t < 2 * MH - 1:
                        differences(*divmod(t + 1, 2))
                    low_to(mod_place(*head_unit(layer, t, 0)) + SPL - 1)
                    if t < 2 * MH - 1:
                        if t % 2 == 0 and t:
                            normalise(t // 2 - 1)
                        if t % 2 and t > 1:
                            sum_squares((t - 3) // 2)
                        weigh(*divmod(t + 1, 2))
                    low_to(mod_place(*head_unit(layer, t, 1)) + SPL - 1)
                low_to(place["wout", layer, 1] + 1)
                sum_squares(MH - 2)
                mod_rows(layer + 1)
                normalise(MH - 1)
                sum_squares(MH - 1)
                mod_cols(layer + 1)
                amplitude(layer, 1)
                if layer == 0:
                    amplitude(1, 0)

            def after_heads(layer):
                lo, hi = cols(layer, False)
                tbs = list(range(NTB)) if layer == 0 else list(range(LTB, NTB))
                b0 = tbs[0]
                dve.wait_ge(hroot_ready, layer + 1)
                link(V.reciprocal(ss16[:, 4 * b0:16], ss16[:, 4 * b0:16]))
                for h in range(MH):
                    for tb in tbs:
                        v = Hs[:, tb, h * P:(h + 1) * P]
                        last = V.scalar_tensor_tensor(v, v, ss16[:, 4 * tb + h:4 * tb + h + 1], sigo[:, tb, h * P:(h + 1) * P],
                                                      ALU.mult, ALU.mult)
                    last.then_inc(ytok_ready, 1)
                low_to(place["wout", layer, 0] + SPL)
                for h in range(MH):
                    dve.wait_ge(yh_ready[layer], h + 1)
                    w = V_MG + layer * MH + h
                    V.scalar_tensor_tensor(y1[1][:, h, lo:hi], head_bank(h)[:, lo:hi], vec[:, w:w + 1], f(y1[0][:, h, lo:hi]),
                                           ALU.mult, ALU.subtract).then_inc(ycat_ready[layer], 1)

            def residual(layer):
                for m in range(KT):
                    dve.wait_ge(wout_mm[layer], m + 1)
                    last = None
                    for s in streams_of(layer):
                        v = xT[:, m, s * 256:(s + 1) * 256]
                        last = V.scalar_tensor_tensor(v, bank[m][:, s * 256:(s + 1) * 256], mod[:, layer, 16 + m, s:s + 1],
                                                      v, ALU.mult, ALU.add)
                    last.then_inc(xo_ready[layer], 1)
                    if m % 2 == 0 and m:
                        low_to(place["wout", layer, m // 2] + SPL)

            dve.wait_ge(vec_ready, 1)
            V.memset(f(condz[:, :, :]), 0.0).then_inc(condh_ready, 1)
            dve.wait_ge(condh_ready, 2)
            V.tensor_tensor(condz[:, :, ROWS - 2:ROWS], cond[:, :, :], f(condz[:, :, ROWS - 4:ROWS - 2]),
                            ALU.subtract).then_inc(condz_ready, 1)
            for n in range(KT):
                dve.wait_ge(xt_tp, n + 1)
                V.tensor_copy(xT[:, n, :], bank[5 + n % 2][:, :]).then_inc(xt_ready, 1)
            low_to(SPL)
            for layer in range(LAYERS):
                norm(layer, 0)
                dve.wait_ge(h_ready[layer][0], KT)
                V.memset(apad[:, :, :, 0:HALF], 0.0)
                V.memset(apad[:, :, :, HALF + CTX:PADW], 0.0).then_inc(pad_ready, 1)
                link(V.memset(vtok[:, :, :, P:P + 1], 1.0))
                n0 = place["g", layer, 0]
                low_to(n0 + SPL + 1)
                gates(layer)
                low_to(n0 + SPL + 3)
                convolution(layer)
                conv_norm(layer)
                mixer_low(layer)
                heads(layer)
                after_heads(layer)
                residual(layer)
                norm(layer, 1)
                if layer == 0:
                    for j in range(GU):
                        low_to(place["mlp", 0, 2 * j + 1] + SPL)
                        for t in range(2):
                            i = 2 * j + t
                            dve.wait_ge(sil0_ready, i + 1)
                            dve.wait_ge(gu0_mm, 4 * j + 2 * t + 2)
                            V.tensor_tensor(act0[:, i, :], sil0[:, t, :], bank[4 * (j % 2) + 2 * t + 1][:, :],
                                            ALU.mult).then_inc(act0_ready, 1)

                    def hidden_low(i):
                        dve.wait_ge(a0h_ready, i + 1)
                        V.tensor_tensor(a0[1][:, i % 4, :], act0[:, i, :], f(a0[0][:, i % 4, :]),
                                        ALU.subtract).then_inc(a0_ready, 1)

                    hidden_low(0)
                    hidden_low(1)
                    for n in range(DN):
                        if n < DN - 1:
                            hidden_low(2 * n + 2)
                            hidden_low(2 * n + 3)
                        low_to(place["mlp", 0, 2 * GU + n] + SPL)
                    for m in range(KT):
                        dve.wait_ge(down0_mm, NHT - 2 + m + 1)
                        last = None
                        for s in range(2):
                            v = xT[:, m, s * 256:(s + 1) * 256]
                            last = V.scalar_tensor_tensor(v, bank[m][:, s * 256:(s + 1) * 256], mod[:, 0, 40 + m, s:s + 1],
                                                          v, ALU.mult, ALU.add)
                        last.then_inc(x2_ready, 1)

            dve.sem_inc(act_ready, 2)
            V.memset(ysb[:, :], 0.0).then_inc(y_ready, 1)
            V.memset(spread[:, :], 0.0).then_inc(spread_ready, 1)
            dve.wait_ge(logit_mm, 1)
            mask = rt[:, 0:16].rearrange("p (b e) -> p b e", b=LTB)
            lg = rt[:, 16:32].rearrange("p (b e) -> p b e", b=LTB)
            hot = rt[:, 32:64].rearrange("p (r b e) -> p r b e", r=2, b=LTB)
            tie = rt[:, 64:80].rearrange("p (b e) -> p b e", b=LTB)
            top = rt[:, 80:84].rearrange("p (r b) -> p r b", r=2)
            tmx = rt[:, 84:86]
            wts = rt[:, 86:90].rearrange("p (r b) -> p r b", r=2)
            down_to = iota[:, 0:NE]
            desc = rt[:, 96:104]
            gat = rt[:, 104:120].rearrange("p (b e) -> p b e", b=LTB)
            cnt = rt[:, 120:128]
            posn = rt[:, 128:144].rearrange("p (b e) -> p b e", b=LTB)
            mxc = rt[:, 144:145]
            link(V.tensor_scalar(desc, down_to, -1.0, float(NE), ALU.mult, ALU.add))
            for b in range(LTB):
                link(V.tensor_tensor(lg[:, b, :], bank[b][:, 0:NE], rbias[:, :], ALU.add))
            for r in range(2):
                link(V.tensor_reduce(top[:, r, :], lg, AX.X, ALU.max))
                link(V.tensor_tensor(tie, lg, top[:, r, :].unsqueeze(2).to_broadcast([P, LTB, NE]), ALU.is_equal))
                link(V.tensor_tensor(tie, tie, desc.unsqueeze(1).to_broadcast([P, LTB, NE]), ALU.mult))
                link(V.tensor_reduce(tmx, tie, AX.X, ALU.max))
                link(V.tensor_tensor(hot[:, r], desc.unsqueeze(1).to_broadcast([P, LTB, NE]),
                                     tmx.unsqueeze(2).to_broadcast([P, LTB, NE]), ALU.is_equal))
                if r == 0:
                    link(V.scalar_tensor_tensor(lg, hot[:, 0], -3e38, lg, ALU.mult, ALU.add))
            V.tensor_tensor(mask, hot[:, 0], hot[:, 1], ALU.add).then_inc(mask_ready, 1)
            V.tensor_tensor(wts[:, 1, :], top[:, 1, :], top[:, 0, :], ALU.subtract).then_inc(wdiff_ready, 1)
            link(V.memset(gatecol[:, :, :], 0.0))
            link(V.memset(slotpos[:, :, :], -1.0))
            dve.wait_ge(pos_mm, 1)
            link(V.scalar_tensor_tensor(posn, bank[1][:, 0:16].rearrange("p (b e) -> p b e", b=LTB), 1.0, mask, ALU.add, ALU.mult))
            for r in range(2):
                link(V.tensor_scalar(slotpos[:, :, r * NE:(r + 1) * NE], posn, -1.0 - P * r, None, ALU.add))

            def build_pick(item):
                last = None
                for b in range(LTB):
                    last = V.tensor_scalar(pick[:, b, :], iota, slotpos[:, b, bass.ds(item, 1)], None, ALU.is_equal)
                last.then_inc(pick_ready, 1)

            build_pick(0)
            link(V.tensor_reduce(mxc, bank[1][:, 16:24], AX.X, ALU.max))
            link(V.tensor_scalar(mxc, mxc, float(P), float(NE), ALU.is_gt, ALU.mult))
            link(V.tensor_scalar(nitems[0:1, 0:1], mxc[0:1, :], float(NE), None, ALU.add))
            dve.sem_inc(route_ready, 1)
            dve.wait_ge(wexp_ready, 1)
            link(V.tensor_scalar(wts[:, 0, :], wts[:, 1, :], 1.0, None, ALU.add))
            link(V.reciprocal(wts[:, 0, :], wts[:, 0, :]))
            link(V.tensor_tensor(wts[:, 1, :], wts[:, 1, :], wts[:, 0, :], ALU.mult))
            link(V.tensor_tensor(gat, hot[:, 0], wts[:, 0, :].unsqueeze(2).to_broadcast([P, LTB, NE]), ALU.mult))
            link(V.tensor_tensor(tie, hot[:, 1], wts[:, 1, :].unsqueeze(2).to_broadcast([P, LTB, NE]), ALU.mult))
            for r in range(2):
                link(V.tensor_tensor(gatecol[:, :, r * NE:(r + 1) * NE], gat, tie, ALU.add))

            def accumulate(r):
                last = None
                for j in range(4):
                    m = 4 * r + j
                    v = xT[:, m, CTX:TOK]
                    last = V.scalar_tensor_tensor(v, bank[6 + j // 2][:, (j % 2) * LAT:(j % 2 + 1) * LAT],
                                                  mod[:, 1, 40 + m, 1:2], v, ALU.mult, ALU.add)
                last.then_inc(xacc_ready, 1)

            def low(item, p, ahead=False):
                n = BASE + p
                dve.wait_ge(high_ready, item * EXP + (BASE + p + 1 + (EXP if ahead else 0)))
                V.tensor_tensor(wL[:, n % SPL, :], raw[:, n % RAW, :], f(wH[:, n % SPL, :]), ALU.subtract).then_inc(unit_ready, 1)

            def gathered_low(count):
                dve.wait_ge(hteh_ready, count + 1)
                for half in range(2):
                    ks = slice(4 * half, 4 * half + 4)
                    last = V.tensor_tensor(hTe[1][:, ks, :], bank[6 + half][:, :].rearrange("p (k t) -> p k t", k=4),
                                           f(hTe[0][:, ks, :]), ALU.subtract)
                last.then_inc(hte_ready, 1)

            def transposed_low(item, j):
                dve.wait_ge(actTh_ready, item * GU + j + 1)
                ks = slice(2 * j, 2 * j + 2)
                V.tensor_tensor(actT[1][:, ks, :], bank[2 + j % 2][:, 0:256].rearrange("p (i t) -> p i t", i=2),
                                f(actT[0][:, ks, :]), ALU.subtract).then_inc(actT_ready, 1)

            dve.sem_inc(xacc_ready, 1)
            dve.sem_inc(act_tp, 2)
            dve.sem_inc(actT_ready, 2)
            gathered_low(0)
            n_items = dve.value_load(nitems[0:1, 0:1], min_val=NE, max_val=2 * NE)
            with dve.Fori(0, n_items) as item:
                dve.wait_ge(gather_mm, item + 1)
                build_pick(item + 1)
                for b in range(LTB):
                    last = V.tensor_scalar(wpick[:, b, :], iota, slotpos[:, b, bass.ds(item, 1)],
                                           gatecol[:, b, bass.ds(item, 1)], ALU.is_equal, ALU.mult)
                last.then_inc(wpick_ready, 1)
                for j in range(GU):
                    low(item, 2 * j + 2)
                    low(item, 2 * j + 3)
                    dve.wait_ge(sil_ready, item * GU + j + 1)
                    dve.wait_ge(act_tp, item * GU + j + (2 if j == 0 else 1))
                    V.tensor_tensor(act[:, j % 2, :], sil[:, j % 2, :], bank[j % 2][:, 256:512], ALU.mult).then_inc(act_ready, 1)
                    if j < 2:
                        dve.wait_ge(scatter_mm, 2 * item + j + 1)
                        dve.wait_ge(xacc_ready, 2 * item + j + 1)
                        accumulate(j)
                    if j >= 1:
                        transposed_low(item, j - 1)
                    if j == 3:
                        dve.wait_ge(spread_tp, item + 1)
                        V.tensor_copy(spread[:, :], bank[3][:, 256:512]).then_inc(spread_ready, 1)
                gathered_low(item + 1)
                transposed_low(item, GU - 1)
                for p in range(2 * GU + 2, EXP):
                    low(item, p)
                for p in range(2):
                    low(item, p, ahead=True)
            for q in range(4):
                dve.wait_ge(scatter_mm, 2 * n_items + q + 1)
                for j in range(2):
                    m = 2 * q + j
                    v = xT[:, m, CTX:TOK]
                    last = V.scalar_tensor_tensor(v, last_bank(q)[:, j * LAT:(j + 1) * LAT], mod[:, 1, 40 + m, 1:2], v,
                                                  ALU.mult, ALU.add)
                last.then_inc(xacc_ready, 1)

            dve.wait_ge(froot_ready, 1)
            dve.wait_ge(xacc_ready, 2 * n_items + 5)
            link(V.reciprocal(rsf[:, :], rsf[:, :]))
            for k in range(KT):
                v = xT[:, k, CTX:TOK]
                V.scalar_tensor_tensor(v, v, vec[:, V_FIN + k:V_FIN + k + 1], rsf[:, :], ALU.mult, ALU.mult).then_inc(fin_ready, 1)


_INS = ["x", "c", "ctx", "c_ctx", "norm1_g", "norm2_g", "w_mod", "b_mod", "w_in", "b_gate", "mlstm_norm_g", "conv_dw",
        "conv_db", "conv_norm_g", "conv_norm_b", "w_out", "ffn_w_gate_up", "ffn_w_down", "moe_w_router",
        "moe_b_router", "moe_w_gate_up", "moe_w_down", "final_norm_g"]


def _constants(np):
    t = np.zeros((P, NCONST), np.float32)
    i = np.arange(P)
    t[:, C_ID:C_ID + P] = np.eye(P)
    t[:, C_ONE:C_ONE + P] = 1.0
    t[:, C_GRP:C_GRP + P] = (i[:, None] // 64 == i[None, :] // 64) / 64.0
    t[:, C_UT:C_UT + P] = i[:, None] < i[None, :]
    t[:, C_IOTA:C_IOTA + P] = i[None, :]
    t[:, C_MF:C_MF + P] = np.where(i[:, None] <= i[None, :], 0.0, NEG)
    t[:, C_MB:C_MB + P] = np.where(i[:, None] >= i[None, :], 0.0, NEG)
    n = np.arange(256)
    for b in range(2):
        ang = 2 * np.pi * ((i[:, None] + b * P) * n[None, :] % 256) / 256.0
        t[:, C_COS + b * 256:C_COS + (b + 1) * 256] = np.cos(ang)
        t[:, C_SIN + b * 256:C_SIN + (b + 1) * 256] = -np.sin(ang)
    same = i[:, None] // 64 == i[None, :] // 64
    ang = 2 * np.pi * ((i[:, None] % 64) * (i[None, :] % 64) % 64) / 64.0
    t[:, C_BD:C_BD + P] = np.where(same, np.cos(ang), 0.0) / 128.0
    t[:, C_BD + P:C_BD + 2 * P] = np.where(same, np.sin(ang), 0.0) / 128.0
    t[:, C_EPS] = EPS
    for g in range(2):
        for m in range(8):
            t[(2 * (m // MH) + g) * MH + m % MH, C_PERM + 8 * g + m] = 1.0
    for m in range(ROWS):
        t[m, C_PAIR + m // 4 * 2 + m % 2] = 1.0
    return t


def kernel(**inputs):
    import numpy as _np
    import concourse.bacc as _bacc
    from concourse import mybir as _mybir
    from concourse.bass_utils import run_bass_kernel_spmd as _run

    nc = _bacc.Bacc("TRN2", target_bir_lowering=False, num_devices=1)
    arrays, args = {}, []
    for name in _INS:
        a = _np.ascontiguousarray(inputs[name])
        arrays[f"in_{name}_dram"] = a
        args.append(nc.dram_tensor(f"in_{name}_dram", a.shape, _mybir.dt.from_np(a.dtype), kind="ExternalInput").ap())
    table = _constants(_np)
    arrays["constants_dram"] = table
    args.append(nc.dram_tensor("constants_dram", table.shape, _mybir.dt.float32, kind="ExternalInput").ap())
    args.append(nc.dram_tensor("out_0_dram", (1, LAT, D), _mybir.dt.float32, kind="ExternalOutput").ap())
    build(nc, *args)
    r = _run(nc, [arrays], core_ids=[0])
    return r.results[0]["out_0_dram"]
```
